# Optimizing a Trainium2 kernel written in Bass

```python
import jax, jax.numpy as jnp
from jax import lax
import numpy as np

D_MODEL = 1024
BATCH = 1
SEQ = 256
DEPTH = 2

CTX_LEN = 256
GRID_W = 64

POOL_GROUPS = 4
POOL_WINDOWS = (2, 4, 8, 16)
POOL_GROUP_DIM = 64
POOL_WIDTH = POOL_GROUPS * POOL_GROUP_DIM
NA_HEADS = 4
NA_HEAD_DIM = 64
NA_WIDTH = NA_HEADS * NA_HEAD_DIM
NA_WIN_ROWS = 8
NA_WIN_COLS = 16
NA_QCOLS = 16
NA_KCOLS = NA_QCOLS + NA_WIN_COLS
SGU_GROUPS = 4
SGU_GROUP_DIM = 64
SGU_WIDTH = SGU_GROUPS * SGU_GROUP_DIM
SGU_CHUNK = 128
MLA_HEADS = 4
MLA_Q_RANK = 256
MLA_KV_RANK = 128
MLA_NOPE_DIM = 64
MLA_ROPE_DIM = 32
MLA_V_DIM = 64
MLA_WIDTH = MLA_HEADS * MLA_V_DIM
MLA_SCALE = (MLA_NOPE_DIM + MLA_ROPE_DIM) ** -0.5
ROPE_BASE = 10000.0
ATTN_Q_BLOCK = 128

MIX_WIDTH = POOL_WIDTH + NA_WIDTH + SGU_WIDTH + MLA_WIDTH
IN_A = POOL_WIDTH
IN_B = 3 * NA_WIDTH
IN_C = 2 * SGU_WIDTH
IN_D = MLA_Q_RANK + MLA_KV_RANK + MLA_ROPE_DIM
OFF_B = IN_A
OFF_C = OFF_B + IN_B
OFF_D = OFF_C + IN_C
IN_WIDTH = OFF_D + IN_D

N_EXPERTS = 16
N_EXPERT_GROUPS = 4
EXPERTS_PER_GROUP = N_EXPERTS // N_EXPERT_GROUPS
TOP_K = 2
D_EXPERT = 256

N_MOD = 6
EPS = 1e-6
NEG_INF = -1e30

kernel_name = 'hybrid_parallel_group_diffusion_block'

def rms_norm(x, g):
    xf = x.astype(jnp.float32)
    y = xf * lax.rsqrt(jnp.mean(xf * xf, axis=-1, keepdims=True) + EPS)
    return (y * g.astype(jnp.float32)).astype(x.dtype)

def modulate(h, shift, scale):
    return h * (1 + scale) + shift

def axial_rope_tables(S):
    t = jnp.arange(S)
    row = (t // GRID_W).astype(jnp.float32)
    col = (t % GRID_W).astype(jnp.float32)
    nf = MLA_ROPE_DIM // 4
    inv = ROPE_BASE ** (-jnp.arange(nf, dtype=jnp.float32) / nf)
    ang = jnp.concatenate([row[:, None] * inv, col[:, None] * inv], axis=-1)
    return jnp.cos(ang), jnp.sin(ang)

def rope_2d(x, cos, sin):
    r1, r2, c1, c2 = jnp.split(x, 4, axis=-1)
    x1 = jnp.concatenate([r1, c1], axis=-1)
    x2 = jnp.concatenate([r2, c2], axis=-1)
    cos = cos.astype(x.dtype)
    sin = sin.astype(x.dtype)
    o1 = x1 * cos - x2 * sin
    o2 = x1 * sin + x2 * cos
    nf = o1.shape[-1] // 2
    return jnp.concatenate([o1[..., :nf], o2[..., :nf], o1[..., nf:], o2[..., nf:]], axis=-1)

def multiscale_pool(u, w, s):
    B, L, _ = u.shape
    ug = u.reshape(B, L, POOL_GROUPS, POOL_GROUP_DIM).astype(jnp.float32)
    csum = jnp.concatenate([jnp.zeros_like(ug[:, :1]), jnp.cumsum(ug, axis=1)], axis=1)
    t = jnp.arange(L)
    diffs = []
    for g, win in enumerate(POOL_WINDOWS):
        lo = jnp.clip(t - win // 2, 0, L)
        hi = jnp.clip(t - win // 2 + win, 0, L)
        cg = csum[:, :, g]
        mean = (cg[:, hi] - cg[:, lo]) / (hi - lo).astype(jnp.float32)[:, None]
        diffs.append(mean - ug[:, :, g])
    d = jnp.stack(diffs, axis=2).astype(u.dtype)
    y = jnp.einsum('blgc,gcd->blgd', d, w).reshape(B, L, POOL_WIDTH)
    return y * s

def spatial_gating(uv, g_norm, w_s, b_s):
    B, L, _ = uv.shape
    uv = jax.nn.gelu(uv)
    u, v = uv[..., :SGU_WIDTH], uv[..., SGU_WIDTH:]
    n = L // SGU_CHUNK
    vg = rms_norm(v.reshape(B, n, SGU_CHUNK, SGU_GROUPS, SGU_GROUP_DIM),
                  g_norm.reshape(SGU_GROUPS, SGU_GROUP_DIM))
    mixed = jnp.einsum('gpq,bnqgc->bnpgc', w_s, vg) + b_s.T[:, :, None]
    return u * mixed.reshape(B, L, SGU_WIDTH)

def dense_attention(q, k, v):
    s = jnp.einsum('bqhe,bkhe->bhqk', q, k).astype(jnp.float32) * (q.shape[-1] ** -0.5)
    p = jax.nn.softmax(s, axis=-1).astype(v.dtype)
    return jnp.einsum('bhqk,bkhe->bqhe', p, v)

def neighborhood_attention(q, k, v, kc, vc, rpb, rows):
    B, S, H, E = q.shape
    kr = min(NA_WIN_ROWS, rows)
    ncb = GRID_W // NA_QCOLS
    r = jnp.arange(rows)
    row_idx = jnp.clip(r - kr // 2, 0, rows - kr)[:, None] + jnp.arange(kr)
    qcol = (jnp.arange(ncb) * NA_QCOLS)[:, None] + jnp.arange(NA_QCOLS)
    ws = jnp.clip(qcol - NA_WIN_COLS // 2, 0, GRID_W - NA_WIN_COLS)
    cs = jnp.minimum(ws[:, 0], GRID_W - NA_KCOLS)
    col_idx = cs[:, None] + jnp.arange(NA_KCOLS)
    key_tok = (row_idx[:, None, :, None] * GRID_W + col_idx[None, :, None, :]).reshape(rows, ncb, kr * NA_KCOLS)
    kcol = col_idx[:, None, :]
    valid = (kcol >= ws[:, :, None]) & (kcol < ws[:, :, None] + NA_WIN_COLS)
    valid = jnp.broadcast_to(valid[:, :, None, :], (ncb, NA_QCOLS, kr, NA_KCOLS)).reshape(ncb, NA_QCOLS, kr * NA_KCOLS)
    dr = row_idx - r[:, None] + NA_WIN_ROWS - 1
    dc = jnp.clip(kcol - qcol[:, :, None] + NA_WIN_COLS - 1, 0, 2 * NA_WIN_COLS - 2)
    bias = rpb[:, dr[:, :, None, None, None], dc[None, None]]
    bias = bias.transpose(0, 1, 3, 4, 2, 5).reshape(H, rows, ncb, NA_QCOLS, kr * NA_KCOLS).astype(jnp.float32)

    scale = E ** -0.5
    qg = q.reshape(B, rows, ncb, NA_QCOLS, H, E)
    kg = jnp.take(k, key_tok, axis=1)
    vg = jnp.take(v, key_tok, axis=1)
    s_win = jnp.einsum('brjqhe,brjkhe->bhrjqk', qg, kg).astype(jnp.float32) * scale + bias
    s_win = jnp.where(valid, s_win, NEG_INF)
    s_ctx = jnp.einsum('brjqhe,bche->bhrjqc', qg, kc).astype(jnp.float32) * scale
    p = jax.nn.softmax(jnp.concatenate([s_win, s_ctx], axis=-1), axis=-1).astype(v.dtype)
    nw = kr * NA_KCOLS
    o = (jnp.einsum('bhrjqk,brjkhe->brjqhe', p[..., :nw], vg)
         + jnp.einsum('bhrjqc,bche->brjqhe', p[..., nw:], vc))
    return o.reshape(B, S, H * E)

def mla_queries(part, gq, w_uq):
    B, L, _ = part.shape
    q = (rms_norm(part[..., :MLA_Q_RANK], gq) @ w_uq).reshape(B, L, MLA_HEADS, MLA_NOPE_DIM + MLA_ROPE_DIM)
    return q[..., :MLA_NOPE_DIM], q[..., MLA_NOPE_DIM:]

def mla_keys(part, gkv, w_ukv):
    B, L, _ = part.shape
    ckv = part[..., MLA_Q_RANK:MLA_Q_RANK + MLA_KV_RANK]
    k_rope = part[..., MLA_Q_RANK + MLA_KV_RANK:]
    kv = (rms_norm(ckv, gkv) @ w_ukv).reshape(B, L, MLA_HEADS, MLA_NOPE_DIM + MLA_V_DIM)
    return kv[..., :MLA_NOPE_DIM], k_rope, kv[..., MLA_NOPE_DIM:]

def mla_attend(q_nope, q_rope, k_nope, k_rope, v):
    s = (jnp.einsum('bqhd,bkhd->bhqk', q_nope, k_nope)
         + jnp.einsum('bqhr,bkr->bhqk', q_rope, k_rope)).astype(jnp.float32) * MLA_SCALE
    p = jax.nn.softmax(s, axis=-1).astype(v.dtype)
    return jnp.einsum('bhqk,bkhd->bqhd', p, v)

def blocked_mla(q_nope, q_rope, k_nope, k_rope, v):
    B, S, H, _ = q_nope.shape
    nb = S // ATTN_Q_BLOCK

    def to_blocks(a):
        return jnp.moveaxis(a.reshape(B, nb, ATTN_Q_BLOCK, *a.shape[2:]), 1, 0)

    out = lax.map(lambda qb: mla_attend(qb[0], qb[1], k_nope, k_rope, v),
                  (to_blocks(q_nope), to_blocks(q_rope)))
    return jnp.moveaxis(out, 0, 1).reshape(B, S, H * MLA_V_DIM)

def split_na(part):
    B, L, _ = part.shape
    return [t.reshape(B, L, NA_HEADS, NA_HEAD_DIM) for t in jnp.split(part, 3, axis=-1)]

def token_mixing(pl, pc, cos, sin, rows, pool_w, pool_s, rpb, sgu_g, sgu_w, sgu_b,
                 gq, w_uq, gkv, w_ukv, ctx_out):
    B = pl.shape[0]
    Lc = pc.shape[1]
    y_a = multiscale_pool(pl[..., :OFF_B], pool_w, pool_s)
    ql, kl, vl = split_na(pl[..., OFF_B:OFF_C])
    qc, kc, vc = split_na(pc[..., OFF_B:OFF_C])
    y_b = neighborhood_attention(ql, kl, vl, kc, vc, rpb, rows)
    y_c = spatial_gating(pl[..., OFF_C:OFF_D], sgu_g, sgu_w, sgu_b)
    dl, dc = pl[..., OFF_D:], pc[..., OFF_D:]
    qn_l, qr_l = mla_queries(dl, gq, w_uq)
    kn_l, kr_l, v_l = mla_keys(dl, gkv, w_ukv)
    kn_c, kr_c, v_c = mla_keys(dc, gkv, w_ukv)
    qr_l = rope_2d(qr_l, cos[:, None, :], sin[:, None, :])
    kr_l = rope_2d(kr_l, cos, sin)
    y_d = blocked_mla(qn_l, qr_l,
                      jnp.concatenate([kn_c, kn_l], axis=1),
                      jnp.concatenate([kr_c, kr_l], axis=1),
                      jnp.concatenate([v_c, v_l], axis=1))
    ml = jnp.concatenate([y_a, y_b, y_c, y_d], axis=-1)
    if not ctx_out:
        return ml, None
    yc_a = multiscale_pool(pc[..., :OFF_B], pool_w, pool_s)
    yc_b = dense_attention(qc, kc, vc).reshape(B, Lc, NA_WIDTH)
    yc_c = spatial_gating(pc[..., OFF_C:OFF_D], sgu_g, sgu_w, sgu_b)
    qn_c, qr_c = mla_queries(dc, gq, w_uq)
    yc_d = mla_attend(qn_c, qr_c, kn_c, kr_c, v_c).reshape(B, Lc, MLA_WIDTH)
    mc = jnp.concatenate([yc_a, yc_b, yc_c, yc_d], axis=-1)
    return ml, mc

def grouped_moe(h, router_w, router_b, w_gate, w_up, w_down):
    shp = h.shape
    ht = h.reshape(-1, shp[-1])
    scores = jax.nn.sigmoid((ht @ router_w).astype(jnp.float32))
    biased = scores + router_b.astype(jnp.float32)
    grp_score = lax.top_k(biased.reshape(-1, N_EXPERT_GROUPS, EXPERTS_PER_GROUP), TOP_K)[0].sum(-1)
    sel_group = jnp.argmax(grp_score, axis=-1)
    in_group = (jnp.arange(N_EXPERTS) // EXPERTS_PER_GROUP)[None, :] == sel_group[:, None]
    _, idx = lax.top_k(jnp.where(in_group, biased, NEG_INF), TOP_K)
    w = jnp.take_along_axis(scores, idx, axis=-1)
    w = w / jnp.sum(w, axis=-1, keepdims=True)
    gates = jnp.sum(jax.nn.one_hot(idx, N_EXPERTS, dtype=jnp.float32) * w[..., None], axis=1).astype(h.dtype)
    hid = jax.nn.silu(jnp.einsum('td,edf->tef', ht, w_gate)) * jnp.einsum('td,edf->tef', ht, w_up)
    y = jnp.einsum('tef,efd->td', hid * gates[:, :, None], w_down)
    return y.reshape(shp)

def setup_inputs(seed: int = 0) -> dict:
    key = jax.random.key(seed)
    ks = jax.random.split(key, 32)
    D = D_MODEL
    L = DEPTH

    def nrm(k, shape, s):
        return jax.random.normal(k, shape, jnp.float32) * s

    return {
        'x': nrm(ks[0], (BATCH, SEQ, D), 1.0),
        'c': nrm(ks[1], (BATCH, D), 1.0),
        'ctx': nrm(ks[2], (BATCH, CTX_LEN, D), 1.0),
        'c_ctx': nrm(ks[3], (D,), 1.0),
        'ada_w': nrm(ks[4], (L, D, N_MOD * D), 0.5 * D ** -0.5),
        'ada_b': nrm(ks[5], (L, N_MOD * D), 0.02),
        'norm1_g': 1.0 + nrm(ks[6], (L, D), 0.02),
        'norm2_g': 1.0 + nrm(ks[7], (L, D), 0.02),
        'w_in': nrm(ks[8], (L, D, IN_WIDTH), D ** -0.5),
        'w_out': nrm(ks[9], (L, MIX_WIDTH, D), MIX_WIDTH ** -0.5),
        'pool_w': nrm(ks[10], (L, POOL_GROUPS, POOL_GROUP_DIM, POOL_GROUP_DIM), POOL_GROUP_DIM ** -0.5),
        'pool_s': 1.0 + nrm(ks[11], (L, POOL_WIDTH), 0.1),
        'na_rpb': nrm(ks[12], (L, NA_HEADS, 2 * NA_WIN_ROWS - 1, 2 * NA_WIN_COLS - 1), 0.1),
        'sgu_norm_g': 1.0 + nrm(ks[13], (L, SGU_WIDTH), 0.02),
        'sgu_w': nrm(ks[14], (L, SGU_GROUPS, SGU_CHUNK, SGU_CHUNK), SGU_CHUNK ** -0.5),
        'sgu_b': 1.0 + nrm(ks[15], (L, SGU_GROUPS, SGU_CHUNK), 0.02),
        'mla_q_norm_g': 1.0 + nrm(ks[16], (L, MLA_Q_RANK), 0.02),
        'mla_w_uq': nrm(ks[17], (L, MLA_Q_RANK, MLA_HEADS * (MLA_NOPE_DIM + MLA_ROPE_DIM)), MLA_Q_RANK ** -0.5),
        'mla_kv_norm_g': 1.0 + nrm(ks[18], (L, MLA_KV_RANK), 0.02),
        'mla_w_ukv': nrm(ks[19], (L, MLA_KV_RANK, MLA_HEADS * (MLA_NOPE_DIM + MLA_V_DIM)), MLA_KV_RANK ** -0.5),
        'router_w': nrm(ks[20], (D, N_EXPERTS), D ** -0.5),
        'router_b': nrm(ks[21], (N_EXPERTS,), 0.01),
        'moe_w_gate': nrm(ks[22], (L, N_EXPERTS, D, D_EXPERT), D ** -0.5),
        'moe_w_up': nrm(ks[23], (L, N_EXPERTS, D, D_EXPERT), D ** -0.5),
        'moe_w_down': nrm(ks[24], (L, N_EXPERTS, D_EXPERT, D), D_EXPERT ** -0.5),
        'final_g': 1.0 + nrm(ks[25], (D,), 0.02),
    }

def reference(x, c, ctx, c_ctx, ada_w, ada_b, norm1_g, norm2_g, w_in, w_out, pool_w, pool_s, na_rpb,
              sgu_norm_g, sgu_w, sgu_b, mla_q_norm_g, mla_w_uq, mla_kv_norm_g, mla_w_ukv,
              router_w, router_b, moe_w_gate, moe_w_up, moe_w_down, final_g):
    B, S, _ = x.shape
    rows = S // GRID_W
    cos, sin = axial_rope_tables(S)
    xl, xc = x, ctx
    for l in range(DEPTH):
        ctx_out = l < DEPTH - 1
        mod_l = jnp.split((jax.nn.silu(c) @ ada_w[l] + ada_b[l])[:, None, :], N_MOD, axis=-1)
        mod_c = jnp.split(jax.nn.silu(c_ctx) @ ada_w[l] + ada_b[l], N_MOD, axis=-1)
        pl = modulate(rms_norm(xl, norm1_g[l]), mod_l[0], mod_l[1]) @ w_in[l]
        pc = modulate(rms_norm(xc, norm1_g[l]), mod_c[0], mod_c[1]) @ w_in[l]
        ml, mc = token_mixing(pl, pc, cos, sin, rows, pool_w[l], pool_s[l], na_rpb[l],
                              sgu_norm_g[l], sgu_w[l], sgu_b[l],
                              mla_q_norm_g[l], mla_w_uq[l], mla_kv_norm_g[l], mla_w_ukv[l], ctx_out)
        xl = xl + mod_l[2] * (ml @ w_out[l])
        hl = modulate(rms_norm(xl, norm2_g[l]), mod_l[3], mod_l[4])
        xl = xl + mod_l[5] * grouped_moe(hl, router_w, router_b, moe_w_gate[l], moe_w_up[l], moe_w_down[l])
        if ctx_out:
            xc = xc + mod_c[2] * (mc @ w_out[l])
            hc = modulate(rms_norm(xc, norm2_g[l]), mod_c[3], mod_c[4])
            xc = xc + mod_c[5] * grouped_moe(hc, router_w, router_b, moe_w_gate[l], moe_w_up[l], moe_w_down[l])
    return rms_norm(xl, final_g)


_drawn_inputs = setup_inputs


def setup_inputs(seed=0):
    import zlib

    import numpy as np

    out = dict(_drawn_inputs(seed))
    spreads = {}
    factors = {'norm1_g': 2.975,
     'na_rpb': 8.0,
     'sgu_norm_g': 5.553,
     'sgu_b': 3.176,
     'mla_q_norm_g': 8.0,
     'mla_kv_norm_g': 5.774,
     'final_g': 2.81}
    for name, (base, spread) in spreads.items():
        noise = np.random.default_rng([zlib.crc32(name.encode()), seed]).standard_normal(out[name].shape)
        drawn = base * np.exp(spread * noise) if base else spread * noise
        out[name] = __import__('jax').numpy.asarray(drawn.astype(out[name].dtype))
    for name, factor in factors.items():
        out[name] = (out[name] * factor).astype(out[name].dtype)
    return out
```

```python
from contextlib import ExitStack

import numpy as np

import concourse.bass as bass
from concourse import mybir

F32 = mybir.dt.float32
F32R = mybir.dt.float32r
ALU = mybir.AluOpType
ACT = mybir.ActivationFunctionType
AX = mybir.AxisListType

P = 128
D = 1024
KC = D // P
S = 256
T = 2 * S
DEPTH = 2
GRID = 64
ROWS = S // GRID
IN_W = 1952
HEADS = 4
E = 16
FE = 256
WIN_COLS = 16
NOPE, ROPE = 64, 32
QK = NOPE + ROPE
MLA_SCALE = float(QK) ** -0.5
NA_SCALE = 64.0 ** -0.5
EPS = 1e-6
NEG = -1e30
PAD = 8
PW = S + 2 * PAD

BW = 256
N_ADA, N_WIN, N_WOUT = 24, 8, 4
N_MOE = 3 * E
PER_LAYER = N_ADA + N_WIN + N_WOUT + N_MOE
SPLIT_PER_LAYER = PER_LAYER - N_ADA
RAW = 6
HL = 3

C_ID, C_FLIP, C_ONE, C_NEGM, C_INV, C_COS, C_SIN, C_RANK, C_EPS = np.cumsum(
    [0, P, P, P, GRID, 2 * S, S, S, 64]).tolist()
N_CONST = C_EPS + 2
V_ADAB, V_C = 0, DEPTH * 48
V_N1 = V_C + 16
V_N2 = V_N1 + DEPTH * KC
V_FIN = V_N2 + DEPTH * KC
V_PS = V_FIN + KC
V_QG = V_PS + 2 * DEPTH
V_KVG = V_QG + 2 * DEPTH
V_SB = V_KVG + DEPTH
N_VEC = V_SB + 4 * DEPTH


def constants():
    c = np.zeros((P, N_CONST), np.float32)
    c[:, C_ID:C_ID + P] = np.eye(P)
    for p in range(P):
        c[p, C_FLIP + (p // GRID) * GRID + GRID - 1 - p % GRID] = 1
    c[:, C_ONE:C_ONE + P] = 1
    for p in range(P):
        qc = GRID - 1 - p % GRID
        ws = min(max(qc - WIN_COLS // 2, 0), GRID - WIN_COLS)
        kc = np.arange(GRID)
        c[p, C_NEGM:C_NEGM + GRID] = np.where((kc >= ws) & (kc < ws + WIN_COLS), 0, NEG)
    t = np.arange(S)
    for g, w in enumerate((2, 4, 8, 16)):
        n = np.clip(t - w // 2 + w, 0, S) - np.clip(t - w // 2, 0, S)
        half, ch = g % 2, g // 2
        c[half * 64:half * 64 + 64, C_INV + ch * S:C_INV + (ch + 1) * S] = (1.0 / n.astype(np.float64)).astype(np.float32)
    nf = ROPE // 4
    inv = (np.float32(10000.0) ** (-np.arange(nf, dtype=np.float32) / np.float32(nf))).astype(np.float32)
    ang = np.concatenate([(t // GRID).astype(np.float32)[:, None] * inv, (t % GRID).astype(np.float32)[:, None] * inv], 1)
    cos, sin = np.cos(ang).T, np.sin(ang).T
    for part in range(2):
        for half in range(2):
            r = NOPE + part * 2 * nf + half * nf
            c[r:r + nf, C_COS:C_COS + S] = cos[part * nf:(part + 1) * nf]
            c[r:r + nf, C_SIN:C_SIN + S] = sin[part * nf:(part + 1) * nf] * (-1 if half == 0 else 1)
    c[:, C_RANK:C_RANK + 64] = np.tile(np.array([3, 2, 1, 0], np.float32), 16)
    c[:, C_EPS] = EPS
    return c


def build(nc, a, out):
    with ExitStack() as ctx:
        def sem(name):
            return ctx.enter_context(nc.semaphore(name))

        at = [16512]

        def sb(name, shape, dt=F32, offset=None):
            size = int(np.prod(shape[1:])) * 4
            if offset is None:
                offset = at[0]
                at[0] += (size + 31) // 32 * 32
            return nc.alloc_sbuf_tensor_at(name, shape, dt, offset=offset)

        class Region:

            def __init__(self, base, size):
                self.at, self.end = base, base + size

            def sb(self, name, shape, dt=F32):
                size = (int(np.prod(shape[1:])) * 4 + 31) // 32 * 32
                t = nc.alloc_sbuf_tensor_at(name, shape, dt, offset=self.at)
                self.at += size
                assert self.at <= self.end, name
                return t

        const = sb("const", [P, N_CONST])
        vec = sb("vec", [P, N_VEC])
        x_t = sb("x_t", [P, KC, T])
        raw = [sb(f"raw{i}", [P, KC, BW]) for i in range(RAW)]
        ring_at = at[0]
        w_hi = [sb(f"w_hi{i}", [P, KC, BW], F32R) for i in range(HL)]
        w_lo = [sb(f"w_lo{i}", [P, KC, BW], F32R) for i in range(HL)]
        ring_size = at[0] - ring_at
        h_at = at[0]
        h_hi = sb("h_hi", [P, KC, T], F32R)
        h_lo = sb("h_lo", [P, KC, T], F32R)
        h_size = at[0] - h_at
        pool_bd = sb("pool_bd", [P, 2, P])
        w_uq = sb("w_uq", [P, 2, HEADS * QK])
        w_uqs = sb("w_uqs", [P, 2, HEADS, QK])
        w_ukv = sb("w_ukv", [P, 4 * P])
        sgu_w = sb("sgu_w", [P, 4, P])
        sgu_wt = sb("sgu_wt", [P, 4, P])
        na_bias = sb("na_bias", [P, HEADS, 6, GRID])
        sgu_g = sb("sgu_g", [P, S])
        rb_row = sb("rb_row", [P, E])
        rw_hi = sb("rw_hi", [P, KC, E], F32R)
        rw_lo = sb("rw_lo", [P, KC, E], F32R)
        c_act = sb("c_act", [P, 16])
        mod = sb("mod", [P, 2, 48])
        amp = sb("amp", [P, 2, 2, KC])
        mod_row = sb("mod_row", [2, 2, BW])
        col = sb("col", [P, 64])
        rstd = sb("rstd", [P, 4])
        stat = sb("stat", [P, 4, 3])
        area_at = at[0]
        area_size = 33024
        at[0] += area_size
        assert at[0] <= 229344, at[0]

        A = Region(area_at, area_size)
        a_pad = A.sb("a_pad", [P, 2, 2, PW])
        q_na = A.sb("q_na", [P, 2, T])
        k_na = A.sb("k_na", [P, 2, T])
        v_na = A.sb("v_na", [P, 4, S])
        sgu_u = A.sb("sgu_u", [P, 4, S])
        sgu_v = A.sb("sgu_v", [P, 4, S])
        q_low = A.sb("q_low", [P, 2, T])
        kv_low = A.sb("kv_low", [P, T])
        k_rope = A.sb("k_rope", [P, T])
        N = Region(area_at, area_size)
        nsq = N.sb("nsq", [P, 4, T])
        nx = N.sb("nx", [P, 2, T])
        nh = N.sb("nh", [P, 2, T])
        I = Region(area_at + 4096, area_size - 4096)
        x_tok = [I.sb(f"x_tok{t}", [P, D]) for t in range(4)]
        M = Region(area_at, area_size)
        hid_hi = M.sb("hid_hi", [P, 2, T], F32R)
        hid_lo = M.sb("hid_lo", [P, 2, T], F32R)
        hid_s = M.sb("hid_s", [P, 2, T])
        hid_t = M.sb("hid_t", [P, 2, T])
        gcol = M.sb("gcol", [P, 4, P])
        logit = M.sb("logit", [P, 4, E])
        score = M.sb("score", [P, 4, E])
        biased = M.sb("biased", [P, 4, E])
        rank = M.sb("rank", [P, 4, E])
        cmp = M.sb("cmp", [P, 4, E])
        grp = M.sb("grp", [P, 4, 4])
        grank = M.sb("grank", [P, 4, 4])
        gates = sb("gates", [P, 4, E])
        B = Region(ring_at, ring_size)
        o_tok = B.sb("o_tok", [P, 4, 3 * S])
        v_mla = B.sb("v_mla", [P, 4, S])
        pool_d = B.sb("pool_d", [P, 2, T])
        prob = [B.sb(f"prob{i}", [P, T]) for i in range(3)]
        prob_t = [B.sb(f"prob_t{i}", [P, 4, P]) for i in range(3)]
        sgu_sq = B.sb("sgu_sq", [P, 4, S])
        win_a = B.sb("win_a", [P, 2, 2, PW])
        win_b = B.sb("win_b", [P, 2, 2, PW])
        H = Region(h_at, h_size)
        q_mla = H.sb("q_mla", [P, HEADS, T])
        k_mla = H.sb("k_mla", [P, HEADS, T])
        low_sq = H.sb("low_sq", [P, 3, T])
        rope_t = H.sb("rope_t", [P, HEADS, S])
        raw_vec = [nc.alloc_sbuf_tensor_at(f"raw_vec{i}", [P, P], F32, offset=area_at + i * 512) for i in range(2)]
        rw_in = nc.alloc_sbuf_tensor_at("rw_in", [P, KC, E], F32, offset=area_at + 1024)

        y_tok = nc.alloc_sbuf_tensor_at("y_tok", [P, 2, D], F32, offset=ring_at)

        ident = const[:, C_ID:C_ID + P]
        ones = const[:, C_ONE:C_ONE + P]
        eps = const[:, C_EPS:C_EPS + 1]

        bank = [ctx.enter_context(nc.psum_tensor(f"bank{i}", [P, 512], F32)) for i in range(8)]

        loaded = [sem(f"loaded{i}") for i in range(RAW)]
        s_const, s_vecin, s_xin, s_xevd = sem("s_const"), sem("s_vecin"), sem("s_xin"), sem("s_xevd")
        s_bcast = sem("s_bcast")
        s_small, s_zero = sem("s_small"), sem("s_zero")
        s_vt, s_vec, s_cact = sem("s_vt"), sem("s_vec"), sem("s_cact")
        s_xt, s_xev = sem("s_xt"), sem("s_xev")
        s_rw = sem("s_rw")
        split_hi, split_lo, used = sem("split_hi"), sem("split_lo"), sem("used")
        ada_mm, ada_ea, ada_ed, ada_tr, s_mod, s_amp = sem("ada_mm"), sem("ada_ea"), sem("ada_ed"), sem("ada_tr"), sem("s_mod"), sem("s_amp")
        NORMS = 2 * DEPTH + 1
        n_sqa, n_sqd, n_sum, n_root, n_rstd, n_bc, n_x, n_hi, n_lo = (sem(n) for n in (
            "n_sqa", "n_sqd", "n_sum", "n_root", "n_rstd", "n_bc", "n_x", "n_hi", "n_lo"))
        n_h = [sem(f"n_h{i}") for i in range(2 * DEPTH + 1)]
        chain_d, chain_p = sem("chain_d"), sem("chain_p")
        s_swap, s_pads, s_wg, s_bias, s_pool = (sem(n) for n in ("s_swap", "s_pads", "s_wg", "s_bias", "s_pool"))
        proj_ea, proj_ed = sem("proj_ea"), sem("proj_ed")
        s_wt, s_wte = sem("s_wt"), sem("s_wte")
        s_lsq, s_lsum, s_lroot, s_lrstd, s_lbc, s_low = (sem(n) for n in (
            "s_lsq", "s_lsum", "s_lroot", "s_lrstd", "s_lbc", "s_low"))
        s_up, s_qe, s_ke, s_ve, s_rot = (sem(n) for n in ("s_up", "s_qe", "s_ke", "s_ve", "s_rot"))
        s_gv, s_groot, s_gn, s_mix, s_go = (sem(n) for n in ("s_gv", "s_groot", "s_gn", "s_mix", "s_go"))
        t_sc, t_mx, t_ex, t_tr, t_pa, t_pd, t_pv, t_o = (sem(n) for n in (
            "t_sc", "t_mx", "t_ex", "t_tr", "t_pa", "t_pd", "t_pv", "t_o"))
        m_ps, m_hi, m_lo, o_ev = sem("m_ps"), sem("m_hi"), sem("m_lo"), sem("o_ev")
        r_lg, r_sg, r_gate = sem("r_lg"), sem("r_sg"), sem("r_gate")
        e_gc, e_gb, e_s, e_m, e_t, e_hi, e_lo, e_d, e_x = (sem(n) for n in (
            "e_gc", "e_gb", "e_s", "e_m", "e_t", "e_hi", "e_lo", "e_d", "e_x"))
        f_y, f_ev, f_out = sem("f_y"), sem("f_ev"), sem("f_out")

        def streams(l):
            return 2 if l < DEPTH - 1 else 1

        def split_index(l, r):
            return l * SPLIT_PER_LAYER + r - N_ADA

        def raw_index(l, r):
            return l * PER_LAYER + r

        def block_cols(r):
            return IN_W - 7 * BW + ROPE if r == N_ADA + 7 else BW

        def attention_jobs(l):
            jobs = [("na", h, t) for h in range(HEADS) for t in (0, 1)]
            if streams(l) == 2:
                jobs += [("na", h, t) for h in range(HEADS) for t in (2, 3)]
            jobs += [("mla", h, t) for h in range(HEADS) for t in (0, 1)]
            if streams(l) == 2:
                jobs += [("mla", h, t) for h in range(HEADS) for t in (2, 3)]
            return jobs

        SMALL = 8

        JOBS = 32

        def done(l, r):
            return split_index(l, r) + 1

        ada_w, w_in, w_out = a["ada_w"], a["w_in"], a["w_out"]
        w_gate, w_up, w_down = a["moe_w_gate"], a["moe_w_up"], a["moe_w_down"]

        block = ctx.enter_context(nc.Block())

        @block.sync
        def _(sp):
            def free_slot(l, r):
                n = raw_index(l, r) - RAW
                if n < 0:
                    return
                pl, pr = divmod(n, PER_LAYER)
                if pr < N_ADA:
                    sp.wait_ge(ada_mm, pl * N_ADA + pr + 1)
                else:
                    sp.wait_ge(split_hi, split_index(pl, pr) + 1)
                    sp.wait_ge(split_lo, split_index(pl, pr) + 1)

            for l in range(DEPTH):
                for r in range(N_ADA + N_WIN + N_WOUT):
                    free_slot(l, r)
                    n = raw_index(l, r)
                    if r < N_ADA:
                        src, c0, w = ada_w[l], r * BW, BW
                    elif r < N_ADA + N_WIN:
                        src, c0 = w_in[l], (r - N_ADA) * BW
                        w = min(BW, IN_W - c0)
                    else:
                        src, c0, w = w_out[l], (r - N_ADA - N_WIN) * BW, BW
                    sp.dma_start(raw[n % RAW][:, :, 0:w],
                                 src[:, c0:c0 + w].rearrange("(k p) n -> p k n", p=P)).then_inc(loaded[n % RAW], 16)
                first = raw_index(l, N_ADA + N_WIN + N_WOUT)
                assert first % RAW == 0
                s0 = split_index(l, N_ADA + N_WIN + N_WOUT)
                with sp.Fori(0, E // 2) as i:
                    for j in range(2):
                        for role, w in enumerate((w_gate, w_up, w_down)):
                            slot = 3 * j + role
                            sp.wait_ge(split_hi, i * RAW + (s0 + slot - RAW + 1))
                            sp.wait_ge(split_lo, i * RAW + (s0 + slot - RAW + 1))
                            src = w[l][bass.ds(2 * i + j, 1)]
                            if role < 2:
                                src = src.rearrange("a (k p) n -> p (a k) n", p=P)
                                dst = raw[slot][:, :, :]
                            else:
                                src = src.rearrange("a (f p) n -> p (a f) n", p=P)
                                dst = raw[slot][:, :, :].rearrange("p (f k) n -> p f (k n)", f=2)
                            sp.dma_start(dst, src).then_inc(loaded[slot], 16)
            for t in range(2):
                sp.wait_ge(f_ev, 4)
                sp.dma_start(out[t * P:(t + 1) * P, :], y_tok[:, t, :]).then_inc(f_out, 16)
            sp.wait_ge(f_out, 32)


        @block.gpsimd
        def _(pool):
            made = [0]

            def then(ins):
                made[0] += 1
                ins.then_inc(chain_p, 1)
                pool.wait_ge(chain_p, made[0])

            for l in range(DEPTH):
                ns = streams(l)
                if l:
                    pool.wait_ge(m_ps, (l - 1) * (KC) + 2)
                pool.memset(pool_bd[:, :, :], 0.0).then_inc(s_zero, 1)
                pool.wait_ge(s_small, l * (16 * SMALL) + 16 * SMALL)
                pool.wait_ge(s_vec, 1)
                for c in range(2):
                    pool.tensor_scalar(w_uq[:, c, :], w_uq[:, c, :], vec[:, V_QG + 2 * l + c:V_QG + 2 * l + c + 1], 1.0,
                                       ALU.mult, ALU.mult)
                then(pool.tensor_scalar(w_ukv[:, :], w_ukv[:, :], vec[:, V_KVG + l:V_KVG + l + 1], 1.0, ALU.mult, ALU.mult))
                w4 = w_uq[:, :, :].rearrange("p c (h m) -> p c h m", m=QK)
                for c in range(2):
                    pool.tensor_copy(w_uqs[:, c, :, 0:NOPE], w4[:, c, :, 0:NOPE])
                    for half in range(2):
                        for part in range(2):
                            to, fr = NOPE + 16 * part + 8 * half, NOPE + 16 * part + 8 * (1 - half)
                            last = pool.tensor_copy(w_uqs[:, c, :, to:to + 8], w4[:, c, :, fr:fr + 8])
                last.then_inc(s_wg, 1)
                for h in range(HEADS):
                    last = pool.tensor_tensor(na_bias[:, h, :, :], na_bias[:, h, :, :],
                                              const[:, C_NEGM:C_NEGM + GRID][:, None, :].to_broadcast([P, 6, GRID]), ALU.add)
                last.then_inc(s_bias, 1)
                n = raw_index(l, N_ADA + 7)
                pool.wait_ge(loaded[n % RAW], 16 * (n // RAW + 1))
                rk = raw[n % RAW]
                for half in range(2):
                    for part in range(2):
                        to, fr = 160 + 16 * part + 8 * half, 128 + 16 * part + 8 * (1 - half)
                        last = pool.tensor_copy(rk[:, :, to:to + 8], rk[:, :, fr:fr + 8])
                last.then_inc(s_swap, 1)
                pool.wait_ge(used, done(l, N_ADA))
                pool.memset(a_pad[:, :, :, 0:PAD], 0.0)
                pool.memset(a_pad[:, :, :, PAD + S:PW], 0.0).then_inc(s_pads, 1)
                pool.wait_ge(proj_ed, l * 5 + 1)
                pool.wait_ge(s_pads, l + 1)
                pool.wait_ge(used, split_index(l, N_ADA + 7) + 1)

                def window(dst, src, ch, p0, lo, hi, back, ahead):
                    return pool.tensor_tensor(dst[p0:P, ch, 0:ns, lo:hi], src[p0:P, ch, 0:ns, lo - back:hi - back],
                                              src[p0:P, ch, 0:ns, lo + ahead:hi + ahead], ALU.add)

                window(win_a, a_pad, 0, 0, 1, PW, 1, 0)
                then(window(win_a, a_pad, 1, 0, 1, PW, 1, 0))
                then(window(win_b, win_a, 0, 64, 2, PW - 1, 1, 1))
                then(window(win_b, win_a, 1, 0, 2, PW - 1, 1, 1))
                then(window(win_a, win_b, 1, 0, 4, PW - 3, 2, 2))
                then(window(win_b, win_a, 1, 64, 8, PW - 8, 4, 4))
                for g, w in enumerate((win_a, win_b, win_a, win_b)):
                    ch, p0 = g // 2, 64 * (g % 2)
                    sl = w[p0:p0 + 64, ch, 0:ns, PAD:PAD + S]
                    inv = const[p0:p0 + 64, C_INV + ch * S:C_INV + (ch + 1) * S][:, None, :].to_broadcast([64, ns, S])
                    then(pool.tensor_tensor(sl, sl, inv, ALU.mult))
                for g, w in enumerate((win_a, win_b, win_a, win_b)):
                    ch, p0 = g // 2, 64 * (g % 2)
                    ins = pool.tensor_tensor(pool_d[p0:p0 + 64, ch, 0:ns * S].rearrange("p (s t) -> p s t", s=ns),
                                             w[p0:p0 + 64, ch, 0:ns, PAD:PAD + S],
                                             a_pad[p0:p0 + 64, ch, 0:ns, PAD:PAD + S], ALU.subtract)
                    if g < 3:
                        then(ins)
                ins.then_inc(s_pool, 1)

        @block.scalar
        def _(act):
            def small_loads(l):
                if l:
                    act.wait_ge(m_ps, (l - 1) * (KC) + 8)
                act.wait_ge(s_zero, l + 1)
                pw = a["pool_w"]
                for half in range(2):
                    src = bass.AP(pw.tensor, (l * 4 + half) * 4096, [[64, 64], [8192, 2], [1, 64]])
                    act.dma_start(pool_bd[64 * half:64 * half + 64, :, 64 * half:64 * half + 64], src).then_inc(s_small, 16)
                act.dma_start(w_uq[:, :, :], a["mla_w_uq"][l].rearrange("(c p) n -> p c n", p=P)).then_inc(s_small, 16)
                act.dma_start(w_ukv[:, :], a["mla_w_ukv"][l]).then_inc(s_small, 16)
                act.dma_start(sgu_g[:, :], bass.AP(a["sgu_norm_g"].tensor, l * S, [[0, P], [1, S]])).then_inc(s_small, 16)
                act.dma_start(sgu_w[:, :, :], a["sgu_w"][l].rearrange("g p q -> p g q")).then_inc(s_small, 16)
                rp = a["na_rpb"]
                for half in range(2):
                    src = bass.AP(rp.tensor, (2 * l + half) * HEADS * 6 * P, [[1, GRID], [P, HEADS * 6], [1, GRID]])
                    act.dma_start(na_bias[64 * half:64 * half + 64, :, :, :].rearrange("p h r c -> p (h r) c"), src).then_inc(s_small, 16)

            act.dma_start(const[:, :], a["const"]).then_inc(s_const, 16)
            for t in range(4):
                act.dma_start(x_tok[t][:, :], a["x" if t < 2 else "ctx"][(t % 2) * P:(t % 2 + 1) * P, :]).then_inc(s_xin, 16)
            act.dma_start(raw_vec[0][0:112, :], a["vec0"]).then_inc(s_vecin, 16)
            act.dma_start(raw_vec[1][0:N_VEC - 112, :], a["vec1"]).then_inc(s_vecin, 16)
            act.dma_start(rw_in[:, :, :], a["router_w"].rearrange("(k p) e -> p k e", p=P)).then_inc(s_bcast, 16)
            act.dma_start(rb_row[:, :], bass.AP(a["router_b"].tensor, 0, [[0, P], [1, E]])).then_inc(s_bcast, 16)
            small_loads(0)
            act.wait_ge(s_vec, 1)
            act.activation(c_act[:, :], vec[:, V_C:V_C + 16], ACT.Silu).then_inc(s_cact, 1)
            act.wait_ge(s_bcast, 32)
            act.activation(rw_hi[:, :, :], rw_in[:, :, :], ACT.Copy).then_inc(s_rw, 1)

            def split(l, r):
                s, n = split_index(l, r), raw_index(l, r)
                act.wait_ge(loaded[n % RAW], 16 * (n // RAW + 1))
                if r == N_ADA + 7:
                    act.wait_ge(s_swap, l + 1)
                if s >= HL:
                    act.wait_ge(used, s - HL + 1)
                w = block_cols(r)
                act.activation(w_hi[s % HL][:, :, 0:w], raw[n % RAW][:, :, 0:w], ACT.Copy).then_inc(split_hi, 1)

            def norm(i, width, which, l):
                ns = width // S
                if i % 2:
                    act.wait_ge(o_ev, l * KC + KC)
                if which is None:
                    act.wait_ge(e_x, (DEPTH - 1) * (KC * E) + KC * E)
                for k in range(0, KC, 2):
                    if k >= 4:
                        act.wait_ge(n_sum, i * KC + k - 3)
                    act.activation(nsq[:, k % 4, 0:width], x_t[:, k, 0:width], ACT.Square).then_inc(n_sqa, 1)
                act.wait_ge(n_sum, i * KC + KC)
                act.activation(col[:, 0:width // P], bank[6][:, 0:width // P], ACT.Sqrt, bias=eps, scale=1.0 / D).then_inc(n_root, 1)
                for k in range(KC):
                    act.wait_ge(n_x, i * KC + k + 1)
                    if k >= 2:
                        if which is None:
                            act.wait_ge(f_y, k - 1)
                        else:
                            act.wait_ge(n_lo, i * KC + k - 1)
                    if which is None:
                        act.activation(nh[:, k % 2, 0:width], nx[:, k % 2, 0:width], ACT.Identity,
                                       scale=vec[:, V_FIN + k:V_FIN + k + 1]).then_inc(n_h[i], 1)
                        continue
                    for s in range(ns):
                        act.activation(nh[:, k % 2, s * S:(s + 1) * S], nx[:, k % 2, s * S:(s + 1) * S], ACT.Identity,
                                       bias=mod[:, s, 24 * which + k:24 * which + k + 1],
                                       scale=amp[:, which, s, k:k + 1]).then_inc(n_h[i], 1)
                    act.wait_ge(n_h[i], ns * (k + 1))
                    act.activation(h_hi[:, k, 0:width], nh[:, k % 2, 0:width], ACT.Copy).then_inc(n_hi, 1)

            for l in range(DEPTH):
                ns = streams(l)
                nt, width = 2 * ns, ns * S
                for j in range(1, N_ADA, 2):
                    act.wait_ge(ada_mm, l * N_ADA + j + 1)
                    if j >= 2:
                        act.wait_ge(ada_tr, l * N_ADA + j - 1)
                    act.activation(mod_row[:, j % 2, :], bank[j % 4][0:2, 0:BW], ACT.Copy).then_inc(ada_ea, 1)
                    if l == 0 and 4 <= j < 12:
                        k = j - 4
                        act.wait_ge(s_xt, k + 1)
                        act.activation(x_t[:, k, :], bank[4 + k % 3][:, :], ACT.Copy).then_inc(s_xev, 1)
                for r in range(N_ADA, N_ADA + HL):
                    split(l, r)
                act.wait_ge(s_amp, l + 1)
                norm(2 * l, T, 0, l)
                for b in range(N_WIN):
                    if b == 1:
                        act.wait_ge(used, done(l, N_ADA + 1))
                        act.activation(q_na[:, 0, 0:width], bank[2][:, 0:width], ACT.Copy, scale=NA_SCALE)
                        act.activation(q_na[:, 1, 0:width], bank[3][:, 0:width], ACT.Copy, scale=NA_SCALE).then_inc(proj_ea, 1)
                    if b in (4, 5):
                        act.wait_ge(used, done(l, N_ADA + b))
                        dst = sgu_u if b == 4 else sgu_v
                        for s in range(ns):
                            last = act.activation(dst[:, 2 * s:2 * s + 2, :].rearrange("p t n -> p (t n)"),
                                                  bank[2 * (b % 4) + s][:, :], ACT.Gelu_apprx_tanh)
                        last.then_inc(proj_ea, 1)
                    if b == 7:
                        act.wait_ge(used, done(l, N_ADA + 7))
                        act.activation(kv_low[:, :], bank[6][:, :], ACT.Copy).then_inc(proj_ea, 1)
                    if b + HL < N_WIN:
                        split(l, N_ADA + b + HL)
                act.wait_ge(used, split_index(l, N_ADA + 7) + 1)
                act.wait_ge(proj_ed, l * 5 + 4)
                act.activation(low_sq[:, 0:2, 0:width], q_low[:, :, 0:width], ACT.Square).then_inc(s_lsq, 1)
                act.wait_ge(proj_ea, l * 4 + 4)
                act.activation(low_sq[:, 2, :], kv_low[:, :], ACT.Square).then_inc(s_lsq, 1)
                act.wait_ge(s_lsum, l + 1)
                act.activation(col[:, 8:8 + nt], bank[7][:, 0:nt], ACT.Sqrt, bias=eps, scale=1.0 / 256)
                act.activation(col[:, 12:16], bank[7][:, 4:8], ACT.Sqrt, bias=eps, scale=1.0 / P).then_inc(s_lroot, 1)
                act.wait_ge(s_gv, l + 1)
                act.activation(col[:, 32:32 + 4 * nt], col[:, 16:16 + 4 * nt], ACT.Sqrt, bias=eps, scale=1.0 / 64).then_inc(s_groot, 1)
                act.wait_ge(s_wt, l + 1)
                act.activation(sgu_wt[:, :, :].rearrange("p g n -> p (g n)"), bank[6][:, :], ACT.Copy).then_inc(s_wte, 1)
                for h in range(HEADS):
                    act.wait_ge(s_up, l * 11 + h + 1)
                    act.activation(q_mla[0:QK, h, 0:width], bank[2 + h][0:QK, 0:width], ACT.Copy, scale=MLA_SCALE).then_inc(s_qe, 1)
                for h in range(HEADS):
                    act.wait_ge(s_up, l * 11 + 6 + h + 1)
                    act.activation(k_mla[0:NOPE, h, :], bank[h][0:NOPE, :], ACT.Copy).then_inc(s_ke, 1)
                act.wait_ge(s_up, l * 11 + 11)
                act.activation(v_mla[:, 0:2, :].rearrange("p t n -> p (t n)"), bank[4][:, :], ACT.Copy)
                act.activation(v_mla[:, 2:4, :].rearrange("p t n -> p (t n)"), bank[5][:, :], ACT.Copy).then_inc(s_ve, 1)
                jobs = attention_jobs(l)
                for i in range(len(jobs) + 1):
                    if i < len(jobs):
                        nk = T if jobs[i][2] < 2 else S
                        act.wait_ge(t_mx, l * JOBS + i + 1)
                        if i >= 3:
                            act.wait_ge(t_tr, l * JOBS + i - 2)
                        act.activation(prob[i % 3][:, 0:nk], bank[i % 3][:, 0:nk], ACT.Exp, bias=stat[:, i % 4, 0:1],
                                       accum_out=stat[:, i % 4, 1:2]).then_inc(t_ex, 1)
                    if i >= 1 and i % 2 == 1:
                        q = i - 1
                        nkt = 4 if jobs[q][2] < 2 else 2
                        act.wait_ge(t_tr, l * JOBS + q + 1)
                        if q >= 3:
                            act.wait_ge(t_pv, l * JOBS + q - 2)
                        act.activation(prob_t[q % 3][:, 0:nkt, :].rearrange("p k n -> p (k n)"),
                                       bank[3 + q % 2][:, 0:nkt * P], ACT.Copy).then_inc(t_pa, 1)
                for c in range(KC):
                    act.wait_ge(m_ps, l * KC + c + 1)
                    if c == 0:
                        act.wait_ge(t_pv, l * JOBS + len(jobs))
                    scale = vec[:, V_PS + 2 * l + c:V_PS + 2 * l + c + 1] if c < 2 else 1.0
                    act.activation(h_hi[:, c, 0:width], bank[c][:, 0:width], ACT.Identity if c < 2 else ACT.Copy,
                                   scale=scale).then_inc(m_hi, 1)
                for r in range(N_ADA + N_WIN, N_ADA + N_WIN + N_WOUT):
                    split(l, r)
                if l + 1 < DEPTH:
                    small_loads(l + 1)
                norm(2 * l + 1, width, 1, l)
                act.wait_ge(r_lg, l + 1)
                act.activation(score[:, 0:nt, :].rearrange("p t e -> p (t e)"), bank[5][:, 0:nt * E], ACT.Sigmoid).then_inc(r_sg, 1)

                s0 = split_index(l, N_ADA + N_WIN + N_WOUT)
                r0 = raw_index(l, N_ADA + N_WIN + N_WOUT)

                def expert(e, i, j, ahead):
                    def sp_(i2, j2, role):
                        act.wait_ge(loaded[3 * j2 + role], 16 * i2 + 16 * (r0 // RAW + 1))
                        act.wait_ge(used, 6 * i2 + (3 * j2 + s0 + role - HL + 1))
                        act.activation(w_hi[role][:, :, :], raw[3 * j2 + role][:, :, :], ACT.Copy).then_inc(split_hi, 1)
                    sp_(i, j, 2)
                    act.wait_ge(used, 3 * e + (s0 + 1))
                    for c in range(2):
                        act.activation(hid_s[:, c, 0:width], bank[c][:, 0:width], ACT.Silu).then_inc(e_s, 1)
                    for c in range(2):
                        act.wait_ge(e_t, l * (2 * E) + 2 * e + (c + 1))
                        act.activation(hid_hi[:, c, 0:width], hid_t[:, c, 0:width], ACT.Copy).then_inc(e_hi, 1)
                    if ahead:
                        i2, j2 = (i, 1) if j == 0 else (i + 1, 0)
                        sp_(i2, j2, 0)
                        sp_(i2, j2, 1)
                for role in range(2):
                    act.wait_ge(loaded[role], 16 * (r0 // RAW + 1))
                    act.wait_ge(used, s0 + role - HL + 1)
                    act.activation(w_hi[role][:, :, :], raw[role][:, :, :], ACT.Copy).then_inc(split_hi, 1)
                with act.Fori(0, E // 2 - 1) as i:
                    for j in range(2):
                        expert(2 * i + j, i, j, True)
                for j in range(2):
                    expert(E - 2 + j, E // 2 - 1, j, j == 0)
            norm(2 * DEPTH, S, None, DEPTH)
            for t in range(2):
                act.wait_ge(f_y, KC)
                act.activation(y_tok[:, t, 512:1024], bank[1 + 2 * t][:, :], ACT.Copy).then_inc(f_ev, 1)

        @block.tensor
        def _(pe):
            def product(dst, w_hi_, w_lo_, x_hi_, x_lo_, first, last):
                pe.matmul(dst, w_hi_, x_hi_, start=first, stop=False)
                pe.matmul(dst, w_hi_, x_lo_, start=False, stop=False)
                return pe.matmul(dst, w_lo_, x_hi_, start=False, stop=last)

            def wait_split(l, r):
                pe.wait_ge(split_lo, split_index(l, r) + 1)

            def column_sums(dst, src, k, n, last):
                for t in range(n):
                    ins = pe.matmul(dst[:, t:t + 1], src[:, t * P:(t + 1) * P], ones[:, 0:1], start=(k == 0 and t == 0),
                                    stop=last, skip_group_check=True)
                return ins

            def rows_of(dst, column, n):
                for t in range(n):
                    ap = column[:, t:t + 1].to_broadcast([P, P])
                    ins = pe.matmul(dst[:, t * P:(t + 1) * P], ap, ident, start=True, stop=True)
                return ins

            def norm(i, width):
                n = width // P
                for k in range(KC):
                    pe.wait_ge(n_sqa if k % 2 == 0 else n_sqd, i * (KC // 2) + k // 2 + 1)
                    column_sums(bank[6], nsq[:, k % 4, :], k, n, k == KC - 1).then_inc(n_sum, 1)
                pe.wait_ge(n_rstd, i + 1)
                rows_of(bank[7], rstd, n).then_inc(n_bc, 1)

            pe.wait_ge(s_const, 16)
            pe.wait_ge(s_vecin, 32)
            pe.transpose(bank[0][:, 0:112], raw_vec[0][0:112, :], ident[0:112, 0:112])
            pe.transpose(bank[0][:, 112:N_VEC], raw_vec[1][0:N_VEC - 112, :], ident[0:N_VEC - 112, 0:N_VEC - 112]).then_inc(s_vt, 1)
            pe.wait_ge(s_cact, 1)

            for l in range(DEPTH):
                ns = streams(l)
                nt, width = 2 * ns, ns * S

                def turn(j):
                    pe.wait_ge(ada_ea if j % 2 else ada_ed, l * (N_ADA // 2) + j // 2 + 1)
                    for i in range(2):
                        c = 2 * j + i
                        ins = pe.transpose(bank[7][:, 2 * c:2 * c + 2], mod_row[:, j % 2, i * P:(i + 1) * P], ident[0:2, 0:2])
                    ins.then_inc(ada_tr, 1)

                for j in range(N_ADA):
                    n = raw_index(l, j)
                    pe.wait_ge(loaded[n % RAW], 16 * (n // RAW + 1))
                    if j >= 4:
                        pe.wait_ge(ada_ea if j % 2 else ada_ed, l * (N_ADA // 2) + (j - 4) // 2 + 1)
                    for k in range(KC):
                        ins = pe.matmul(bank[j % 4][0:2, 0:BW], c_act[:, k:k + 9:8], raw[n % RAW][:, k, :],
                                        start=(k == 0), stop=(k == KC - 1))
                    ins.then_inc(ada_mm, 1)
                    if j:
                        turn(j - 1)
                    if l == 0 and 4 <= j < 12:
                        k = j - 4
                        pe.wait_ge(s_xin, 64)
                        if k >= 3:
                            pe.wait_ge(s_xev if (k - 3) % 2 else s_xevd, (k - 3) // 2 + 1)
                        for t in range(4):
                            ins = pe.transpose(bank[4 + k % 3][:, t * P:(t + 1) * P], x_tok[t][:, k * P:(k + 1) * P], ident)
                        ins.then_inc(s_xt, 1)
                turn(N_ADA - 1)

                norm(2 * l, T)

                def by_feature(b, c, dst, c0, m, width, l=l):
                    s = split_index(l, N_ADA + b) % HL
                    for k in range(KC):
                        if b == 0 and c == 0:
                            pe.wait_ge(n_lo, (2 * l) * (KC) + k + 1)
                        ins = product(dst[0:m, 0:width], w_hi[s][:, k, c0:c0 + m], w_lo[s][:, k, c0:c0 + m],
                                      h_hi[:, k, 0:width], h_lo[:, k, 0:width], k == 0, k == KC - 1)
                    return ins

                for b in range(N_WIN):
                    wait_split(l, N_ADA + b)
                    if b == 4:
                        pe.wait_ge(proj_ed, l * 5 + 1)
                    if b == 5:
                        pe.wait_ge(proj_ea, l * 4 + 1)
                    if b == 6:
                        pe.wait_ge(proj_ed, l * 5 + 2)
                    if b == 7:
                        pe.wait_ge(proj_ed, l * 5 + 3)
                        pe.wait_ge(proj_ea, l * 4 + 2)
                    b0 = 2 * (b % 4)
                    if b in (3, 4, 5):
                        s = split_index(l, N_ADA + b) % HL
                        for t in range(4 if b == 3 else nt):
                            dst = bank[b0 + t // 2][:, (t % 2) * BW:(t % 2 + 1) * BW]
                            for k in range(KC):
                                pe.matmul(dst, h_hi[:, k, t * P:(t + 1) * P], w_hi[s][:, k, :], start=(k == 0), stop=False)
                                pe.matmul(dst, h_hi[:, k, t * P:(t + 1) * P], w_lo[s][:, k, :], start=False, stop=False)
                                ins = pe.matmul(dst, h_lo[:, k, t * P:(t + 1) * P], w_hi[s][:, k, :], start=False, stop=(k == KC - 1))
                    elif b == 7:
                        by_feature(b, 0, bank[6], 0, P, T)
                        by_feature(b, 1, bank[7], 64, QK, T)
                        ins = by_feature(b, 1, bank[0], 96, QK, S)
                    else:
                        for c in range(2):
                            ins = by_feature(b, c, bank[b0 + c], c * P, P, T if b == 2 else width)
                    ins.then_inc(used, 1)

                pe.wait_ge(s_small, l * (16 * SMALL) + 16 * SMALL)
                pe.wait_ge(proj_ea, l * 4 + 4)
                for g in range(4):
                    ins = pe.transpose(bank[6][:, g * P:(g + 1) * P], sgu_w[:, g, :], ident)
                ins.then_inc(s_wt, 1)
                pe.wait_ge(s_lsq, l * 2 + 2)
                pe.wait_ge(proj_ed, l * 5 + 5)
                for c in range(2):
                    column_sums(bank[7][:, 0:4], low_sq[:, c, :], c, nt, c == 1)
                for t in range(4):
                    ins = pe.matmul(bank[7][:, 4 + t:5 + t], low_sq[:, 2, t * P:(t + 1) * P], ones[:, 0:1], start=False,
                                    stop=True, skip_group_check=True)
                ins.then_inc(s_lsum, 1)
                pe.wait_ge(s_lrstd, l + 1)
                rows_of(bank[0], col[:, 48:52], nt)
                rows_of(bank[1], col[:, 52:56], 4).then_inc(s_lbc, 1)
                pe.wait_ge(s_wg, l + 1)
                pe.wait_ge(s_low, l * 3 + 2)
                for h in range(HEADS):
                    for c in range(2):
                        ins = pe.matmul(bank[2 + h][0:QK, 0:width], w_uq[:, c, h * QK:(h + 1) * QK], q_low[:, c, 0:width],
                                        start=(c == 0), stop=(c == 1))
                    ins.then_inc(s_up, 1)
                pe.wait_ge(s_wte, l + 1)
                pe.wait_ge(s_lroot, l + 1)
                for h in range(HEADS):
                    for c in range(2):
                        ins = pe.matmul(bank[6 + h // 2][0:QK, (h % 2) * S:(h % 2 + 1) * S], w_uqs[:, c, h, :],
                                        q_low[:, c, 0:S], start=(c == 0), stop=(c == 1))
                    if h % 2:
                        ins.then_inc(s_up, 1)
                for h in range(HEADS):
                    if h == 0:
                        pe.wait_ge(s_low, l * 3 + 3)
                    if h == 2:
                        pe.wait_ge(s_qe, l * 4 + 2)
                    pe.matmul(bank[h][0:NOPE, :], w_ukv[:, h * P:h * P + NOPE], kv_low[:, :], start=True, stop=True).then_inc(s_up, 1)
                pe.wait_ge(s_qe, l * 4 + 4)
                for t in range(4):
                    ins = pe.matmul(bank[4 + t // 2][:, (t % 2) * S:(t % 2 + 1) * S], kv_low[:, t * P:(t + 1) * P],
                                    w_ukv[:, :].rearrange("p (h m) -> p h m", m=P)[:, :, NOPE:P], start=True, stop=True)
                ins.then_inc(s_up, 1)
                pe.wait_ge(s_gn, l + 1)
                pe.wait_ge(s_rot, l * 2 + 1)
                for g in range(4):
                    ins = pe.matmul(bank[6 + g // 2][:, (g % 2) * S:(g % 2) * S + nt * 64], sgu_wt[:, g, :],
                                    sgu_v[:, 0:nt, g * 64:(g + 1) * 64], start=True, stop=True)
                ins.then_inc(s_mix, 1)

                jobs = attention_jobs(l)
                n_jobs = len(jobs)
                pe.wait_ge(s_ke, l * 4 + 4)
                pe.wait_ge(s_ve, l + 1)
                pe.wait_ge(s_bias, l + 1)
                pe.wait_ge(s_rot, l * 2 + 2)
                pe.wait_ge(s_go, l + 1)
                for i in range(n_jobs + 2):
                    if i < n_jobs:
                        kind, h, t = jobs[i]
                        keys = slice(0, T) if t < 2 else slice(S, T)
                        nk = keys.stop - keys.start
                        if i >= 3:
                            pe.wait_ge(t_ex, l * JOBS + i - 2)
                        if kind == "na":
                            r = slice(64 * (h % 2), 64 * (h % 2) + 64)
                            ins = pe.matmul(bank[i % 3][:, 0:nk], q_na[r, h // 2, t * P:(t + 1) * P], k_na[r, h // 2, keys],
                                            start=True, stop=True)
                            if t < 2:
                                s = 2 - 2 * t
                                ins = pe.matmul(bank[i % 3][:, 0:S], const[:, C_FLIP:C_FLIP + P],
                                                na_bias[:, h, s:s + 4, :].rearrange("p r c -> p (r c)"),
                                                start=False, stop=True, skip_group_check=True)
                        else:
                            ins = pe.matmul(bank[i % 3][:, 0:nk], q_mla[0:QK, h, t * P:(t + 1) * P], k_mla[0:QK, h, keys],
                                            start=True, stop=True)
                        ins.then_inc(t_sc, 1)
                    if 1 <= i <= n_jobs:
                        q = i - 1
                        pe.wait_ge(t_ex, l * JOBS + q + 1)
                        if q >= 2:
                            pe.wait_ge(t_pa if q % 2 == 0 else t_pd, l * (JOBS // 2) + (q - 2) // 2 + 1)
                        for kt in range(4 if jobs[q][2] < 2 else 2):
                            ins = pe.transpose(bank[3 + q % 2][:, kt * P:(kt + 1) * P], prob[q % 3][:, kt * P:(kt + 1) * P], ident)
                        ins.then_inc(t_tr, 1)
                    if i >= 2:
                        q = i - 2
                        kind, h, t = jobs[q]
                        pe.wait_ge(t_pa if q % 2 == 0 else t_pd, l * (JOBS // 2) + q // 2 + 1)
                        if q >= 2:
                            pe.wait_ge(t_o, l * JOBS + q - 1)
                        v = v_na if kind == "na" else v_mla
                        tiles = range(4) if t < 2 else range(2, 4)
                        for n, kt in enumerate(tiles):
                            ins = pe.matmul(bank[5 + q % 2][:, 0:64], prob_t[q % 3][:, n, :], v[:, kt, h * 64:(h + 1) * 64],
                                            start=(n == 0), stop=(n == len(tiles) - 1))
                        ins.then_inc(t_pv, 1)
                pe.wait_ge(s_pool, l + 1)
                pe.wait_ge(t_o, l * JOBS + n_jobs)
                for c in range(KC):
                    if c < 2:
                        ins = pe.matmul(bank[c][:, 0:width], pool_bd[:, c, :], pool_d[:, c, 0:width], start=True, stop=True)
                    else:
                        for t in range(nt):
                            ins = pe.transpose(bank[c][:, t * P:(t + 1) * P], o_tok[:, t, (c - 2) * P:(c - 1) * P], ident)
                    ins.then_inc(m_ps, 1)
                pe.wait_ge(m_lo, l * KC + KC)
                for b in range(N_WOUT):
                    r = N_ADA + N_WIN + b
                    wait_split(l, r)
                    s = split_index(l, r) % HL
                    for c in range(2):
                        for k in range(KC):
                            ins = product(bank[2 * b + c][:, 0:width], w_hi[s][:, k, c * P:(c + 1) * P], w_lo[s][:, k, c * P:(c + 1) * P],
                                          h_hi[:, k, 0:width], h_lo[:, k, 0:width], k == 0, k == KC - 1)
                    ins.then_inc(used, 1)

                norm(2 * l + 1, width)
                pe.wait_ge(s_rw, 2)
                pe.wait_ge(n_lo, (2 * l + 1) * (KC) + KC)
                for t in range(nt):
                    for k in range(KC):
                        ts = slice(t * P, (t + 1) * P)
                        dst = bank[5][:, t * E:(t + 1) * E]
                        pe.matmul(dst, h_hi[:, k, ts], rw_hi[:, k, :], start=(k == 0), stop=False)
                        pe.matmul(dst, h_hi[:, k, ts], rw_lo[:, k, :], start=False, stop=False)
                        ins = pe.matmul(dst, h_lo[:, k, ts], rw_hi[:, k, :], start=False, stop=(k == KC - 1))
                ins.then_inc(r_lg, 1)

                s0 = split_index(l, N_ADA + N_WIN + N_WOUT)
                pe.wait_ge(r_gate, l + 1)

                def expert(e, first):
                    for role in range(2):
                        pe.wait_ge(split_lo, 3 * e + (s0 + role + 1))
                        if not first:
                            pe.wait_ge(e_t, l * (2 * E) + 2 * e)
                        for c in range(2):
                            for k in range(KC):
                                ins = product(bank[2 * role + c][:, 0:width], w_hi[role][:, k, c * P:(c + 1) * P],
                                              w_lo[role][:, k, c * P:(c + 1) * P], h_hi[:, k, 0:width], h_lo[:, k, 0:width],
                                              k == 0, k == KC - 1)
                        ins.then_inc(used, 1)
                    pe.wait_ge(e_gc, l * E + e + 1)
                    for t in range(nt):
                        ins = pe.matmul(bank[7][:, t * P:(t + 1) * P], gcol[:, t, :], ident, start=True, stop=True)
                    ins.then_inc(e_gb, 1)
                    pe.wait_ge(split_lo, 3 * e + (s0 + 3))
                    pe.wait_ge(e_lo, l * (2 * E) + 2 * e + 2)
                    dh = w_hi[2][:, :, :].rearrange("p (f k) n -> p f (k n)", f=2)
                    dl = w_lo[2][:, :, :].rearrange("p (f k) n -> p f (k n)", f=2)
                    for dc in range(KC):
                        if dc >= 3:
                            pe.wait_ge(e_x, l * (KC * E) + KC * e + (dc - 2))
                        elif not first:
                            pe.wait_ge(e_x, l * (KC * E) + KC * e)
                        for f in range(2):
                            ins = product(bank[4 + dc % 3][:, 0:width], dh[:, f, dc * P:(dc + 1) * P], dl[:, f, dc * P:(dc + 1) * P],
                                          hid_hi[:, f, 0:width], hid_lo[:, f, 0:width], f == 0, f == 1)
                        ins.then_inc(e_d if dc < KC - 1 else used, 1)

                expert(0, True)
                with pe.Fori(1, E) as e:
                    expert(e, False)

            norm(2 * DEPTH, S)
            for k in range(KC):
                pe.wait_ge(n_h[2 * DEPTH], k + 1)
                for t in range(2):
                    ins = pe.transpose(bank[2 * t + k // 4][:, (k % 4) * P:(k % 4 + 1) * P], nh[:, k % 2, t * P:(t + 1) * P], ident)
                ins.then_inc(f_y, 1)

        @block.vector
        def _(dve):
            made = [0]

            def then(ins):
                made[0] += 1
                ins.then_inc(chain_d, 1)
                dve.wait_ge(chain_d, made[0])

            def split(l, r):
                s, n = split_index(l, r), raw_index(l, r)
                dve.wait_ge(split_hi, s + 1)
                w = block_cols(r)
                dve.tensor_tensor(w_lo[s % HL][:, :, 0:w], raw[n % RAW][:, :, 0:w], w_hi[s % HL][:, :, 0:w].bitcast(F32),
                                  ALU.subtract).then_inc(split_lo, 1)

            def norm(i, width, last):
                n = width // P
                for k in range(1, KC, 2):
                    if k >= 4:
                        dve.wait_ge(n_sum, i * KC + k - 3)
                    dve.tensor_tensor(nsq[:, k % 4, 0:width], x_t[:, k, 0:width], x_t[:, k, 0:width], ALU.mult).then_inc(n_sqd, 1)
                dve.wait_ge(n_root, i + 1)
                dve.reciprocal(rstd[:, 0:n], col[:, 0:n]).then_inc(n_rstd, 1)
                dve.wait_ge(n_bc, i + 1)

                def low(k):
                    dve.wait_ge(n_hi, i * KC + k + 1)
                    dve.tensor_tensor(h_lo[:, k, 0:width], nh[:, k % 2, 0:width], h_hi[:, k, 0:width].bitcast(F32),
                                      ALU.subtract).then_inc(n_lo, 1)
                for k in range(KC):
                    if k >= 2:
                        dve.wait_ge(n_h[i], (k - 1) * (1 if last else width // S))
                    dve.tensor_tensor(nx[:, k % 2, 0:width], x_t[:, k, 0:width], bank[7][:, 0:width], ALU.mult).then_inc(n_x, 1)
                    if k and not last:
                        low(k - 1)
                if not last:
                    low(KC - 1)

            dve.wait_ge(s_vt, 1)
            dve.tensor_copy(vec[:, :], bank[0][:, 0:N_VEC]).then_inc(s_vec, 1)
            dve.wait_ge(s_rw, 1)
            dve.tensor_tensor(rw_lo[:, :, :], rw_in[:, :, :], rw_hi[:, :, :].bitcast(F32), ALU.subtract).then_inc(s_rw, 1)
            for l in range(DEPTH):
                ns = streams(l)
                nt, width = 2 * ns, ns * S
                for j in range(0, N_ADA, 2):
                    dve.wait_ge(ada_mm, l * N_ADA + j + 1)
                    if j >= 2 or l:
                        dve.wait_ge(ada_tr, l * N_ADA + j - 1)
                    dve.tensor_copy(mod_row[:, 0, :], bank[j % 4][0:2, 0:BW]).then_inc(ada_ed, 1)
                    if l == 0 and 4 <= j < 12:
                        k = j - 4
                        dve.wait_ge(s_xt, k + 1)
                        dve.tensor_copy(x_t[:, k, :], bank[4 + k % 3][:, :]).then_inc(s_xevd, 1)
                dve.wait_ge(ada_tr, (l + 1) * N_ADA)
                for s in range(2):
                    ins = dve.tensor_tensor(mod[:, s, :], bank[7][:, s:96:2], vec[:, V_ADAB + 48 * l:V_ADAB + 48 * (l + 1)], ALU.add)
                then(ins)
                for which, v in enumerate((V_N1, V_N2)):
                    for s in range(2):
                        m = 24 * which + KC
                        ins = dve.scalar_tensor_tensor(amp[:, which, s, :], mod[:, s, m:m + KC], 1.0, vec[:, v + KC * l:v + KC * (l + 1)],
                                                       ALU.add, ALU.mult)
                if l == 0:
                    dve.wait_ge(s_xev, 4)
                ins.then_inc(s_amp, 1)
                for r in range(N_ADA, N_ADA + HL):
                    split(l, r)
                norm(2 * l, T, False)
                for b in range(N_WIN):
                    if b in (0, 2, 3, 6, 7):
                        dve.wait_ge(used, done(l, N_ADA + b))
                    b0 = 2 * (b % 4)
                    if b == 0:
                        for c in range(2):
                            ins = dve.tensor_copy(a_pad[:, c, 0:ns, PAD:PAD + S], bank[c][:, 0:width].rearrange("p (s t) -> p s t", s=ns))
                        ins.then_inc(proj_ed, 1)
                    if b in (2, 6):
                        dst, w = (k_na, T) if b == 2 else (q_low, width)
                        for c in range(2):
                            ins = dve.tensor_copy(dst[:, c, 0:w], bank[b0 + c][:, 0:w])
                        ins.then_inc(proj_ed, 1)
                    if b == 3:
                        for c in range(2):
                            ins = dve.tensor_copy(v_na[:, 2 * c:2 * c + 2, :].rearrange("p t n -> p (t n)"), bank[6 + c][:, :])
                        ins.then_inc(proj_ed, 1)
                    if b == 7:
                        rr = slice(NOPE, QK)
                        dve.tensor_copy(k_rope[rr, :], bank[7][rr, :])
                        then(dve.tensor_tensor(rope_t[rr, 0, :], bank[0][rr, 0:S], const[rr, C_SIN:C_SIN + S], ALU.mult))
                        ins = dve.tensor_tensor(k_rope[rr, 0:S], k_rope[rr, 0:S], const[rr, C_COS:C_COS + S], ALU.mult)
                        ins.then_inc(proj_ed, 1)
                        dve.wait_ge(proj_ed, l * 5 + 5)
                        then(dve.tensor_tensor(k_rope[rr, 0:S], k_rope[rr, 0:S], rope_t[rr, 0, :], ALU.add))
                        dve.tensor_copy(k_mla[rr, :, :], k_rope[rr, :][:, None, :].to_broadcast([ROPE, HEADS, T]))
                    if b + HL < N_WIN:
                        split(l, N_ADA + b + HL)
                n = 4 * nt
                dve.wait_ge(proj_ea, l * 4 + 3)
                vv = sgu_v[:, 0:nt, :].rearrange("p t (g c) -> p (t g) c", c=64)
                sq = sgu_sq[:, 0:nt, :].rearrange("p t (g c) -> p (t g) c", c=64)
                then(dve.tensor_tensor(sq, vv, vv, ALU.mult))
                dve.tensor_reduce(col[:, 16:16 + n], sq, AX.X, ALU.add).then_inc(s_gv, 1)
                dve.wait_ge(s_lroot, l + 1)
                dve.reciprocal(col[:, 48:48 + nt], col[:, 8:8 + nt])
                dve.reciprocal(col[:, 52:56], col[:, 12:16]).then_inc(s_lrstd, 1)
                dve.wait_ge(s_groot, l + 1)
                then(dve.reciprocal(col[:, 16:16 + n], col[:, 32:32 + n]))
                dve.wait_ge(s_lbc, l + 1)
                for c in range(2):
                    dve.tensor_tensor(q_low[:, c, 0:width], q_low[:, c, 0:width], bank[0][:, 0:width], ALU.mult).then_inc(s_low, 1)
                dve.wait_ge(proj_ea, l * 4 + 4)
                dve.tensor_tensor(kv_low[:, :], kv_low[:, :], bank[1][:, :], ALU.mult).then_inc(s_low, 1)
                then(dve.tensor_tensor(vv, vv, col[:, 16:16 + n][:, :, None].to_broadcast([P, n, 64]), ALU.mult))
                dve.tensor_tensor(sgu_v[:, 0:nt, :], sgu_v[:, 0:nt, :], sgu_g[:, :][:, None, :].to_broadcast([P, nt, S]),
                                  ALU.mult).then_inc(s_gn, 1)
                rr = slice(NOPE, QK)
                dve.wait_ge(s_up, l * 11 + 6)
                for h2 in range(2):
                    ins = dve.scalar_tensor_tensor(rope_t[rr, 2 * h2:2 * h2 + 2, :], bank[6 + h2][rr, :].rearrange("p (h t) -> p h t", h=2),
                                                   MLA_SCALE, const[rr, C_SIN:C_SIN + S][:, None, :].to_broadcast([ROPE, 2, S]),
                                                   ALU.mult, ALU.mult)
                ins.then_inc(s_rot, 1)
                dve.wait_ge(s_qe, l * 4 + 4)
                dve.wait_ge(s_rot, l * 2 + 1)
                then(dve.tensor_tensor(q_mla[rr, :, 0:S], q_mla[rr, :, 0:S], const[rr, C_COS:C_COS + S][:, None, :].to_broadcast([ROPE, HEADS, S]), ALU.mult))
                dve.tensor_tensor(q_mla[rr, :, 0:S], q_mla[rr, :, 0:S], rope_t[rr, :, :], ALU.add).then_inc(s_rot, 1)
                dve.wait_ge(s_mix, l + 1)
                for g in range(4):
                    v0 = V_SB + 4 * l + g
                    ins = dve.scalar_tensor_tensor(o_tok[:, 0:nt, S + g * 64:S + (g + 1) * 64],
                                                   bank[6 + g // 2][:, (g % 2) * S:(g % 2) * S + nt * 64].rearrange("p (t c) -> p t c", c=64),
                                                   vec[:, v0:v0 + 1], sgu_u[:, 0:nt, g * 64:(g + 1) * 64], ALU.add, ALU.mult)
                ins.then_inc(s_go, 1)
                jobs = attention_jobs(l)
                for i in range(len(jobs) + 2):
                    if i < len(jobs):
                        nk = T if jobs[i][2] < 2 else S
                        dve.wait_ge(t_sc, l * JOBS + i + 1)
                        dve.tensor_reduce(stat[:, i % 4, 0:1], bank[i % 3][:, 0:nk], AX.X, ALU.max, negate=True).then_inc(t_mx, 1)
                    if 1 <= i <= len(jobs) and i % 2 == 0:
                        q = i - 1
                        nkt = 4 if jobs[q][2] < 2 else 2
                        dve.wait_ge(t_tr, l * JOBS + q + 1)
                        if q >= 3:
                            dve.wait_ge(t_pv, l * JOBS + q - 2)
                        dve.tensor_copy(prob_t[q % 3][:, 0:nkt, :].rearrange("p k n -> p (k n)"), bank[3 + q % 2][:, 0:nkt * P]).then_inc(t_pd, 1)
                    if i >= 2:
                        q = i - 2
                        kind, h, t = jobs[q]
                        dve.wait_ge(t_pv, l * JOBS + q + 1)
                        then(dve.reciprocal(stat[:, q % 4, 2:3], stat[:, q % 4, 1:2]))
                        c0 = (0 if kind == "na" else 2 * S) + h * 64
                        dve.tensor_scalar(o_tok[:, t, c0:c0 + 64], bank[5 + q % 2][:, 0:64], stat[:, q % 4, 2:3], None, ALU.mult).then_inc(t_o, 1)
                for c in range(KC):
                    dve.wait_ge(m_hi, l * KC + c + 1)
                    hi = h_hi[:, c, 0:width].bitcast(F32)
                    if c < 2:
                        v0 = V_PS + 2 * l + c
                        dve.scalar_tensor_tensor(h_lo[:, c, 0:width], bank[c][:, 0:width], vec[:, v0:v0 + 1], hi, ALU.mult, ALU.subtract).then_inc(m_lo, 1)
                    else:
                        dve.tensor_tensor(h_lo[:, c, 0:width], bank[c][:, 0:width], hi, ALU.subtract).then_inc(m_lo, 1)

                def add_gated(dc, src, gate, signal):
                    for s in range(ns):
                        sl = slice(s * S, (s + 1) * S)
                        ins = dve.scalar_tensor_tensor(x_t[:, dc, sl], src[:, sl], mod[:, s, gate * KC + dc:gate * KC + dc + 1], x_t[:, dc, sl],
                                                       ALU.mult, ALU.add)
                    ins.then_inc(signal, 1)

                for b in range(N_WOUT):
                    split(l, N_ADA + N_WIN + b)
                    if b >= 1:
                        dve.wait_ge(used, done(l, N_ADA + N_WIN + b - 1))
                        for c in range(2):
                            add_gated(2 * (b - 1) + c, bank[2 * (b - 1) + c], 2, o_ev)
                dve.wait_ge(used, done(l, N_ADA + N_WIN + 3))
                for c in range(2):
                    add_gated(6 + c, bank[6 + c], 2, o_ev)
                dve.wait_ge(o_ev, l * KC + KC)
                norm(2 * l + 1, width, False)

                dve.wait_ge(r_sg, l + 1)
                sc = score[:, 0:nt, :]
                bi, rk, cm = biased[:, 0:nt, :], rank[:, 0:nt, :], cmp[:, 0:nt, :]
                then(dve.tensor_tensor(bi, sc, rb_row[:, :][:, None, :].to_broadcast([P, nt, E]), ALU.add))

                def rank_of_four(values, ranks, scratch):
                    then(dve.tensor_copy(ranks, const[:, C_RANK:C_RANK + ranks.shape[1] * 4].rearrange("p (n f) -> p n f", f=4)))
                    for d in range(1, 4):
                        then(dve.tensor_tensor(scratch[:, :, 0:4 - d], values[:, :, 0:4 - d], values[:, :, d:4], ALU.is_ge))
                        then(dve.tensor_tensor(ranks[:, :, d:4], ranks[:, :, d:4], scratch[:, :, 0:4 - d], ALU.add))
                        then(dve.tensor_tensor(ranks[:, :, 0:4 - d], ranks[:, :, 0:4 - d], scratch[:, :, 0:4 - d], ALU.subtract))

                four = lambda ap: ap.rearrange("p t (g f) -> p (t g) f", f=4)
                rank_of_four(four(bi), four(rk), four(cm))
                then(dve.tensor_scalar(rk, rk, 1.5, None, ALU.is_lt))
                then(dve.tensor_tensor(cm, rk, bi, ALU.mult))
                g2 = grp[:, 0:nt, :]
                then(dve.tensor_reduce(g2.rearrange("p t g -> p (t g)"), four(cm), AX.X, ALU.add))
                gr = grank[:, 0:nt, :]
                rank_of_four(g2, gr, cmp[:, 0:nt, 0:4])
                then(dve.tensor_scalar(gr, gr, 0.5, None, ALU.is_lt))
                then(dve.tensor_tensor(four(rk), four(rk), gr.rearrange("p t g -> p (t g)")[:, :, None].to_broadcast([P, 4 * nt, 4]), ALU.mult))
                then(dve.tensor_tensor(rk, rk, sc, ALU.mult))
                then(dve.tensor_reduce(grp[:, 0:nt, 0], rk, AX.X, ALU.add))
                then(dve.reciprocal(grp[:, 0:nt, 1], grp[:, 0:nt, 0]))
                dve.tensor_tensor(gates[:, 0:nt, :], rk, grp[:, 0:nt, 1:2].to_broadcast([P, nt, E]), ALU.mult).then_inc(r_gate, 1)
                dve.wait_ge(r_gate, l + 1)

                s0 = split_index(l, N_ADA + N_WIN + N_WOUT)

                def split_e(e, slot, role):
                    dve.wait_ge(split_hi, 3 * e + (s0 + role + 1))
                    dve.tensor_tensor(w_lo[role][:, :, :], raw[slot][:, :, :], w_hi[role][:, :, :].bitcast(F32), ALU.subtract).then_inc(split_lo, 1)

                def expert(e, j, ahead):
                    dve.tensor_copy(gcol[:, 0:nt, :], gates[:, 0:nt, bass.ds(e, 1)].to_broadcast([P, nt, P])).then_inc(e_gc, 1)
                    split_e(e, 3 * j + 2, 2)
                    dve.wait_ge(used, 3 * e + (s0 + 2))
                    for c in range(2):
                        dve.wait_ge(e_s, l * (2 * E) + 2 * e + (c + 1))
                        ins = dve.tensor_tensor(hid_t[:, c, 0:width], bank[2 + c][:, 0:width], hid_s[:, c, 0:width], ALU.mult)
                        ins.then_inc(e_m, 1)
                    dve.wait_ge(e_gb, l * E + e + 1)
                    for c in range(2):
                        dve.wait_ge(e_m, l * (2 * E) + 2 * e + (c + 1))
                        dve.tensor_tensor(hid_t[:, c, 0:width], hid_t[:, c, 0:width], bank[7][:, 0:width], ALU.mult).then_inc(e_t, 1)
                    for c in range(2):
                        dve.wait_ge(e_hi, l * (2 * E) + 2 * e + (c + 1))
                        dve.tensor_tensor(hid_lo[:, c, 0:width], hid_t[:, c, 0:width], hid_hi[:, c, 0:width].bitcast(F32), ALU.subtract).then_inc(e_lo, 1)
                    if ahead:
                        for role in range(2):
                            split_e(e + 1, 3 * (1 - j) + role, role)
                    for dc in range(KC):
                        if dc < KC - 1:
                            dve.wait_ge(e_d, l * (KC - 1) * E + (KC - 1) * e + (dc + 1))
                        else:
                            dve.wait_ge(used, 3 * e + (s0 + 3))
                        add_gated(dc, bank[4 + dc % 3], 5, e_x)

                for role in range(2):
                    split_e(0, role, role)
                for j in range(2):
                    expert(j, j, True)
                with dve.Fori(1, E // 2 - 1) as i:
                    for j in range(2):
                        expert(2 * i + j, j, True)
                for j in range(2):
                    expert(E - 2 + j, j, j == 0)
                dve.wait_ge(e_x, l * (KC * E) + KC * E)
            norm(2 * DEPTH, S, True)
            for t in range(2):
                dve.wait_ge(f_y, KC)
                dve.tensor_copy(y_tok[:, t, 0:512], bank[2 * t][:, :]).then_inc(f_ev, 1)


def kernel(**inputs):
    import numpy as _np
    import concourse.bacc as _bacc
    from concourse import mybir as _mybir
    from concourse.bass_utils import run_bass_kernel_spmd as _run

    g = {k: _np.ascontiguousarray(v) for k, v in inputs.items()}
    arrays = {n: g[n] for n in ("ada_w", "w_in", "w_out", "pool_w", "mla_w_uq", "mla_w_ukv", "sgu_norm_g", "sgu_w", "router_w",
                                "router_b", "moe_w_gate", "moe_w_up", "moe_w_down")}
    arrays["x"], arrays["ctx"] = g["x"][0], g["ctx"][0]
    arrays["vec0"] = _np.concatenate([g[n].reshape(-1, P) for n in ("ada_b", "c", "c_ctx")])
    arrays["vec1"] = _np.concatenate([g[n].reshape(-1, P) for n in (
        "norm1_g", "norm2_g", "final_g", "pool_s", "mla_q_norm_g", "mla_kv_norm_g", "sgu_b")])
    rpb = _np.zeros((DEPTH, 2, HEADS, 6, P), _np.float32)
    for half in range(2):
        rpb[:, half, :, :, 48:79] = g["na_rpb"][:, :, 5 - half:11 - half]
    arrays["na_rpb"] = rpb
    arrays["const"] = constants()
    nc = _bacc.Bacc("TRN2", target_bir_lowering=False, num_devices=1)
    aps = {}
    for n, v in arrays.items():
        aps[n] = nc.dram_tensor(f"in_{n}", v.shape, _mybir.dt.from_np(v.dtype), kind="ExternalInput").ap()
    out = nc.dram_tensor("out_0", (S, D), F32, kind="ExternalOutput").ap()
    build(nc, aps, out)
    r = _run(nc, [{f"in_{n}": v for n, v in arrays.items()}], core_ids=[0])
    return r.results[0]["out_0"].reshape(1, S, D)
```

```python
from contextlib import ExitStack

import numpy as np

import concourse.bass as bass
from concourse import mybir

F32 = mybir.dt.float32
F32R = mybir.dt.float32r
ALU = mybir.AluOpType
ACT = mybir.ActivationFunctionType
AX = mybir.AxisListType

P = 128
D = 1024
KC = D // P
S = 256
T = 2 * S
DEPTH = 2
GRID = 64
ROWS = S // GRID
IN_W = 1952
HEADS = 4
E = 16
FE = 256
SLOTS = P
WIN_COLS = 16
NOPE, ROPE = 64, 32
QK = NOPE + ROPE
MLA_SCALE = float(QK) ** -0.5
NA_SCALE = 64.0 ** -0.5
EPS = 1e-6
NEG = -1e30
PAD = 8
PW = S + 2 * PAD

BW = 256
N_ADA, N_WIN, N_WOUT = 24, 8, 4
N_MOE = 3 * E
PER_LAYER = N_ADA + N_WIN + N_WOUT + N_MOE
SPLIT_PER_LAYER = PER_LAYER - N_ADA
ROUNDS = [T // SLOTS if l < DEPTH - 1 else S // SLOTS for l in range(DEPTH)]
RAW = 6
HL = 3

C_ID, C_FLIP, C_ONE, C_NEGM, C_INV, C_COS, C_SIN, C_RANK, C_EPS = np.cumsum(
    [0, P, P, P, GRID, 2 * S, S, S, 64]).tolist()
N_CONST = C_EPS + 2
V_ADAB, V_C = 0, DEPTH * 48
V_N1 = V_C + 16
V_N2 = V_N1 + DEPTH * KC
V_FIN = V_N2 + DEPTH * KC
V_PS = V_FIN + KC
V_QG = V_PS + 2 * DEPTH
V_KVG = V_QG + 2 * DEPTH
V_SB = V_KVG + DEPTH
N_VEC = V_SB + 4 * DEPTH


C2_TRI, C2_EBASE = 0, P
C2_IOTA = C2_EBASE + E
N_CONST2 = C2_IOTA + T


def router_constants():
    c = np.zeros((P, N_CONST2), np.float32)
    c[:, C2_TRI:C2_TRI + P] = np.triu(np.ones((P, P)), 1)
    c[:, C2_EBASE:C2_EBASE + E] = SLOTS * np.arange(E) + 1
    c[:, C2_IOTA:C2_IOTA + T] = np.arange(T)
    return c


def constants():
    c = np.zeros((P, N_CONST), np.float32)
    c[:, C_ID:C_ID + P] = np.eye(P)
    for p in range(P):
        c[p, C_FLIP + (p // GRID) * GRID + GRID - 1 - p % GRID] = 1
    c[:, C_ONE:C_ONE + P] = 1
    for p in range(P):
        qc = GRID - 1 - p % GRID
        ws = min(max(qc - WIN_COLS // 2, 0), GRID - WIN_COLS)
        kc = np.arange(GRID)
        c[p, C_NEGM:C_NEGM + GRID] = np.where((kc >= ws) & (kc < ws + WIN_COLS), 0, NEG)
    t = np.arange(S)
    for g, w in enumerate((2, 4, 8, 16)):
        n = np.clip(t - w // 2 + w, 0, S) - np.clip(t - w // 2, 0, S)
        half, ch = g % 2, g // 2
        c[half * 64:half * 64 + 64, C_INV + ch * S:C_INV + (ch + 1) * S] = (1.0 / n.astype(np.float64)).astype(np.float32)
    nf = ROPE // 4
    inv = (np.float32(10000.0) ** (-np.arange(nf, dtype=np.float32) / np.float32(nf))).astype(np.float32)
    ang = np.concatenate([(t // GRID).astype(np.float32)[:, None] * inv, (t % GRID).astype(np.float32)[:, None] * inv], 1)
    cos, sin = np.cos(ang).T, np.sin(ang).T
    for part in range(2):
        for half in range(2):
            r = NOPE + part * 2 * nf + half * nf
            c[r:r + nf, C_COS:C_COS + S] = cos[part * nf:(part + 1) * nf]
            c[r:r + nf, C_SIN:C_SIN + S] = sin[part * nf:(part + 1) * nf] * (-1 if half == 0 else 1)
    c[:, C_RANK:C_RANK + 64] = np.tile(np.array([3, 2, 1, 0], np.float32), 16)
    c[:, C_EPS] = EPS
    return c


def build(nc, a, out):
    with ExitStack() as ctx:
        def sem(name):
            return ctx.enter_context(nc.semaphore(name))

        at = [16512]

        def sb(name, shape, dt=F32, offset=None):
            size = int(np.prod(shape[1:])) * 4
            if offset is None:
                offset = at[0]
                at[0] += (size + 31) // 32 * 32
            return nc.alloc_sbuf_tensor_at(name, shape, dt, offset=offset)

        class Region:

            def __init__(self, base, size):
                self.at, self.end = base, base + size

            def sb(self, name, shape, dt=F32):
                size = (int(np.prod(shape[1:])) * 4 + 31) // 32 * 32
                t = nc.alloc_sbuf_tensor_at(name, shape, dt, offset=self.at)
                self.at += size
                assert self.at <= self.end, name
                return t

        const = sb("const", [P, N_CONST])
        vec = sb("vec", [P, N_VEC])
        x_t = sb("x_t", [P, KC, T])
        raw = [sb(f"raw{i}", [P, KC, BW]) for i in range(RAW)]
        ring_at = at[0]
        w_hi = [sb(f"w_hi{i}", [P, KC, BW], F32R) for i in range(HL)]
        w_lo = [sb(f"w_lo{i}", [P, KC, BW], F32R) for i in range(HL)]
        ring_size = at[0] - ring_at
        h_at = at[0]
        h_hi = sb("h_hi", [P, KC, T], F32R)
        h_lo = sb("h_lo", [P, KC, T], F32R)
        h_size = at[0] - h_at
        small_at = at[0]
        pool_bd = sb("pool_bd", [P, 2, P])
        w_uq = sb("w_uq", [P, 2, HEADS * QK])
        w_uqs = sb("w_uqs", [P, 2, HEADS, QK])
        w_ukv = sb("w_ukv", [P, 4 * P])
        sgu_w = sb("sgu_w", [P, 4, P])
        sgu_wt = sb("sgu_wt", [P, 4, P])
        na_bias = sb("na_bias", [P, HEADS, 6, GRID])
        sgu_g = sb("sgu_g", [P, S])
        G = Region(small_at, at[0] - small_at)
        xg_hi = G.sb("xg_hi", [P, KC, 2 * SLOTS], F32R)
        xg_lo = G.sb("xg_lo", [P, KC, 2 * SLOTS], F32R)
        rb_row = sb("rb_row", [P, E])
        rw_hi = sb("rw_hi", [P, KC, E], F32R)
        rw_lo = sb("rw_lo", [P, KC, E], F32R)
        c_act = sb("c_act", [P, 16])
        mod = sb("mod", [P, 2, 48])
        amp = sb("amp", [P, 2, 2, KC])
        mod_row = sb("mod_row", [2, 2, BW])
        col = sb("col", [P, 64])
        rstd = sb("rstd", [P, 4])
        stat = sb("stat", [P, 4, 3])
        gates = sb("gates", [P, 4, E])
        pick_row = sb("pick_row", [P, 4, 2], mybir.dt.uint32)
        more = sb("more", [P, 4], mybir.dt.int32)
        area_at = at[0]
        area_size = 33024
        at[0] += area_size
        assert at[0] <= 229344, at[0]

        A = Region(area_at, area_size)
        a_pad = A.sb("a_pad", [P, 2, 2, PW])
        q_na = A.sb("q_na", [P, 2, T])
        k_na = A.sb("k_na", [P, 2, T])
        v_na = A.sb("v_na", [P, 4, S])
        sgu_u = A.sb("sgu_u", [P, 4, S])
        sgu_v = A.sb("sgu_v", [P, 4, S])
        q_low = A.sb("q_low", [P, 2, T])
        kv_low = A.sb("kv_low", [P, T])
        k_rope = A.sb("k_rope", [P, T])
        N = Region(area_at, area_size)
        nsq = N.sb("nsq", [P, 4, T])
        nx = N.sb("nx", [P, 2, T])
        nh = N.sb("nh", [P, 2, T])
        I = Region(area_at + 4096, area_size - 4096)
        x_tok = [I.sb(f"x_tok{t}", [P, D]) for t in range(4)]
        M = Region(area_at, area_size)
        y_sb = [M.sb(f"y_sb{i}", [P, D]) for i in range(2)]
        onehot = M.sb("onehot", [P, 4, 2 * SLOTS], F32R)
        hid_g = M.sb("hid_g", [P, FE])
        hid_m = M.sb("hid_m", [P, FE])
        M.at = area_at + 16384
        const2 = M.sb("const2", [P, N_CONST2])
        score = M.sb("score", [P, 4, E])
        biased = M.sb("biased", [P, 4, E])
        rank = M.sb("rank", [P, 4, E])
        cmp = M.sb("cmp", [P, 4, E])
        grp = M.sb("grp", [P, 4, 4])
        grank = M.sb("grank", [P, 4, 4])
        sel = M.sb("sel", [P, 4, E])
        slot = M.sb("slot", [P, 4, E])
        row = M.sb("row", [P, 4, E])
        pick = M.sb("pick", [P, 4, 4])
        pick0 = M.sb("pick0", [P, 4, 2])
        ht_hi = [M.sb(f"ht_hi{i}", [P, 2, SLOTS], F32R) for i in range(2)]
        ht_lo = [M.sb(f"ht_lo{i}", [P, 2, SLOTS], F32R) for i in range(2)]
        h_tok = [nc.alloc_sbuf_tensor_at(f"h_tok{i}", [P, 4, D], F32R, offset=h_at + 4 * KC * T * i) for i in range(2)]
        y_back = nc.alloc_sbuf_tensor_at("y_back", [P, 4, 2, D], F32, offset=h_at)
        y_rows = nc.dram_tensor("y_rows", (T // SLOTS * E * SLOTS, D), F32, kind="Internal").ap()
        B = Region(ring_at, ring_size)
        o_tok = B.sb("o_tok", [P, 4, 3 * S])
        v_mla = B.sb("v_mla", [P, 4, S])
        pool_d = B.sb("pool_d", [P, 2, T])
        prob = [B.sb(f"prob{i}", [P, T]) for i in range(3)]
        prob_t = [B.sb(f"prob_t{i}", [P, 4, P]) for i in range(3)]
        sgu_sq = B.sb("sgu_sq", [P, 4, S])
        win_a = B.sb("win_a", [P, 2, 2, PW])
        win_b = B.sb("win_b", [P, 2, 2, PW])
        H = Region(h_at, h_size)
        q_mla = H.sb("q_mla", [P, HEADS, T])
        k_mla = H.sb("k_mla", [P, HEADS, T])
        low_sq = H.sb("low_sq", [P, 3, T])
        rope_t = H.sb("rope_t", [P, HEADS, S])
        raw_vec = [nc.alloc_sbuf_tensor_at(f"raw_vec{i}", [P, P], F32, offset=area_at + i * 512) for i in range(2)]
        rw_in = nc.alloc_sbuf_tensor_at("rw_in", [P, KC, E], F32, offset=area_at + 1024)

        y_tok = nc.alloc_sbuf_tensor_at("y_tok", [P, 2, D], F32, offset=ring_at)

        ident = const[:, C_ID:C_ID + P]
        ones = const[:, C_ONE:C_ONE + P]
        eps = const[:, C_EPS:C_EPS + 1]

        bank = [ctx.enter_context(nc.psum_tensor(f"bank{i}", [P, 512], F32)) for i in range(8)]

        loaded = [sem(f"loaded{i}") for i in range(RAW)]
        s_ident = sem("s_ident")
        s_const, s_vecin, s_xin, s_xevd = sem("s_const"), sem("s_vecin"), sem("s_xin"), sem("s_xevd")
        s_bcast = sem("s_bcast")
        s_small, s_zero = sem("s_small"), sem("s_zero")
        s_vt, s_vec, s_cact = sem("s_vt"), sem("s_vec"), sem("s_cact")
        s_xt, s_xev = sem("s_xt"), sem("s_xev")
        s_rw = sem("s_rw")
        split_hi, split_lo, used = sem("split_hi"), sem("split_lo"), sem("used")
        ada_mm, ada_ea, ada_ed, ada_tr, s_mod, s_amp = sem("ada_mm"), sem("ada_ea"), sem("ada_ed"), sem("ada_tr"), sem("s_mod"), sem("s_amp")
        NORMS = 2 * DEPTH + 1
        n_sqa, n_sqd, n_sum, n_root, n_rstd, n_bc, n_x, n_hi, n_lo = (sem(n) for n in (
            "n_sqa", "n_sqd", "n_sum", "n_root", "n_rstd", "n_bc", "n_x", "n_hi", "n_lo"))
        n_h = [sem(f"n_h{i}") for i in range(2 * DEPTH + 1)]
        chain_d, chain_p = sem("chain_d"), sem("chain_p")
        s_swap, s_pads, s_wg, s_bias, s_pool = (sem(n) for n in ("s_swap", "s_pads", "s_wg", "s_bias", "s_pool"))
        proj_ea, proj_ed = sem("proj_ea"), sem("proj_ed")
        s_wt, s_wte = sem("s_wt"), sem("s_wte")
        s_lsq, s_lsum, s_lroot, s_lrstd, s_lbc, s_low = (sem(n) for n in (
            "s_lsq", "s_lsum", "s_lroot", "s_lrstd", "s_lbc", "s_low"))
        s_up, s_qe, s_ke, s_ve, s_rot = (sem(n) for n in ("s_up", "s_qe", "s_ke", "s_ve", "s_rot"))
        s_gv, s_groot, s_gn, s_mix, s_go = (sem(n) for n in ("s_gv", "s_groot", "s_gn", "s_mix", "s_go"))
        t_sc, t_mx, t_ex, t_tr, t_pa, t_pd, t_pv, t_o = (sem(n) for n in (
            "t_sc", "t_mx", "t_ex", "t_tr", "t_pa", "t_pd", "t_pv", "t_o"))
        m_ps, m_hi, m_lo, o_ev = sem("m_ps"), sem("m_hi"), sem("m_lo"), sem("o_ev")
        r_lg, r_sg, r_gate = sem("r_lg"), sem("r_sg"), sem("r_gate")
        s_const2, s_sel, s_pos, s_more, q_tok, q_ta, q_td = (sem(n) for n in (
            "s_const2", "s_sel", "s_pos", "s_more", "q_tok", "q_ta", "q_td"))
        q_p, g_hi, g_lo, x_hi, x_lo, q_s, q_m, q_t, q_th, q_tl, q_ya, q_yd = (sem(n) for n in (
            "q_p", "g_hi", "g_lo", "x_hi", "x_lo", "q_s", "q_m", "q_t", "q_th", "q_tl", "q_ya", "q_yd"))
        q_out = [sem("q_out_even"), sem("q_out_odd")]
        q_row, q_c, q_ct, x_moe = sem("q_row"), sem("q_c"), sem("q_ct"), sem("x_moe")
        q_back = [sem(f"q_back{t}") for t in range(4)]
        f_y, f_ev, f_out = sem("f_y"), sem("f_ev"), sem("f_out")

        def blocks_before(l):
            return N_MOE * sum(n - 1 for n in ROUNDS[:l])

        def rounds_before(l):
            return sum(ROUNDS[:l])

        def streams(l):
            return 2 if l < DEPTH - 1 else 1

        def split_index(l, r):
            return blocks_before(l) + l * SPLIT_PER_LAYER + r - N_ADA

        def raw_index(l, r):
            return blocks_before(l) + l * PER_LAYER + r

        def block_cols(r):
            return IN_W - 7 * BW + ROPE if r == N_ADA + 7 else BW

        def attention_jobs(l):
            jobs = [("na", h, t) for h in range(HEADS) for t in (0, 1)]
            if streams(l) == 2:
                jobs += [("na", h, t) for h in range(HEADS) for t in (2, 3)]
            jobs += [("mla", h, t) for h in range(HEADS) for t in (0, 1)]
            if streams(l) == 2:
                jobs += [("mla", h, t) for h in range(HEADS) for t in (2, 3)]
            return jobs

        SMALL = 8

        JOBS = 32

        def nth(role, i, j):
            if isinstance(i, int):
                e = 2 * i + j
                if role < 2:
                    return 3 * e + role if e else 1 + role
                return min(3 * e + 5, N_MOE)
            return i * 6 + (3 * j + (role if role < 2 else 5))

        def raw_place(role, i, j):
            if isinstance(i, int):
                q = nth(role, i, j) - 1
                return q % RAW, q // RAW + 1
            q = 3 * j + (role if role < 2 else 5) - 1
            return q % RAW, i + (q // RAW + 1)

        def before(role, i, j):
            if isinstance(i, int) and 2 * i + j == 0:
                return 0
            return nth(role, i, j - 1)

        def round_start(l, k):
            m = rounds_before(l) + k
            r = N_ADA + N_WIN + N_WOUT
            s0 = split_index(l, r) + k * N_MOE
            n0 = raw_index(l, r) + k * N_MOE
            assert n0 % RAW == 0 and s0 % HL == 0
            return m, s0, n0 // RAW

        def rounds(eng, l, one_round, skip):
            one_round(0)
            for k in range(1, ROUNDS[l]):
                if k == 1:
                    eng.wait_ge(s_more, l + 1)
                again = eng.value_load(more[0:1, k - 1:k], min_val=0, max_val=1)
                with eng.If(again > 0):
                    one_round(k)
                with eng.Else():
                    skip(k)

        def steps(eng, step, n_tail, m):
            peeled = 2 if m else 4
            for e in range(peeled):
                step(e // 2, e % 2, e)
            with eng.Fori(peeled // 2, E // 2 - 1) as i:
                for j in range(2):
                    step(i, j, None)
            for e in range(E - 2, E + n_tail):
                step(E // 2 - 1, e - (E - 2), e)

        def combine_units(l):
            return [(t, half) for t in range(2 * streams(l)) for half in range(2)]

        COMBINE_AT = 8

        def done(l, r):
            return split_index(l, r) + 1

        ada_w, w_in, w_out = a["ada_w"], a["w_in"], a["w_out"]
        w_gate, w_up, w_down = a["moe_w_gate"], a["moe_w_up"], a["moe_w_down"]

        block = ctx.enter_context(nc.Block())

        @block.sync
        def _(sp):
            def free_slot(l, r):
                if l and r < RAW:
                    sp.wait_ge(split_hi, split_index(l, N_ADA) - RAW + r + 1)
                    sp.wait_ge(split_lo, split_index(l, N_ADA) - RAW + r + 1)
                elif RAW <= r < N_ADA + RAW:
                    sp.wait_ge(ada_mm, l * N_ADA + r - RAW + 1)
                elif r >= N_ADA + RAW:
                    sp.wait_ge(split_hi, split_index(l, r - RAW) + 1)
                    sp.wait_ge(split_lo, split_index(l, r - RAW) + 1)

            for l in range(DEPTH):
                for r in range(N_ADA + N_WIN + N_WOUT):
                    free_slot(l, r)
                    n = raw_index(l, r)
                    if r < N_ADA:
                        src, c0, w = ada_w[l], r * BW, BW
                    elif r < N_ADA + N_WIN:
                        src, c0 = w_in[l], (r - N_ADA) * BW
                        w = min(BW, IN_W - c0)
                    else:
                        src, c0, w = w_out[l], (r - N_ADA - N_WIN) * BW, BW
                    sp.dma_start(raw[n % RAW][:, :, 0:w],
                                 src[:, c0:c0 + w].rearrange("(k p) n -> p k n", p=P)).then_inc(loaded[n % RAW], 16)

                def one_round(k, l=l):
                    m, s0, n0 = round_start(l, k)

                    def load(role, i, j):
                        q, _ = raw_place(role, i, j)
                        sp.wait_ge(split_hi, nth(role, i, j) + (s0 - RAW))
                        sp.wait_ge(split_lo, nth(role, i, j) + (s0 - RAW))
                        src = (w_gate, w_up, w_down)[role][l][bass.ds(2 * i + j, 1)]
                        dst = raw[q][:, :, :]
                        if role < 2:
                            src = src.rearrange("a (k p) n -> p (a k) n", p=P)
                        else:
                            src = src.rearrange("a (f p) n -> p (a f) n", p=P)
                            dst = dst.rearrange("p (f k) n -> p f (k n)", f=2)
                        sp.dma_start(dst, src).then_inc(loaded[q], 16)

                    def step(i, j, e):
                        if e != E:
                            load(0, i, j)
                            load(1, i, j)
                        if e != 0:
                            load(2, i, j - 1)

                    steps(sp, step, 1, m)

                def skip(k, l=l):
                    m, s0, n0 = round_start(l, k)
                    for q in range(RAW):
                        sp.wait_ge(loaded[q], 16 * n0)
                        sp.sem_inc(loaded[q], 16 * (N_MOE // RAW))

                rounds(sp, l, one_round, skip)
            for t in range(2):
                sp.wait_ge(f_ev, 4)
                sp.dma_start(out[t * P:(t + 1) * P, :], y_tok[:, t, :]).then_inc(f_out, 16)
            sp.wait_ge(f_out, 32)


        @block.gpsimd
        def _(pool):
            made = [0]

            def then(ins):
                made[0] += 1
                ins.then_inc(chain_p, 1)
                pool.wait_ge(chain_p, made[0])

            def small_weights(l):
                if l:
                    pool.wait_ge(used, split_index(l, N_ADA))
                pool.memset(pool_bd[:, :, :], 0.0).then_inc(s_zero, 1)
                pool.wait_ge(s_small, l * (16 * SMALL) + 16 * SMALL)
                pool.wait_ge(s_vec, 1)
                pool.wait_ge(s_const, 16)
                for c in range(2):
                    pool.tensor_scalar(w_uq[:, c, :], w_uq[:, c, :], vec[:, V_QG + 2 * l + c:V_QG + 2 * l + c + 1], 1.0,
                                       ALU.mult, ALU.mult)
                then(pool.tensor_scalar(w_ukv[:, :], w_ukv[:, :], vec[:, V_KVG + l:V_KVG + l + 1], 1.0, ALU.mult, ALU.mult))
                w4 = w_uq[:, :, :].rearrange("p c (h m) -> p c h m", m=QK)
                for c in range(2):
                    pool.tensor_copy(w_uqs[:, c, :, 0:NOPE], w4[:, c, :, 0:NOPE])
                    for half in range(2):
                        for part in range(2):
                            to, fr = NOPE + 16 * part + 8 * half, NOPE + 16 * part + 8 * (1 - half)
                            last = pool.tensor_copy(w_uqs[:, c, :, to:to + 8], w4[:, c, :, fr:fr + 8])
                last.then_inc(s_wg, 1)
                for h in range(HEADS):
                    last = pool.tensor_tensor(na_bias[:, h, :, :], na_bias[:, h, :, :],
                                              const[:, C_NEGM:C_NEGM + GRID][:, None, :].to_broadcast([P, 6, GRID]), ALU.add)
                last.then_inc(s_bias, 1)

            small_weights(0)
            for l in range(DEPTH):
                ns = streams(l)
                n = raw_index(l, N_ADA + 7)
                pool.wait_ge(loaded[n % RAW], 16 * (n // RAW + 1))
                rk = raw[n % RAW]
                for half in range(2):
                    for part in range(2):
                        to, fr = 160 + 16 * part + 8 * half, 128 + 16 * part + 8 * (1 - half)
                        last = pool.tensor_copy(rk[:, :, to:to + 8], rk[:, :, fr:fr + 8])
                last.then_inc(s_swap, 1)
                pool.wait_ge(used, done(l, N_ADA))
                pool.memset(a_pad[:, :, :, 0:PAD], 0.0)
                pool.memset(a_pad[:, :, :, PAD + S:PW], 0.0).then_inc(s_pads, 1)
                pool.wait_ge(proj_ed, l * 5 + 1)
                pool.wait_ge(s_pads, l + 1)
                pool.wait_ge(used, split_index(l, N_ADA + 7) + 1)

                def window(dst, src, ch, p0, lo, hi, back, ahead):
                    return pool.tensor_tensor(dst[p0:P, ch, 0:ns, lo:hi], src[p0:P, ch, 0:ns, lo - back:hi - back],
                                              src[p0:P, ch, 0:ns, lo + ahead:hi + ahead], ALU.add)

                window(win_a, a_pad, 0, 0, 1, PW, 1, 0)
                then(window(win_a, a_pad, 1, 0, 1, PW, 1, 0))
                then(window(win_b, win_a, 0, 64, 2, PW - 1, 1, 1))
                then(window(win_b, win_a, 1, 0, 2, PW - 1, 1, 1))
                then(window(win_a, win_b, 1, 0, 4, PW - 3, 2, 2))
                then(window(win_b, win_a, 1, 64, 8, PW - 8, 4, 4))
                for g, w in enumerate((win_a, win_b, win_a, win_b)):
                    ch, p0 = g // 2, 64 * (g % 2)
                    sl = w[p0:p0 + 64, ch, 0:ns, PAD:PAD + S]
                    inv = const[p0:p0 + 64, C_INV + ch * S:C_INV + (ch + 1) * S][:, None, :].to_broadcast([64, ns, S])
                    then(pool.tensor_tensor(sl, sl, inv, ALU.mult))
                for g, w in enumerate((win_a, win_b, win_a, win_b)):
                    ch, p0 = g // 2, 64 * (g % 2)
                    ins = pool.tensor_tensor(pool_d[p0:p0 + 64, ch, 0:ns * S].rearrange("p (s t) -> p s t", s=ns),
                                             w[p0:p0 + 64, ch, 0:ns, PAD:PAD + S],
                                             a_pad[p0:p0 + 64, ch, 0:ns, PAD:PAD + S], ALU.subtract)
                    if g < 3:
                        then(ins)
                ins.then_inc(s_pool, 1)

                pool.wait_ge(q_row, l + 1)
                for par in range(2):
                    pool.wait_ge(q_out[par], 16 * (E // 2) * rounds_before(l + 1))

                def take(n):
                    if n < ROUNDS[l]:
                        again = pool.value_load(more[0:1, n - 1:n], min_val=0, max_val=1)
                        with pool.If(again > 0):
                            take(n + 1)
                        with pool.Else():
                            take_from(n)
                    else:
                        take_from(n)

                def take_from(n):
                    for t in range(2 * ns):
                        for i in range(2):
                            pool.indirect_dma_start(y_back[:, t, i, :], None, y_rows[0:n * E * SLOTS, :],
                                                    bass.IndirectOffsetOnAxis(ap=pick_row[:, t, i:i + 1], axis=0)).then_inc(q_back[t], 16)

                take(1)
                if l + 1 < DEPTH:
                    small_weights(l + 1)

        @block.scalar
        def _(act):
            def small_loads(l):
                if l:
                    act.wait_ge(used, split_index(l, N_ADA))
                act.wait_ge(s_zero, l + 1)
                pw = a["pool_w"]
                for half in range(2):
                    src = bass.AP(pw.tensor, (l * 4 + half) * 4096, [[64, 64], [8192, 2], [1, 64]])
                    act.dma_start(pool_bd[64 * half:64 * half + 64, :, 64 * half:64 * half + 64], src).then_inc(s_small, 16)
                act.dma_start(w_uq[:, :, :], a["mla_w_uq"][l].rearrange("(c p) n -> p c n", p=P)).then_inc(s_small, 16)
                act.dma_start(w_ukv[:, :], a["mla_w_ukv"][l]).then_inc(s_small, 16)
                act.dma_start(sgu_g[:, :], bass.AP(a["sgu_norm_g"].tensor, l * S, [[0, P], [1, S]])).then_inc(s_small, 16)
                act.dma_start(sgu_w[:, :, :], a["sgu_w"][l].rearrange("g p q -> p g q")).then_inc(s_small, 16)
                rp = a["na_rpb"]
                for half in range(2):
                    src = bass.AP(rp.tensor, (2 * l + half) * HEADS * 6 * P, [[1, GRID], [P, HEADS * 6], [1, GRID]])
                    act.dma_start(na_bias[64 * half:64 * half + 64, :, :, :].rearrange("p h r c -> p (h r) c"), src).then_inc(s_small, 16)

            act.dma_start(raw_vec[0][0:112, :], a["vec0"]).then_inc(s_vecin, 16)
            act.dma_start(raw_vec[1][0:N_VEC - 112, :], a["vec1"]).then_inc(s_vecin, 16)
            act.dma_start(const[:, 0:P], a["const"][:, 0:P]).then_inc(s_ident, 16)
            act.wait_ge(s_vec, 1)
            act.activation(c_act[:, :], vec[:, V_C:V_C + 16], ACT.Silu).then_inc(s_cact, 1)
            for t in range(4):
                act.dma_start(x_tok[t][:, :], a["x" if t < 2 else "ctx"][(t % 2) * P:(t % 2 + 1) * P, :]).then_inc(s_xin, 16)
            act.dma_start(const[:, P:N_CONST], a["const"][:, P:N_CONST]).then_inc(s_const, 16)
            act.dma_start(rw_in[:, :, :], a["router_w"].rearrange("(k p) e -> p k e", p=P)).then_inc(s_bcast, 16)
            act.dma_start(rb_row[:, :], bass.AP(a["router_b"].tensor, 0, [[0, P], [1, E]])).then_inc(s_bcast, 16)
            small_loads(0)
            act.wait_ge(s_bcast, 32)
            act.activation(rw_hi[:, :, :], rw_in[:, :, :], ACT.Copy).then_inc(s_rw, 1)

            def split(l, r):
                s, n = split_index(l, r), raw_index(l, r)
                act.wait_ge(loaded[n % RAW], 16 * (n // RAW + 1))
                if r == N_ADA + 7:
                    act.wait_ge(s_swap, l + 1)
                if s >= HL:
                    act.wait_ge(used, s - HL + 1)
                w = block_cols(r)
                act.activation(w_hi[s % HL][:, :, 0:w], raw[n % RAW][:, :, 0:w], ACT.Copy).then_inc(split_hi, 1)

            def norm(i, width, which, l):
                ns = width // S
                if i % 2:
                    act.wait_ge(o_ev, l * KC + KC)
                if which is None:
                    act.wait_ge(x_moe, sum(len(combine_units(n)) for n in range(DEPTH)))
                for k in range(0, KC, 2):
                    if k >= 4:
                        act.wait_ge(n_sum, i * KC + k - 3)
                    act.activation(nsq[:, k % 4, 0:width], x_t[:, k, 0:width], ACT.Square).then_inc(n_sqa, 1)
                act.wait_ge(n_sum, i * KC + KC)
                act.activation(col[:, 0:width // P], bank[6][:, 0:width // P], ACT.Sqrt, bias=eps, scale=1.0 / D).then_inc(n_root, 1)
                for k in range(KC):
                    act.wait_ge(n_x, i * KC + k + 1)
                    if k >= 2:
                        if which is None:
                            act.wait_ge(f_y, k - 1)
                        else:
                            act.wait_ge(n_lo, i * KC + k - 1)
                    if which is None:
                        act.activation(nh[:, k % 2, 0:width], nx[:, k % 2, 0:width], ACT.Identity,
                                       scale=vec[:, V_FIN + k:V_FIN + k + 1]).then_inc(n_h[i], 1)
                        continue
                    for s in range(ns):
                        act.activation(nh[:, k % 2, s * S:(s + 1) * S], nx[:, k % 2, s * S:(s + 1) * S], ACT.Identity,
                                       bias=mod[:, s, 24 * which + k:24 * which + k + 1],
                                       scale=amp[:, which, s, k:k + 1]).then_inc(n_h[i], 1)
                    act.wait_ge(n_h[i], ns * (k + 1))
                    act.activation(h_hi[:, k, 0:width], nh[:, k % 2, 0:width], ACT.Copy).then_inc(n_hi, 1)

            for l in range(DEPTH):
                ns = streams(l)
                nt, width = 2 * ns, ns * S
                for j in range(1, N_ADA, 2):
                    act.wait_ge(ada_mm, l * N_ADA + j + 1)
                    if j >= 2:
                        act.wait_ge(ada_tr, l * N_ADA + j - 1)
                    act.activation(mod_row[:, j % 2, :], bank[j % 4][0:2, 0:BW], ACT.Copy).then_inc(ada_ea, 1)
                    if l == 0 and 4 <= j < 12:
                        k = j - 4
                        act.wait_ge(s_xt, k + 1)
                        act.activation(x_t[:, k, :], bank[4 + k % 3][:, :], ACT.Copy).then_inc(s_xev, 1)
                for r in range(N_ADA, N_ADA + HL):
                    split(l, r)
                act.wait_ge(s_amp, l + 1)
                if l == 0:
                    act.wait_ge(s_const, 16)
                norm(2 * l, T, 0, l)
                for b in range(N_WIN):
                    if b == 1:
                        act.wait_ge(used, done(l, N_ADA + 1))
                        act.activation(q_na[:, 0, 0:width], bank[2][:, 0:width], ACT.Copy, scale=NA_SCALE)
                        act.activation(q_na[:, 1, 0:width], bank[3][:, 0:width], ACT.Copy, scale=NA_SCALE).then_inc(proj_ea, 1)
                    if b in (4, 5):
                        act.wait_ge(used, done(l, N_ADA + b))
                        dst = sgu_u if b == 4 else sgu_v
                        for s in range(ns):
                            last = act.activation(dst[:, 2 * s:2 * s + 2, :].rearrange("p t n -> p (t n)"),
                                                  bank[2 * (b % 4) + s][:, :], ACT.Gelu_apprx_tanh)
                        last.then_inc(proj_ea, 1)
                    if b == 7:
                        act.wait_ge(used, done(l, N_ADA + 7))
                        act.activation(kv_low[:, :], bank[6][:, :], ACT.Copy).then_inc(proj_ea, 1)
                    if b + HL < N_WIN:
                        split(l, N_ADA + b + HL)
                act.wait_ge(used, split_index(l, N_ADA + 7) + 1)
                act.wait_ge(proj_ed, l * 5 + 4)
                act.activation(low_sq[:, 0:2, 0:width], q_low[:, :, 0:width], ACT.Square).then_inc(s_lsq, 1)
                act.wait_ge(proj_ea, l * 4 + 4)
                act.activation(low_sq[:, 2, :], kv_low[:, :], ACT.Square).then_inc(s_lsq, 1)
                act.wait_ge(s_lsum, l + 1)
                act.activation(col[:, 8:8 + nt], bank[7][:, 0:nt], ACT.Sqrt, bias=eps, scale=1.0 / 256)
                act.activation(col[:, 12:16], bank[7][:, 4:8], ACT.Sqrt, bias=eps, scale=1.0 / P).then_inc(s_lroot, 1)
                act.wait_ge(s_gv, l + 1)
                act.activation(col[:, 32:32 + 4 * nt], col[:, 16:16 + 4 * nt], ACT.Sqrt, bias=eps, scale=1.0 / 64).then_inc(s_groot, 1)
                act.wait_ge(s_wt, l + 1)
                act.activation(sgu_wt[:, :, :].rearrange("p g n -> p (g n)"), bank[6][:, :], ACT.Copy).then_inc(s_wte, 1)
                for h in range(HEADS):
                    act.wait_ge(s_up, l * 11 + h + 1)
                    act.activation(q_mla[0:QK, h, 0:width], bank[2 + h][0:QK, 0:width], ACT.Copy, scale=MLA_SCALE).then_inc(s_qe, 1)
                for h in range(HEADS):
                    act.wait_ge(s_up, l * 11 + 6 + h + 1)
                    act.activation(k_mla[0:NOPE, h, :], bank[h][0:NOPE, :], ACT.Copy).then_inc(s_ke, 1)
                act.wait_ge(s_up, l * 11 + 11)
                act.activation(v_mla[:, 0:2, :].rearrange("p t n -> p (t n)"), bank[4][:, :], ACT.Copy)
                act.activation(v_mla[:, 2:4, :].rearrange("p t n -> p (t n)"), bank[5][:, :], ACT.Copy).then_inc(s_ve, 1)
                jobs = attention_jobs(l)
                for i in range(len(jobs) + 1):
                    if i < len(jobs):
                        nk = T if jobs[i][2] < 2 else S
                        act.wait_ge(t_mx, l * JOBS + i + 1)
                        if i >= 3:
                            act.wait_ge(t_tr, l * JOBS + i - 2)
                        act.activation(prob[i % 3][:, 0:nk], bank[i % 3][:, 0:nk], ACT.Exp, bias=stat[:, i % 4, 0:1],
                                       accum_out=stat[:, i % 4, 1:2]).then_inc(t_ex, 1)
                    if i >= 1 and i % 2 == 1:
                        q = i - 1
                        nkt = 4 if jobs[q][2] < 2 else 2
                        act.wait_ge(t_tr, l * JOBS + q + 1)
                        if q >= 3:
                            act.wait_ge(t_pv, l * JOBS + q - 2)
                        act.activation(prob_t[q % 3][:, 0:nkt, :].rearrange("p k n -> p (k n)"),
                                       bank[3 + q % 2][:, 0:nkt * P], ACT.Copy).then_inc(t_pa, 1)
                for c in range(KC):
                    act.wait_ge(m_ps, l * KC + c + 1)
                    if c == 0:
                        act.wait_ge(t_pv, l * JOBS + len(jobs))
                    scale = vec[:, V_PS + 2 * l + c:V_PS + 2 * l + c + 1] if c < 2 else 1.0
                    act.activation(h_hi[:, c, 0:width], bank[c][:, 0:width], ACT.Identity if c < 2 else ACT.Copy,
                                   scale=scale).then_inc(m_hi, 1)
                act.dma_start(const2[:, :], a["const2"]).then_inc(s_const2, 16)
                for r in range(N_ADA + N_WIN, N_ADA + N_WIN + N_WOUT):
                    split(l, r)
                norm(2 * l + 1, width, 1, l)
                act.wait_ge(r_lg, l + 1)
                act.activation(score[:, 0:nt, :].rearrange("p t e -> p (t e)"), bank[5][:, 0:nt * E], ACT.Sigmoid).then_inc(r_sg, 1)

                def split_expert(l, k, role, i, j):
                    m, s0, n0 = round_start(l, k)
                    q, n = raw_place(role, i, j)
                    act.wait_ge(loaded[q], n * 16 + 16 * n0)
                    act.wait_ge(used, before(role, i, j) + s0)
                    act.activation(w_hi[role][:, :, :], raw[q][:, :, :], ACT.Copy).then_inc(split_hi, 1)

                split_expert(l, 0, 0, 0, 0)
                act.wait_ge(q_tok, l * (2 * KC) + KC)
                for c in range(KC):
                    act.activation(h_tok[0][:, 0:nt, c * P:(c + 1) * P], bank[c][:, 0:width].rearrange("p (t d) -> p t d", d=P),
                                   ACT.Copy).then_inc(q_ta, 1)
                split_expert(l, 0, 1, 0, 0)
                act.wait_ge(q_tok, (l + 1) * (2 * KC))
                for c in range(KC // 2):
                    act.activation(h_tok[1][:, 0:nt, c * P:(c + 1) * P], bank[c][:, 0:width].rearrange("p (t d) -> p t d", d=P),
                                   ACT.Copy).then_inc(q_ta, 1)

                def one_round(k, l=l):
                    m, s0, n0 = round_start(l, k)

                    def y_half(i, j, y_rows_=y_rows.rearrange("(k e p) d -> k e p d", e=E, p=SLOTS)):
                        par, i2 = j % 2, i + j // 2
                        act.wait_ge(used, nth(2, i, j) + s0)
                        act.wait_ge(q_out[par], i2 * 16 + 16 * (E // 2) * m)
                        act.activation(y_sb[par][:, 0:512], bank[6][:, :], ACT.Copy).then_inc(q_ya, 1)

                    def y_store(i, j, y_rows_=y_rows.rearrange("(k e p) d -> k e p d", e=E, p=SLOTS)):
                        act.wait_ge(q_ya, 2 * i + (m * E + j + 1))
                        act.wait_ge(q_yd, 2 * i + (m * E + j + 1))
                        act.dma_start(y_rows_[k, bass.ds(2 * i + j, 1), :, :].rearrange("a p d -> p (a d)"),
                                      y_sb[j % 2][:, :]).then_inc(q_out[j % 2], 16)

                    def step(i, j, e):
                        if (e is None or e < E) and j % 2 == 0:
                            for half in range(2):
                                act.wait_ge(g_hi, 2 * i + (m * E + half + 1))
                                for b in range(2):
                                    ins = act.activation(xg_hi[:, 4 * half + 2 * b:4 * half + 2 * b + 2, :].rearrange("p k n -> p (k n)"),
                                                         bank[2 * half + b][:, :], ACT.Copy)
                                ins.then_inc(x_hi, 1)
                        if e is None or e >= 2:
                            y_half(i, j - 2)
                        if e is None or 1 <= e <= E:
                            split_expert(l, k, 2, i, j - 1)
                            act.wait_ge(q_t, 2 * i + (m * E + j))
                            act.wait_ge(used, s0 if e in (1, 2) else nth(2, i, j - 3) + s0)
                            act.activation(ht_hi[(j - 1) % 2][:, :, :].rearrange("p f n -> p (f n)"), bank[5][:, 0:2 * SLOTS],
                                           ACT.Copy).then_inc(q_th, 1)
                        if e is None or e >= 2:
                            y_store(i, j - 2)
                        if e is None or e < E - 1:
                            split_expert(l, k, 0, i, j + 1)
                        if e is None or e < E:
                            act.wait_ge(used, nth(1, i, j) + s0)
                            act.wait_ge(q_m, 2 * i + (m * E + j))
                            act.activation(hid_g[:, :], bank[4][:, 0:FE], ACT.Silu).then_inc(q_s, 1)
                        if e is None or e < E - 1:
                            split_expert(l, k, 1, i, j + 1)

                    if k:
                        split_expert(l, k, 0, 0, 0)
                        split_expert(l, k, 1, 0, 0)
                    steps(act, step, 2, m)

                def skip(k, l=l):
                    m, s0, n0 = round_start(l, k)
                    act.wait_ge(split_hi, s0)
                    act.wait_ge(q_ya, m * E)
                    act.sem_inc(split_hi, N_MOE)
                    for sem_ in (x_hi, q_th, q_ya, q_s):
                        act.sem_inc(sem_, E)
                    for sem_ in q_out:
                        act.wait_ge(sem_, 16 * (E // 2) * m)
                        act.sem_inc(sem_, 16 * (E // 2))

                rounds(act, l, one_round, skip)
                if l + 1 < DEPTH:
                    small_loads(l + 1)
            norm(2 * DEPTH, S, None, DEPTH)
            for t in range(2):
                act.wait_ge(f_y, KC)
                act.activation(y_tok[:, t, 512:1024], bank[1 + 2 * t][:, :], ACT.Copy).then_inc(f_ev, 1)

        @block.tensor
        def _(pe):
            def product(dst, w_hi_, w_lo_, x_hi_, x_lo_, first, last):
                pe.matmul(dst, w_hi_, x_hi_, start=first, stop=False)
                pe.matmul(dst, w_hi_, x_lo_, start=False, stop=False)
                return pe.matmul(dst, w_lo_, x_hi_, start=False, stop=last)

            def wait_split(l, r):
                pe.wait_ge(split_lo, split_index(l, r) + 1)

            def column_sums(dst, src, k, n, last):
                for t in range(n):
                    ins = pe.matmul(dst[:, t:t + 1], src[:, t * P:(t + 1) * P], ones[:, 0:1], start=(k == 0 and t == 0),
                                    stop=last, skip_group_check=True)
                return ins

            def rows_of(dst, column, n):
                for t in range(n):
                    ap = column[:, t:t + 1].to_broadcast([P, P])
                    ins = pe.matmul(dst[:, t * P:(t + 1) * P], ap, ident, start=True, stop=True)
                return ins

            def norm(i, width):
                n = width // P
                for k in range(KC):
                    pe.wait_ge(n_sqa if k % 2 == 0 else n_sqd, i * (KC // 2) + k // 2 + 1)
                    column_sums(bank[6], nsq[:, k % 4, :], k, n, k == KC - 1).then_inc(n_sum, 1)
                pe.wait_ge(n_rstd, i + 1)
                rows_of(bank[7], rstd, n).then_inc(n_bc, 1)

            def combine(l, u):
                units = combine_units(l)
                n = sum(len(combine_units(i)) for i in range(l))
                t, half = units[u]
                pe.wait_ge(q_c, n // 2 + t + 1)
                if u >= 3:
                    pe.wait_ge(x_moe, n + u - 2)
                for c in range(4):
                    k = 4 * half + c
                    ins = pe.transpose(bank[4 + u % 3][:, c * P:(c + 1) * P], y_back[:, t, 0, k * P:(k + 1) * P], ident)
                ins.then_inc(q_ct, 1)

            pe.wait_ge(s_ident, 16)
            pe.wait_ge(s_vecin, 32)
            pe.transpose(bank[0][:, 0:112], raw_vec[0][0:112, :], ident[0:112, 0:112])
            pe.transpose(bank[0][:, 112:N_VEC], raw_vec[1][0:N_VEC - 112, :], ident[0:N_VEC - 112, 0:N_VEC - 112]).then_inc(s_vt, 1)
            pe.wait_ge(s_cact, 1)

            for l in range(DEPTH):
                ns = streams(l)
                nt, width = 2 * ns, ns * S

                def turn(j):
                    pe.wait_ge(ada_ea if j % 2 else ada_ed, l * (N_ADA // 2) + j // 2 + 1)
                    for i in range(2):
                        c = 2 * j + i
                        ins = pe.transpose(bank[7][:, 2 * c:2 * c + 2], mod_row[:, j % 2, i * P:(i + 1) * P], ident[0:2, 0:2])
                    ins.then_inc(ada_tr, 1)

                for j in range(N_ADA):
                    n = raw_index(l, j)
                    pe.wait_ge(loaded[n % RAW], 16 * (n // RAW + 1))
                    if j >= 4:
                        pe.wait_ge(ada_ea if j % 2 else ada_ed, l * (N_ADA // 2) + (j - 4) // 2 + 1)
                    for k in range(KC):
                        ins = pe.matmul(bank[j % 4][0:2, 0:BW], c_act[:, k:k + 9:8], raw[n % RAW][:, k, :],
                                        start=(k == 0), stop=(k == KC - 1))
                    ins.then_inc(ada_mm, 1)
                    if j == 1 and l:
                        pe.wait_ge(q_ya, E * rounds_before(l))
                        pe.wait_ge(q_yd, E * rounds_before(l))
                    if j:
                        turn(j - 1)
                    if l and 0 <= j - COMBINE_AT < len(combine_units(l - 1)):
                        combine(l - 1, j - COMBINE_AT)
                    if l == 0 and 4 <= j < 12:
                        k = j - 4
                        pe.wait_ge(s_xin, 64)
                        if k >= 3:
                            pe.wait_ge(s_xev if (k - 3) % 2 else s_xevd, (k - 3) // 2 + 1)
                        for t in range(4):
                            ins = pe.transpose(bank[4 + k % 3][:, t * P:(t + 1) * P], x_tok[t][:, k * P:(k + 1) * P], ident)
                        ins.then_inc(s_xt, 1)
                turn(N_ADA - 1)

                if l == 0:
                    pe.wait_ge(s_const, 16)
                norm(2 * l, T)

                def by_feature(b, c, dst, c0, m, width, l=l):
                    s = split_index(l, N_ADA + b) % HL
                    for k in range(KC):
                        if b == 0 and c == 0:
                            pe.wait_ge(n_lo, (2 * l) * (KC) + k + 1)
                        ins = product(dst[0:m, 0:width], w_hi[s][:, k, c0:c0 + m], w_lo[s][:, k, c0:c0 + m],
                                      h_hi[:, k, 0:width], h_lo[:, k, 0:width], k == 0, k == KC - 1)
                    return ins

                for b in range(N_WIN):
                    wait_split(l, N_ADA + b)
                    if b == 4:
                        pe.wait_ge(proj_ed, l * 5 + 1)
                    if b == 5:
                        pe.wait_ge(proj_ea, l * 4 + 1)
                    if b == 6:
                        pe.wait_ge(proj_ed, l * 5 + 2)
                    if b == 7:
                        pe.wait_ge(proj_ed, l * 5 + 3)
                        pe.wait_ge(proj_ea, l * 4 + 2)
                    b0 = 2 * (b % 4)
                    if b in (3, 4, 5):
                        s = split_index(l, N_ADA + b) % HL
                        for t in range(4 if b == 3 else nt):
                            dst = bank[b0 + t // 2][:, (t % 2) * BW:(t % 2 + 1) * BW]
                            for k in range(KC):
                                pe.matmul(dst, h_hi[:, k, t * P:(t + 1) * P], w_hi[s][:, k, :], start=(k == 0), stop=False)
                                pe.matmul(dst, h_hi[:, k, t * P:(t + 1) * P], w_lo[s][:, k, :], start=False, stop=False)
                                ins = pe.matmul(dst, h_lo[:, k, t * P:(t + 1) * P], w_hi[s][:, k, :], start=False, stop=(k == KC - 1))
                    elif b == 7:
                        by_feature(b, 0, bank[6], 0, P, T)
                        by_feature(b, 1, bank[7], 64, QK, T)
                        ins = by_feature(b, 1, bank[0], 96, QK, S)
                    else:
                        for c in range(2):
                            ins = by_feature(b, c, bank[b0 + c], c * P, P, T if b == 2 else width)
                    ins.then_inc(used, 1)

                pe.wait_ge(s_small, l * (16 * SMALL) + 16 * SMALL)
                pe.wait_ge(proj_ea, l * 4 + 4)
                for g in range(4):
                    ins = pe.transpose(bank[6][:, g * P:(g + 1) * P], sgu_w[:, g, :], ident)
                ins.then_inc(s_wt, 1)
                pe.wait_ge(s_lsq, l * 2 + 2)
                pe.wait_ge(proj_ed, l * 5 + 5)
                for c in range(2):
                    column_sums(bank[7][:, 0:4], low_sq[:, c, :], c, nt, c == 1)
                for t in range(4):
                    ins = pe.matmul(bank[7][:, 4 + t:5 + t], low_sq[:, 2, t * P:(t + 1) * P], ones[:, 0:1], start=False,
                                    stop=True, skip_group_check=True)
                ins.then_inc(s_lsum, 1)
                pe.wait_ge(s_lrstd, l + 1)
                rows_of(bank[0], col[:, 48:52], nt)
                rows_of(bank[1], col[:, 52:56], 4).then_inc(s_lbc, 1)
                pe.wait_ge(s_wg, l + 1)
                pe.wait_ge(s_low, l * 3 + 2)
                for h in range(HEADS):
                    for c in range(2):
                        ins = pe.matmul(bank[2 + h][0:QK, 0:width], w_uq[:, c, h * QK:(h + 1) * QK], q_low[:, c, 0:width],
                                        start=(c == 0), stop=(c == 1))
                    ins.then_inc(s_up, 1)
                pe.wait_ge(s_wte, l + 1)
                pe.wait_ge(s_lroot, l + 1)
                for h in range(HEADS):
                    for c in range(2):
                        ins = pe.matmul(bank[6 + h // 2][0:QK, (h % 2) * S:(h % 2 + 1) * S], w_uqs[:, c, h, :],
                                        q_low[:, c, 0:S], start=(c == 0), stop=(c == 1))
                    if h % 2:
                        ins.then_inc(s_up, 1)
                for h in range(HEADS):
                    if h == 0:
                        pe.wait_ge(s_low, l * 3 + 3)
                    if h == 2:
                        pe.wait_ge(s_qe, l * 4 + 2)
                    pe.matmul(bank[h][0:NOPE, :], w_ukv[:, h * P:h * P + NOPE], kv_low[:, :], start=True, stop=True).then_inc(s_up, 1)
                pe.wait_ge(s_qe, l * 4 + 4)
                for t in range(4):
                    ins = pe.matmul(bank[4 + t // 2][:, (t % 2) * S:(t % 2 + 1) * S], kv_low[:, t * P:(t + 1) * P],
                                    w_ukv[:, :].rearrange("p (h m) -> p h m", m=P)[:, :, NOPE:P], start=True, stop=True)
                ins.then_inc(s_up, 1)
                pe.wait_ge(s_gn, l + 1)
                pe.wait_ge(s_rot, l * 2 + 1)
                for g in range(4):
                    ins = pe.matmul(bank[6 + g // 2][:, (g % 2) * S:(g % 2) * S + nt * 64], sgu_wt[:, g, :],
                                    sgu_v[:, 0:nt, g * 64:(g + 1) * 64], start=True, stop=True)
                ins.then_inc(s_mix, 1)

                jobs = attention_jobs(l)
                n_jobs = len(jobs)
                pe.wait_ge(s_ke, l * 4 + 4)
                pe.wait_ge(s_ve, l + 1)
                pe.wait_ge(s_bias, l + 1)
                pe.wait_ge(s_rot, l * 2 + 2)
                pe.wait_ge(s_go, l + 1)
                for i in range(n_jobs + 2):
                    if i < n_jobs:
                        kind, h, t = jobs[i]
                        keys = slice(0, T) if t < 2 else slice(S, T)
                        nk = keys.stop - keys.start
                        if i >= 3:
                            pe.wait_ge(t_ex, l * JOBS + i - 2)
                        if kind == "na":
                            r = slice(64 * (h % 2), 64 * (h % 2) + 64)
                            ins = pe.matmul(bank[i % 3][:, 0:nk], q_na[r, h // 2, t * P:(t + 1) * P], k_na[r, h // 2, keys],
                                            start=True, stop=True)
                            if t < 2:
                                s = 2 - 2 * t
                                ins = pe.matmul(bank[i % 3][:, 0:S], const[:, C_FLIP:C_FLIP + P],
                                                na_bias[:, h, s:s + 4, :].rearrange("p r c -> p (r c)"),
                                                start=False, stop=True, skip_group_check=True)
                        else:
                            ins = pe.matmul(bank[i % 3][:, 0:nk], q_mla[0:QK, h, t * P:(t + 1) * P], k_mla[0:QK, h, keys],
                                            start=True, stop=True)
                        ins.then_inc(t_sc, 1)
                    if 1 <= i <= n_jobs:
                        q = i - 1
                        pe.wait_ge(t_ex, l * JOBS + q + 1)
                        if q >= 2:
                            pe.wait_ge(t_pa if q % 2 == 0 else t_pd, l * (JOBS // 2) + (q - 2) // 2 + 1)
                        for kt in range(4 if jobs[q][2] < 2 else 2):
                            ins = pe.transpose(bank[3 + q % 2][:, kt * P:(kt + 1) * P], prob[q % 3][:, kt * P:(kt + 1) * P], ident)
                        ins.then_inc(t_tr, 1)
                    if i >= 2:
                        q = i - 2
                        kind, h, t = jobs[q]
                        pe.wait_ge(t_pa if q % 2 == 0 else t_pd, l * (JOBS // 2) + q // 2 + 1)
                        if q >= 2:
                            pe.wait_ge(t_o, l * JOBS + q - 1)
                        v = v_na if kind == "na" else v_mla
                        tiles = range(4) if t < 2 else range(2, 4)
                        for n, kt in enumerate(tiles):
                            ins = pe.matmul(bank[5 + q % 2][:, 0:64], prob_t[q % 3][:, n, :], v[:, kt, h * 64:(h + 1) * 64],
                                            start=(n == 0), stop=(n == len(tiles) - 1))
                        ins.then_inc(t_pv, 1)
                pe.wait_ge(s_pool, l + 1)
                pe.wait_ge(t_o, l * JOBS + n_jobs)
                for c in range(KC):
                    if c < 2:
                        ins = pe.matmul(bank[c][:, 0:width], pool_bd[:, c, :], pool_d[:, c, 0:width], start=True, stop=True)
                    else:
                        for t in range(nt):
                            ins = pe.transpose(bank[c][:, t * P:(t + 1) * P], o_tok[:, t, (c - 2) * P:(c - 1) * P], ident)
                    ins.then_inc(m_ps, 1)
                pe.wait_ge(m_lo, l * KC + KC)
                for b in range(N_WOUT):
                    r = N_ADA + N_WIN + b
                    wait_split(l, r)
                    s = split_index(l, r) % HL
                    for c in range(2):
                        for k in range(KC):
                            ins = product(bank[2 * b + c][:, 0:width], w_hi[s][:, k, c * P:(c + 1) * P], w_lo[s][:, k, c * P:(c + 1) * P],
                                          h_hi[:, k, 0:width], h_lo[:, k, 0:width], k == 0, k == KC - 1)
                    ins.then_inc(used, 1)

                norm(2 * l + 1, width)
                pe.wait_ge(s_rw, 2)
                pe.wait_ge(n_lo, (2 * l + 1) * (KC) + KC)
                for t in range(nt):
                    for k in range(KC):
                        ts = slice(t * P, (t + 1) * P)
                        dst = bank[5][:, t * E:(t + 1) * E]
                        pe.matmul(dst, h_hi[:, k, ts], rw_hi[:, k, :], start=(k == 0), stop=False)
                        pe.matmul(dst, h_hi[:, k, ts], rw_lo[:, k, :], start=False, stop=False)
                        ins = pe.matmul(dst, h_lo[:, k, ts], rw_hi[:, k, :], start=False, stop=(k == KC - 1))
                ins.then_inc(r_lg, 1)

                pe.wait_ge(r_sg, l + 1)
                for part, h in enumerate((h_hi, h_lo)):
                    for c in range(KC):
                        if part:
                            pe.wait_ge(q_ta, l * (KC + KC // 2) + c + 1)
                        for t in range(nt):
                            ins = pe.transpose(bank[c][:, t * P:(t + 1) * P], h[:, c, t * P:(t + 1) * P].bitcast(F32), ident)
                        ins.then_inc(q_tok, 1)
                pe.wait_ge(s_const2, 16 * (l + 1))
                pe.wait_ge(s_sel, l + 1)
                pe.wait_ge(q_ta, (l + 1) * (KC + KC // 2))
                pe.wait_ge(q_td, (l + 1) * (KC // 2))
                for t in range(nt + 1):
                    for t2 in range(min(t + 1, nt)):
                        lhs = const2[:, C2_TRI:C2_TRI + P] if t2 == t else ones
                        ins = pe.matmul(bank[5][:, t * E:(t + 1) * E], lhs, sel[:, t2, :], start=(t2 == 0), stop=(t2 == min(t, nt - 1)))
                ins.then_inc(s_pos, 1)

                def one_round(k, l=l, nt=nt):
                    m, s0, n0 = round_start(l, k)

                    def gather(i, part):
                        if part == 0:
                            pe.wait_ge(q_p, i + (m * (E // 2) + 1))
                        for half in range(2):
                            if part == 1:
                                pe.wait_ge(x_hi, 2 * i + (m * E + half + 1))
                            for c in range(4 * half, 4 * half + 4):
                                for t in range(nt):
                                    ins = pe.matmul(bank[c // 2][:, (c % 2) * 2 * SLOTS:(c % 2 + 1) * 2 * SLOTS],
                                                    h_tok[part][:, t, c * P:(c + 1) * P], onehot[:, t, :],
                                                    start=(t == 0), stop=(t == nt - 1))
                            ins.then_inc((g_hi, g_lo)[part], 1)

                    def down(i, j, e):
                        pe.wait_ge(split_lo, nth(2, i, j) + s0)
                        pe.wait_ge(q_tl, 2 * i + (m * E + j + 1))
                        if m or e != 0:
                            pe.wait_ge(q_ya, 2 * i + (m * E + j))
                            pe.wait_ge(q_yd, 2 * i + (m * E + j))
                        wh = w_hi[2][:, :, :].rearrange("p (f k) n -> p f (k n)", f=2)
                        wl = w_lo[2][:, :, :].rearrange("p (f k) n -> p f (k n)", f=2)
                        for n in range(2):
                            for f in range(2):
                                cs = slice(n * 512, (n + 1) * 512)
                                ins = product(bank[6 + n][:, :], ht_hi[j % 2][:, f, :], ht_lo[j % 2][:, f, :],
                                              wh[:, f, cs], wl[:, f, cs], f == 0, f == 1)
                        ins.then_inc(used, 1)

                    def step(i, j, e):
                        even = j % 2 == 0 and (e is None or e < E)
                        if even:
                            gather(i, 0)
                        if e is None or e >= 2:
                            down(i, j - 2, e if e is None else e - 2)
                        if even:
                            gather(i, 1)
                        if e is None or 1 <= e <= E:
                            pe.wait_ge(q_m, 2 * i + (m * E + j))
                            if m or e != 1:
                                pe.wait_ge(q_th, 2 * i + (m * E + j - 1))
                                pe.wait_ge(q_tl, 2 * i + (m * E + j - 1))
                            for f in range(2):
                                ins = pe.transpose(bank[5][:, f * P:(f + 1) * P], hid_m[:, f * P:(f + 1) * P], ident)
                            ins.then_inc(q_t, 1)
                        if e is None or e < E:
                            for role in range(2):
                                pe.wait_ge(split_lo, nth(role, i, j) + s0)
                                if role == 0 and (m or e != 0):
                                    pe.wait_ge(q_m, 2 * i + (m * E + j))
                                for c in range(KC):
                                    if even and role == 0 and c % 4 == 0:
                                        pe.wait_ge(x_hi, 2 * i + (m * E + 2))
                                        pe.wait_ge(x_lo, 2 * i + (m * E + c // 4 + 1))
                                    sl = slice((j % 2) * SLOTS, (j % 2 + 1) * SLOTS)
                                    ins = product(bank[4][:, role * FE:(role + 1) * FE], xg_hi[:, c, sl], xg_lo[:, c, sl],
                                                  w_hi[role][:, c, :], w_lo[role][:, c, :], c == 0, c == KC - 1)
                                ins.then_inc(used, 1)

                    steps(pe, step, 2, m)

                def skip(k, l=l):
                    m, s0, n0 = round_start(l, k)
                    pe.wait_ge(used, s0)
                    pe.sem_inc(used, N_MOE)
                    for sem_ in (g_hi, g_lo, q_t):
                        pe.sem_inc(sem_, E)

                rounds(pe, l, one_round, skip)

            for u in range(len(combine_units(DEPTH - 1))):
                combine(DEPTH - 1, u)
            norm(2 * DEPTH, S)
            for k in range(KC):
                pe.wait_ge(n_h[2 * DEPTH], k + 1)
                for t in range(2):
                    ins = pe.transpose(bank[2 * t + k // 4][:, (k % 4) * P:(k % 4 + 1) * P], nh[:, k % 2, t * P:(t + 1) * P], ident)
                ins.then_inc(f_y, 1)

        @block.vector
        def _(dve):
            made = [0]

            def then(ins):
                made[0] += 1
                ins.then_inc(chain_d, 1)
                dve.wait_ge(chain_d, made[0])

            def split(l, r):
                s, n = split_index(l, r), raw_index(l, r)
                dve.wait_ge(split_hi, s + 1)
                w = block_cols(r)
                dve.tensor_tensor(w_lo[s % HL][:, :, 0:w], raw[n % RAW][:, :, 0:w], w_hi[s % HL][:, :, 0:w].bitcast(F32),
                                  ALU.subtract).then_inc(split_lo, 1)

            def norm(i, width, last):
                n = width // P
                for k in range(1, KC, 2):
                    if k >= 4:
                        dve.wait_ge(n_sum, i * KC + k - 3)
                    dve.tensor_tensor(nsq[:, k % 4, 0:width], x_t[:, k, 0:width], x_t[:, k, 0:width], ALU.mult).then_inc(n_sqd, 1)
                dve.wait_ge(n_root, i + 1)
                dve.reciprocal(rstd[:, 0:n], col[:, 0:n]).then_inc(n_rstd, 1)
                dve.wait_ge(n_bc, i + 1)

                def low(k):
                    dve.wait_ge(n_hi, i * KC + k + 1)
                    dve.tensor_tensor(h_lo[:, k, 0:width], nh[:, k % 2, 0:width], h_hi[:, k, 0:width].bitcast(F32),
                                      ALU.subtract).then_inc(n_lo, 1)
                for k in range(KC):
                    if k >= 2:
                        dve.wait_ge(n_h[i], (k - 1) * (1 if last else width // S))
                    dve.tensor_tensor(nx[:, k % 2, 0:width], x_t[:, k, 0:width], bank[7][:, 0:width], ALU.mult).then_inc(n_x, 1)
                    if k and not last:
                        low(k - 1)
                if not last:
                    low(KC - 1)

            dve.wait_ge(s_vt, 1)
            dve.tensor_copy(vec[:, :], bank[0][:, 0:N_VEC]).then_inc(s_vec, 1)
            dve.wait_ge(s_rw, 1)
            dve.tensor_tensor(rw_lo[:, :, :], rw_in[:, :, :], rw_hi[:, :, :].bitcast(F32), ALU.subtract).then_inc(s_rw, 1)
            def combine(l, u):
                units = combine_units(l)
                n = sum(len(combine_units(i)) for i in range(l))
                if u < len(units) and units[u][1] == 0:
                    t = units[u][0]
                    dve.wait_ge(q_back[t], 32 * sum(2 * streams(i) > t for i in range(l + 1)))
                    then(dve.tensor_scalar(y_back[:, t, 0, :], y_back[:, t, 0, :], pick[:, t, 2:3], None, ALU.mult))
                    dve.scalar_tensor_tensor(y_back[:, t, 0, :], y_back[:, t, 1, :], pick[:, t, 3:4], y_back[:, t, 0, :],
                                             ALU.mult, ALU.add).then_inc(q_c, 1)
                if u >= 1:
                    t, half = units[u - 1]
                    dve.wait_ge(q_ct, n + u)
                    for c in range(4):
                        k = 4 * half + c
                        ins = dve.scalar_tensor_tensor(x_t[:, k, t * P:(t + 1) * P], bank[4 + (u - 1) % 3][:, c * P:(c + 1) * P],
                                                       mod[:, t // 2, 5 * KC + k:5 * KC + k + 1], x_t[:, k, t * P:(t + 1) * P],
                                                       ALU.mult, ALU.add)
                    ins.then_inc(x_moe, 1)

            for l in range(DEPTH):
                ns = streams(l)
                nt, width = 2 * ns, ns * S
                for j in range(N_ADA):
                    if l and 0 <= j - COMBINE_AT <= len(combine_units(l - 1)):
                        combine(l - 1, j - COMBINE_AT)
                    if j % 2:
                        continue
                    dve.wait_ge(ada_mm, l * N_ADA + j + 1)
                    if j >= 2 or l:
                        dve.wait_ge(ada_tr, l * N_ADA + j - 1)
                    dve.tensor_copy(mod_row[:, 0, :], bank[j % 4][0:2, 0:BW]).then_inc(ada_ed, 1)
                    if l == 0 and 4 <= j < 12:
                        k = j - 4
                        dve.wait_ge(s_xt, k + 1)
                        dve.tensor_copy(x_t[:, k, :], bank[4 + k % 3][:, :]).then_inc(s_xevd, 1)
                if l:
                    dve.wait_ge(x_moe, sum(len(combine_units(n)) for n in range(l)))
                dve.wait_ge(ada_tr, (l + 1) * N_ADA)
                for s in range(2):
                    ins = dve.tensor_tensor(mod[:, s, :], bank[7][:, s:96:2], vec[:, V_ADAB + 48 * l:V_ADAB + 48 * (l + 1)], ALU.add)
                then(ins)
                for which, v in enumerate((V_N1, V_N2)):
                    for s in range(2):
                        m = 24 * which + KC
                        ins = dve.scalar_tensor_tensor(amp[:, which, s, :], mod[:, s, m:m + KC], 1.0, vec[:, v + KC * l:v + KC * (l + 1)],
                                                       ALU.add, ALU.mult)
                if l == 0:
                    dve.wait_ge(s_xev, 4)
                ins.then_inc(s_amp, 1)
                for r in range(N_ADA, N_ADA + HL):
                    split(l, r)
                if l == 0:
                    dve.wait_ge(s_const, 16)
                norm(2 * l, T, False)
                for b in range(N_WIN):
                    if b in (0, 2, 3, 6, 7):
                        dve.wait_ge(used, done(l, N_ADA + b))
                    b0 = 2 * (b % 4)
                    if b == 0:
                        for c in range(2):
                            ins = dve.tensor_copy(a_pad[:, c, 0:ns, PAD:PAD + S], bank[c][:, 0:width].rearrange("p (s t) -> p s t", s=ns))
                        ins.then_inc(proj_ed, 1)
                    if b in (2, 6):
                        dst, w = (k_na, T) if b == 2 else (q_low, width)
                        for c in range(2):
                            ins = dve.tensor_copy(dst[:, c, 0:w], bank[b0 + c][:, 0:w])
                        ins.then_inc(proj_ed, 1)
                    if b == 3:
                        for c in range(2):
                            ins = dve.tensor_copy(v_na[:, 2 * c:2 * c + 2, :].rearrange("p t n -> p (t n)"), bank[6 + c][:, :])
                        ins.then_inc(proj_ed, 1)
                    if b == 7:
                        rr = slice(NOPE, QK)
                        dve.tensor_copy(k_rope[rr, :], bank[7][rr, :])
                        then(dve.tensor_tensor(rope_t[rr, 0, :], bank[0][rr, 0:S], const[rr, C_SIN:C_SIN + S], ALU.mult))
                        ins = dve.tensor_tensor(k_rope[rr, 0:S], k_rope[rr, 0:S], const[rr, C_COS:C_COS + S], ALU.mult)
                        ins.then_inc(proj_ed, 1)
                        dve.wait_ge(proj_ed, l * 5 + 5)
                        then(dve.tensor_tensor(k_rope[rr, 0:S], k_rope[rr, 0:S], rope_t[rr, 0, :], ALU.add))
                        dve.tensor_copy(k_mla[rr, :, :], k_rope[rr, :][:, None, :].to_broadcast([ROPE, HEADS, T]))
                    if b + HL < N_WIN:
                        split(l, N_ADA + b + HL)
                n = 4 * nt
                dve.wait_ge(proj_ea, l * 4 + 3)
                vv = sgu_v[:, 0:nt, :].rearrange("p t (g c) -> p (t g) c", c=64)
                sq = sgu_sq[:, 0:nt, :].rearrange("p t (g c) -> p (t g) c", c=64)
                then(dve.tensor_tensor(sq, vv, vv, ALU.mult))
                dve.tensor_reduce(col[:, 16:16 + n], sq, AX.X, ALU.add).then_inc(s_gv, 1)
                dve.wait_ge(s_lroot, l + 1)
                dve.reciprocal(col[:, 48:48 + nt], col[:, 8:8 + nt])
                dve.reciprocal(col[:, 52:56], col[:, 12:16]).then_inc(s_lrstd, 1)
                dve.wait_ge(s_groot, l + 1)
                then(dve.reciprocal(col[:, 16:16 + n], col[:, 32:32 + n]))
                dve.wait_ge(s_lbc, l + 1)
                for c in range(2):
                    dve.tensor_tensor(q_low[:, c, 0:width], q_low[:, c, 0:width], bank[0][:, 0:width], ALU.mult).then_inc(s_low, 1)
                dve.wait_ge(proj_ea, l * 4 + 4)
                dve.tensor_tensor(kv_low[:, :], kv_low[:, :], bank[1][:, :], ALU.mult).then_inc(s_low, 1)
                then(dve.tensor_tensor(vv, vv, col[:, 16:16 + n][:, :, None].to_broadcast([P, n, 64]), ALU.mult))
                dve.tensor_tensor(sgu_v[:, 0:nt, :], sgu_v[:, 0:nt, :], sgu_g[:, :][:, None, :].to_broadcast([P, nt, S]),
                                  ALU.mult).then_inc(s_gn, 1)
                rr = slice(NOPE, QK)
                dve.wait_ge(s_up, l * 11 + 6)
                for h2 in range(2):
                    ins = dve.scalar_tensor_tensor(rope_t[rr, 2 * h2:2 * h2 + 2, :], bank[6 + h2][rr, :].rearrange("p (h t) -> p h t", h=2),
                                                   MLA_SCALE, const[rr, C_SIN:C_SIN + S][:, None, :].to_broadcast([ROPE, 2, S]),
                                                   ALU.mult, ALU.mult)
                ins.then_inc(s_rot, 1)
                dve.wait_ge(s_qe, l * 4 + 4)
                dve.wait_ge(s_rot, l * 2 + 1)
                then(dve.tensor_tensor(q_mla[rr, :, 0:S], q_mla[rr, :, 0:S], const[rr, C_COS:C_COS + S][:, None, :].to_broadcast([ROPE, HEADS, S]), ALU.mult))
                dve.tensor_tensor(q_mla[rr, :, 0:S], q_mla[rr, :, 0:S], rope_t[rr, :, :], ALU.add).then_inc(s_rot, 1)
                dve.wait_ge(s_mix, l + 1)
                for g in range(4):
                    v0 = V_SB + 4 * l + g
                    ins = dve.scalar_tensor_tensor(o_tok[:, 0:nt, S + g * 64:S + (g + 1) * 64],
                                                   bank[6 + g // 2][:, (g % 2) * S:(g % 2) * S + nt * 64].rearrange("p (t c) -> p t c", c=64),
                                                   vec[:, v0:v0 + 1], sgu_u[:, 0:nt, g * 64:(g + 1) * 64], ALU.add, ALU.mult)
                ins.then_inc(s_go, 1)
                jobs = attention_jobs(l)
                for i in range(len(jobs) + 2):
                    if i < len(jobs):
                        nk = T if jobs[i][2] < 2 else S
                        dve.wait_ge(t_sc, l * JOBS + i + 1)
                        dve.tensor_reduce(stat[:, i % 4, 0:1], bank[i % 3][:, 0:nk], AX.X, ALU.max, negate=True).then_inc(t_mx, 1)
                    if 1 <= i <= len(jobs) and i % 2 == 0:
                        q = i - 1
                        nkt = 4 if jobs[q][2] < 2 else 2
                        dve.wait_ge(t_tr, l * JOBS + q + 1)
                        if q >= 3:
                            dve.wait_ge(t_pv, l * JOBS + q - 2)
                        dve.tensor_copy(prob_t[q % 3][:, 0:nkt, :].rearrange("p k n -> p (k n)"), bank[3 + q % 2][:, 0:nkt * P]).then_inc(t_pd, 1)
                    if i >= 2:
                        q = i - 2
                        kind, h, t = jobs[q]
                        dve.wait_ge(t_pv, l * JOBS + q + 1)
                        then(dve.reciprocal(stat[:, q % 4, 2:3], stat[:, q % 4, 1:2]))
                        c0 = (0 if kind == "na" else 2 * S) + h * 64
                        dve.tensor_scalar(o_tok[:, t, c0:c0 + 64], bank[5 + q % 2][:, 0:64], stat[:, q % 4, 2:3], None, ALU.mult).then_inc(t_o, 1)
                for c in range(KC):
                    dve.wait_ge(m_hi, l * KC + c + 1)
                    hi = h_hi[:, c, 0:width].bitcast(F32)
                    if c < 2:
                        v0 = V_PS + 2 * l + c
                        dve.scalar_tensor_tensor(h_lo[:, c, 0:width], bank[c][:, 0:width], vec[:, v0:v0 + 1], hi, ALU.mult, ALU.subtract).then_inc(m_lo, 1)
                    else:
                        dve.tensor_tensor(h_lo[:, c, 0:width], bank[c][:, 0:width], hi, ALU.subtract).then_inc(m_lo, 1)

                def add_gated(dc, src, gate, signal):
                    for s in range(ns):
                        sl = slice(s * S, (s + 1) * S)
                        ins = dve.scalar_tensor_tensor(x_t[:, dc, sl], src[:, sl], mod[:, s, gate * KC + dc:gate * KC + dc + 1], x_t[:, dc, sl],
                                                       ALU.mult, ALU.add)
                    ins.then_inc(signal, 1)

                for b in range(N_WOUT):
                    split(l, N_ADA + N_WIN + b)
                    if b >= 1:
                        dve.wait_ge(used, done(l, N_ADA + N_WIN + b - 1))
                        for c in range(2):
                            add_gated(2 * (b - 1) + c, bank[2 * (b - 1) + c], 2, o_ev)
                dve.wait_ge(used, done(l, N_ADA + N_WIN + 3))
                for c in range(2):
                    add_gated(6 + c, bank[6 + c], 2, o_ev)
                dve.wait_ge(o_ev, l * KC + KC)
                norm(2 * l + 1, width, False)

                dve.wait_ge(r_sg, l + 1)
                sc = score[:, 0:nt, :]
                bi, rk, cm = biased[:, 0:nt, :], rank[:, 0:nt, :], cmp[:, 0:nt, :]
                then(dve.tensor_tensor(bi, sc, rb_row[:, :][:, None, :].to_broadcast([P, nt, E]), ALU.add))

                def rank_of_four(values, ranks, scratch):
                    then(dve.tensor_copy(ranks, const[:, C_RANK:C_RANK + ranks.shape[1] * 4].rearrange("p (n f) -> p n f", f=4)))
                    for d in range(1, 4):
                        then(dve.tensor_tensor(scratch[:, :, 0:4 - d], values[:, :, 0:4 - d], values[:, :, d:4], ALU.is_ge))
                        then(dve.tensor_tensor(ranks[:, :, d:4], ranks[:, :, d:4], scratch[:, :, 0:4 - d], ALU.add))
                        then(dve.tensor_tensor(ranks[:, :, 0:4 - d], ranks[:, :, 0:4 - d], scratch[:, :, 0:4 - d], ALU.subtract))

                four = lambda ap: ap.rearrange("p t (g f) -> p (t g) f", f=4)
                rank_of_four(four(bi), four(rk), four(cm))
                then(dve.tensor_scalar(rk, rk, 1.5, None, ALU.is_lt))
                then(dve.tensor_tensor(cm, rk, bi, ALU.mult))
                g2 = grp[:, 0:nt, :]
                then(dve.tensor_reduce(g2.rearrange("p t g -> p (t g)"), four(cm), AX.X, ALU.add))
                gr = grank[:, 0:nt, :]
                rank_of_four(g2, gr, cmp[:, 0:nt, 0:4])
                then(dve.tensor_scalar(gr, gr, 0.5, None, ALU.is_lt))
                se, sl, ro, ga = sel[:, 0:nt, :], slot[:, 0:nt, :], row[:, 0:nt, :], gates[:, 0:nt, :]
                dve.tensor_tensor(four(se), four(rk), gr.rearrange("p t g -> p (t g)")[:, :, None].to_broadcast([P, 4 * nt, 4]),
                                  ALU.mult).then_inc(s_sel, 1)
                dve.wait_ge(s_sel, l + 1)
                then(dve.tensor_tensor(rk, se, sc, ALU.mult))
                then(dve.tensor_reduce(grp[:, 0:nt, 0], rk, AX.X, ALU.add))
                then(dve.reciprocal(grp[:, 0:nt, 1], grp[:, 0:nt, 0]))
                then(dve.tensor_tensor(ga, rk, grp[:, 0:nt, 1:2].to_broadcast([P, nt, E]), ALU.mult))

                def split_expert(l, k, role, i, j):
                    m, s0, n0 = round_start(l, k)
                    q, _ = raw_place(role, i, j)
                    dve.wait_ge(split_hi, nth(role, i, j) + s0)
                    dve.tensor_tensor(w_lo[role][:, :, :], raw[q][:, :, :], w_hi[role][:, :, :].bitcast(F32), ALU.subtract).then_inc(split_lo, 1)

                split_expert(l, 0, 0, 0, 0)
                dve.wait_ge(q_tok, (l + 1) * (2 * KC))
                for c in range(KC // 2, KC):
                    dve.tensor_copy(h_tok[1][:, 0:nt, c * P:(c + 1) * P], bank[c][:, 0:width].rearrange("p (t d) -> p t d", d=P)).then_inc(q_td, 1)
                dve.wait_ge(s_pos, l + 1)
                pos = bank[5][:, 0:nt * E].rearrange("p (t e) -> p t e", e=E)
                then(dve.scalar_tensor_tensor(sl, pos, 1.0, se, ALU.add, ALU.mult))
                then(dve.tensor_scalar(sl, sl, -1.0, None, ALU.add))

                def one_hot(l, k, i, pair):
                    lo = C2_IOTA + k * SLOTS
                    for j in range(2):
                        ins = dve.tensor_tensor(onehot[:, 0:nt, j * SLOTS:(j + 1) * SLOTS],
                                                const2[:, lo:lo + SLOTS][:, None, :].to_broadcast([P, nt, SLOTS]),
                                                slot[:, 0:nt, bass.ds(2 * i + (2 * pair + j), 1)].to_broadcast([P, nt, SLOTS]), ALU.is_equal)
                    ins.then_inc(q_p, 1)

                one_hot(l, 0, 0, 0)
                split_expert(l, 0, 1, 0, 0)
                then(dve.tensor_reduce(col[:, 60:61], bank[5][:, nt * E:(nt + 1) * E], AX.X, ALU.max))
                for k in range(1, ROUNDS[l]):
                    ins = dve.tensor_scalar(col[:, 60 + k:61 + k], col[:, 60:61], k * SLOTS + 0.5, None, ALU.is_gt)
                then(ins)
                dve.tensor_copy(more[:, 0:ROUNDS[l] - 1], col[:, 61:60 + ROUNDS[l]]).then_inc(s_more, 1)
                then(dve.tensor_tensor(cm, pos, const2[:, C2_EBASE:C2_EBASE + E][:, None, :].to_broadcast([P, nt, E]), ALU.add))
                for k in range(1, ROUNDS[l]):
                    then(dve.tensor_scalar(ro, pos, k * SLOTS - 0.5, float(E * SLOTS - SLOTS), ALU.is_gt, ALU.mult))
                    then(dve.tensor_tensor(cm, cm, ro, ALU.add))
                then(dve.tensor_tensor(ro, cm, se, ALU.mult))
                first, second = pick[:, 0:nt, 0:1], pick[:, 0:nt, 1:2]
                dve.tensor_reduce(pick[:, 0:nt, 0], ro, AX.X, ALU.max)
                then(dve.tensor_reduce(pick[:, 0:nt, 1], ro, AX.X, ALU.add))
                then(dve.tensor_tensor(second, second, first, ALU.subtract))
                for n in range(2):
                    then(dve.tensor_tensor(cm, ro, pick[:, 0:nt, n:n + 1].to_broadcast([P, nt, E]), ALU.is_equal))
                    then(dve.tensor_tensor(cm, cm, ga, ALU.mult))
                    then(dve.tensor_reduce(pick[:, 0:nt, 2 + n], cm, AX.X, ALU.add))
                then(dve.tensor_scalar(pick0[:, 0:nt, :], pick[:, 0:nt, 0:2], -1.0, None, ALU.add))
                dve.tensor_copy(pick_row[:, 0:nt, :], pick0[:, 0:nt, :]).then_inc(q_row, 1)

                def one_round(k, l=l):
                    m, s0, n0 = round_start(l, k)

                    def step(i, j, e):
                        if (e is None or e < E - 1) and j % 2:
                            one_hot(l, k, i, 1)
                        if e is None or e >= 2:
                            par, i2 = j % 2, i + (j - 2) // 2
                            dve.wait_ge(used, nth(2, i, j - 2) + s0)
                            dve.wait_ge(q_out[par], i2 * 16 + 16 * (E // 2) * m)
                            dve.tensor_copy(y_sb[par][:, 512:1024], bank[7][:, :]).then_inc(q_yd, 1)
                        if (e is None or e < E) and j % 2 == 0:
                            for half in range(2):
                                dve.wait_ge(g_lo, 2 * i + (m * E + half + 1))
                                for b in range(2):
                                    ins = dve.tensor_copy(xg_lo[:, 4 * half + 2 * b:4 * half + 2 * b + 2, :].rearrange("p k n -> p (k n)"),
                                                          bank[2 * half + b][:, :])
                                ins.then_inc(x_lo, 1)
                        if e is None or 1 <= e <= E:
                            dve.wait_ge(q_th, 2 * i + (m * E + j))
                            p = (j - 1) % 2
                            dve.tensor_tensor(ht_lo[p][:, :, :].rearrange("p f n -> p (f n)"), bank[5][:, 0:2 * SLOTS],
                                              ht_hi[p][:, :, :].rearrange("p f n -> p (f n)").bitcast(F32), ALU.subtract).then_inc(q_tl, 1)
                            split_expert(l, k, 2, i, j - 1)
                        if e is None or e < E - 1:
                            split_expert(l, k, 0, i, j + 1)
                        if e is None or e < E:
                            dve.wait_ge(q_s, 2 * i + (m * E + j + 1))
                            dve.wait_ge(q_t, 2 * i + (m * E + j))
                            dve.tensor_tensor(hid_m[:, :], bank[4][:, FE:2 * FE], hid_g[:, :], ALU.mult).then_inc(q_m, 1)
                        if e is None or e < E - 1:
                            split_expert(l, k, 1, i, j + 1)

                    if k:
                        dve.wait_ge(g_lo, m * E)
                        one_hot(l, k, 0, 0)
                        split_expert(l, k, 0, 0, 0)
                        split_expert(l, k, 1, 0, 0)
                    steps(dve, step, 2, m)

                def skip(k, l=l):
                    m, s0, n0 = round_start(l, k)
                    dve.wait_ge(split_lo, s0)
                    dve.wait_ge(q_yd, m * E)
                    dve.sem_inc(split_lo, N_MOE)
                    dve.sem_inc(q_p, E // 2)
                    for sem_ in (x_lo, q_m, q_tl, q_yd):
                        dve.sem_inc(sem_, E)

                rounds(dve, l, one_round, skip)
            for u in range(len(combine_units(DEPTH - 1)) + 1):
                combine(DEPTH - 1, u)
            dve.wait_ge(x_moe, sum(len(combine_units(n)) for n in range(DEPTH)))
            norm(2 * DEPTH, S, True)
            for t in range(2):
                dve.wait_ge(f_y, KC)
                dve.tensor_copy(y_tok[:, t, 0:512], bank[2 * t][:, :]).then_inc(f_ev, 1)


def kernel(**inputs):
    import numpy as _np
    import concourse.bacc as _bacc
    from concourse import mybir as _mybir
    from concourse.bass_utils import run_bass_kernel_spmd as _run

    g = {k: _np.ascontiguousarray(v) for k, v in inputs.items()}
    arrays = {n: g[n] for n in ("ada_w", "w_in", "w_out", "pool_w", "mla_w_uq", "mla_w_ukv", "sgu_norm_g", "sgu_w", "router_w",
                                "router_b", "moe_w_gate", "moe_w_up", "moe_w_down")}
    arrays["x"], arrays["ctx"] = g["x"][0], g["ctx"][0]
    arrays["vec0"] = _np.concatenate([g[n].reshape(-1, P) for n in ("ada_b", "c", "c_ctx")])
    arrays["vec1"] = _np.concatenate([g[n].reshape(-1, P) for n in (
        "norm1_g", "norm2_g", "final_g", "pool_s", "mla_q_norm_g", "mla_kv_norm_g", "sgu_b")])
    rpb = _np.zeros((DEPTH, 2, HEADS, 6, P), _np.float32)
    for half in range(2):
        rpb[:, half, :, :, 48:79] = g["na_rpb"][:, :, 5 - half:11 - half]
    arrays["na_rpb"] = rpb
    arrays["const"] = constants()
    arrays["const2"] = router_constants()
    nc = _bacc.Bacc("TRN2", target_bir_lowering=False, num_devices=1)
    aps = {}
    for n, v in arrays.items():
        aps[n] = nc.dram_tensor(f"in_{n}", v.shape, _mybir.dt.from_np(v.dtype), kind="ExternalInput").ap()
    out = nc.dram_tensor("out_0", (S, D), F32, kind="ExternalOutput").ap()
    build(nc, aps, out)
    r = _run(nc, [{f"in_{n}": v for n, v in arrays.items()}], core_ids=[0])
    return r.results[0]["out_0"].reshape(1, S, D)
```

```python
from contextlib import ExitStack

import numpy as np

import concourse.bass as bass
from concourse import mybir

F32 = mybir.dt.float32
F32R = mybir.dt.float32r
ALU = mybir.AluOpType
ACT = mybir.ActivationFunctionType
AX = mybir.AxisListType

P = 128
D = 1024
KC = D // P
S = 256
T = 2 * S
DEPTH = 2
GRID = 64
ROWS = S // GRID
IN_W = 1952
HEADS = 4
E = 16
FE = 256
SLOTS = P
WIN_COLS = 16
NOPE, ROPE = 64, 32
QK = NOPE + ROPE
MLA_SCALE = float(QK) ** -0.5
NA_SCALE = 64.0 ** -0.5
EPS = 1e-6
NEG = -1e30
PAD = 8
PW = S + 2 * PAD

BW = 256
N_ADA, N_WIN, N_WOUT = 24, 8, 4
N_MOE = 3 * E
PER_LAYER = N_ADA + N_WIN + N_WOUT + N_MOE
SPLIT_PER_LAYER = PER_LAYER - N_ADA
ROUNDS = [T // SLOTS if l < DEPTH - 1 else S // SLOTS for l in range(DEPTH)]
RAW = 6
HL = 3

C_ID, C_FLIP, C_ONE, C_NEGM, C_INV, C_COS, C_SIN, C_RANK, C_EPS = np.cumsum(
    [0, P, P, P, GRID, 2 * S, S, S, 64]).tolist()
N_CONST = C_EPS + 2
V_ADAB, V_C = 0, DEPTH * 48
V_N1 = V_C + 16
V_N2 = V_N1 + DEPTH * KC
V_FIN = V_N2 + DEPTH * KC
V_PS = V_FIN + KC
V_QG = V_PS + 2 * DEPTH
V_KVG = V_QG + 2 * DEPTH
V_SB = V_KVG + DEPTH
N_VEC = V_SB + 4 * DEPTH


C2_TRI, C2_EBASE = 0, P
C2_IOTA = C2_EBASE + E
N_CONST2 = C2_IOTA + T


def router_constants():
    c = np.zeros((P, N_CONST2), np.float32)
    c[:, C2_TRI:C2_TRI + P] = np.triu(np.ones((P, P)), 1)
    c[:, C2_EBASE:C2_EBASE + E] = SLOTS * np.arange(E) + 1
    c[:, C2_IOTA:C2_IOTA + T] = np.arange(T)
    return c


def constants():
    c = np.zeros((P, N_CONST), np.float32)
    c[:, C_ID:C_ID + P] = np.eye(P)
    for p in range(P):
        c[p, C_FLIP + (p // GRID) * GRID + GRID - 1 - p % GRID] = 1
    c[:, C_ONE:C_ONE + P] = 1
    for p in range(P):
        qc = GRID - 1 - p % GRID
        ws = min(max(qc - WIN_COLS // 2, 0), GRID - WIN_COLS)
        kc = np.arange(GRID)
        c[p, C_NEGM:C_NEGM + GRID] = np.where((kc >= ws) & (kc < ws + WIN_COLS), 0, NEG)
    t = np.arange(S)
    for g, w in enumerate((2, 4, 8, 16)):
        n = np.clip(t - w // 2 + w, 0, S) - np.clip(t - w // 2, 0, S)
        half, ch = g % 2, g // 2
        c[half * 64:half * 64 + 64, C_INV + ch * S:C_INV + (ch + 1) * S] = (1.0 / n.astype(np.float64)).astype(np.float32)
    nf = ROPE // 4
    inv = (np.float32(10000.0) ** (-np.arange(nf, dtype=np.float32) / np.float32(nf))).astype(np.float32)
    ang = np.concatenate([(t // GRID).astype(np.float32)[:, None] * inv, (t % GRID).astype(np.float32)[:, None] * inv], 1)
    cos, sin = np.cos(ang).T, np.sin(ang).T
    for part in range(2):
        for half in range(2):
            r = NOPE + part * 2 * nf + half * nf
            c[r:r + nf, C_COS:C_COS + S] = cos[part * nf:(part + 1) * nf]
            c[r:r + nf, C_SIN:C_SIN + S] = sin[part * nf:(part + 1) * nf] * (-1 if half == 0 else 1)
    c[:, C_RANK:C_RANK + 64] = np.tile(np.array([3, 2, 1, 0], np.float32), 16)
    c[:, C_EPS] = EPS
    return c


def build(nc, a, out):
    with ExitStack() as ctx:
        def sem(name):
            return ctx.enter_context(nc.semaphore(name))

        at = [16512]

        def sb(name, shape, dt=F32, offset=None):
            size = int(np.prod(shape[1:])) * 4
            if offset is None:
                offset = at[0]
                at[0] += (size + 31) // 32 * 32
            return nc.alloc_sbuf_tensor_at(name, shape, dt, offset=offset)

        class Region:

            def __init__(self, base, size):
                self.at, self.end = base, base + size

            def sb(self, name, shape, dt=F32):
                size = (int(np.prod(shape[1:])) * 4 + 31) // 32 * 32
                t = nc.alloc_sbuf_tensor_at(name, shape, dt, offset=self.at)
                self.at += size
                assert self.at <= self.end, name
                return t

        const = sb("const", [P, N_CONST])
        vec = sb("vec", [P, N_VEC])
        x_t = sb("x_t", [P, KC, T])
        raw = [sb(f"raw{i}", [P, KC, BW]) for i in range(RAW)]
        ring_at = at[0]
        w_hi = [sb(f"w_hi{i}", [P, KC, BW], F32R) for i in range(HL)]
        w_lo = [sb(f"w_lo{i}", [P, KC, BW], F32R) for i in range(HL)]
        ring_size = at[0] - ring_at
        h_at = at[0]
        h_hi = sb("h_hi", [P, KC, T], F32R)
        h_lo = sb("h_lo", [P, KC, T], F32R)
        h_size = at[0] - h_at
        small_at = at[0]
        pool_bd = sb("pool_bd", [P, 2, P])
        w_uq = sb("w_uq", [P, 2, HEADS * QK])
        w_uqs = sb("w_uqs", [P, 2, HEADS, QK])
        w_ukv = sb("w_ukv", [P, 4 * P])
        sgu_w = sb("sgu_w", [P, 4, P])
        sgu_wt = sb("sgu_wt", [P, 4, P])
        na_bias = sb("na_bias", [P, HEADS, 6, GRID])
        sgu_g = sb("sgu_g", [P, S])
        G = Region(small_at, at[0] - small_at)
        xg_hi = G.sb("xg_hi", [P, KC, 2 * SLOTS], F32R)
        xg_lo = G.sb("xg_lo", [P, KC, 2 * SLOTS], F32R)
        rb_row = sb("rb_row", [P, E])
        rw_hi = sb("rw_hi", [P, KC, E], F32R)
        rw_lo = sb("rw_lo", [P, KC, E], F32R)
        c_act = sb("c_act", [P, 16])
        mod_of = [sb(f"mod{l}", [P, 2, 48]) for l in range(DEPTH)]
        amp = sb("amp", [P, 2, 2, KC])
        col = sb("col", [P, 64])
        rstd = sb("rstd", [P, 4])
        stat = sb("stat", [P, 4, 3])
        gates = sb("gates", [P, 4, E])
        pick_row = sb("pick_row", [P, 4, 2], mybir.dt.uint32)
        more = sb("more", [P, 4], mybir.dt.int32)
        area_at = at[0]
        area_size = 33024
        at[0] += area_size
        assert at[0] <= 229344, at[0]

        A = Region(area_at, area_size)
        a_pad = A.sb("a_pad", [P, 2, 2, PW])
        q_na = A.sb("q_na", [P, 2, T])
        k_na = A.sb("k_na", [P, 2, T])
        v_na = A.sb("v_na", [P, 4, S])
        sgu_u = A.sb("sgu_u", [P, 4, S])
        sgu_v = A.sb("sgu_v", [P, 4, S])
        q_low = A.sb("q_low", [P, 2, T])
        kv_low = A.sb("kv_low", [P, T])
        k_rope = A.sb("k_rope", [P, T])
        N = Region(area_at, area_size)
        nsq = N.sb("nsq", [P, 4, T])
        nsq_t = nc.alloc_sbuf_tensor_at("nsq_t", [P, 2, KC, P], F32, offset=area_at)
        nx = N.sb("nx", [P, 2, T])
        nh = N.sb("nh", [P, 2, T])
        I = Region(area_at + 4096, area_size - 4096)
        x_tok = [I.sb(f"x_tok{t}", [P, D]) for t in range(4)]
        M = Region(area_at, area_size)
        y_sb = [M.sb(f"y_sb{i}", [P, D]) for i in range(2)]
        onehot = M.sb("onehot", [P, 4, 2 * SLOTS], F32R)
        hid_g = M.sb("hid_g", [P, FE])
        hid_m = M.sb("hid_m", [P, FE])
        M.at = area_at + 16384
        const2 = M.sb("const2", [P, N_CONST2])
        score = M.sb("score", [P, 4, E])
        biased = M.sb("biased", [P, 4, E])
        rank = M.sb("rank", [P, 4, E])
        cmp = M.sb("cmp", [P, 4, E])
        grp = M.sb("grp", [P, 4, 4])
        grank = M.sb("grank", [P, 4, 4])
        sel = M.sb("sel", [P, 4, E])
        slot = M.sb("slot", [P, 4, E])
        row = M.sb("row", [P, 4, E])
        pick = M.sb("pick", [P, 4, 4])
        pick0 = M.sb("pick0", [P, 4, 2])
        ht_hi = [M.sb(f"ht_hi{i}", [P, 2, SLOTS], F32R) for i in range(2)]
        ht_lo = [M.sb(f"ht_lo{i}", [P, 2, SLOTS], F32R) for i in range(2)]
        logit_t = M.sb("logit_t", [P, T])
        placed = M.sb("placed", [P, 5, E])
        assert M.at <= area_at + area_size - 16 * BW
        mod_row = nc.alloc_sbuf_tensor_at("mod_row", [2, 2, 2 * BW], F32, offset=area_at + area_size - 16 * BW)
        h_tok = [nc.alloc_sbuf_tensor_at(f"h_tok{i}", [P, 4, D], F32R, offset=h_at + 4 * KC * T * i) for i in range(2)]
        y_back = nc.alloc_sbuf_tensor_at("y_back", [P, 4, 2, D], F32, offset=h_at)
        y_rows = nc.dram_tensor("y_rows", (T // SLOTS * E * SLOTS, D), F32, kind="Internal").ap()
        B = Region(ring_at, ring_size)
        o_tok = B.sb("o_tok", [P, 4, 3 * S])
        v_mla = B.sb("v_mla", [P, 4, S])
        pool_d = B.sb("pool_d", [P, 2, T])
        prob = [B.sb(f"prob{i}", [P, T]) for i in range(3)]
        prob_t = [B.sb(f"prob_t{i}", [P, 4, P]) for i in range(3)]
        sgu_sq = B.sb("sgu_sq", [P, 4, S])
        win_a = B.sb("win_a", [P, 2, 2, PW])
        win_b = B.sb("win_b", [P, 2, 2, PW])
        H = Region(h_at, h_size)
        q_mla = H.sb("q_mla", [P, HEADS, T])
        k_mla = H.sb("k_mla", [P, HEADS, T])
        low_sq = H.sb("low_sq", [P, 3, T])
        rope_t = H.sb("rope_t", [P, HEADS, S])
        raw_vec = [nc.alloc_sbuf_tensor_at(f"raw_vec{i}", [P, P], F32, offset=area_at + i * 512) for i in range(2)]
        rw_in = nc.alloc_sbuf_tensor_at("rw_in", [P, KC, E], F32, offset=area_at + 1024)

        y_tok = nc.alloc_sbuf_tensor_at("y_tok", [P, 2, D], F32, offset=ring_at)

        ident = const[:, C_ID:C_ID + P]
        ones = const[:, C_ONE:C_ONE + P]
        eps = const[:, C_EPS:C_EPS + 1]

        bank = [ctx.enter_context(nc.psum_tensor(f"bank{i}", [P, 512], F32)) for i in range(8)]

        loaded = [sem(f"loaded{i}") for i in range(RAW)]
        s_ident = sem("s_ident")
        s_const, s_vecin, s_xin, s_xevd = sem("s_const"), sem("s_vecin"), sem("s_xin"), sem("s_xevd")
        s_bcast = sem("s_bcast")
        s_small, s_zero = sem("s_small"), sem("s_zero")
        s_vt, s_vec, s_cact = sem("s_vt"), sem("s_vec"), sem("s_cact")
        s_xt, s_xev = sem("s_xt"), sem("s_xev")
        s_rw = sem("s_rw")
        split_hi, split_lo, used = sem("split_hi"), sem("split_lo"), sem("used")
        ada_mm, m_row, m_turn, s_mod = sem("ada_mm"), sem("m_row"), sem("m_turn"), sem("s_mod")
        n_sqa, n_sqd, n_sum, n_root, n_rstd, n_bc, n_x, n_hi, n_lo = (sem(n) for n in (
            "n_sqa", "n_sqd", "n_sum", "n_root", "n_rstd", "n_bc", "n_x", "n_hi", "n_lo"))
        n_sqc, n_suc, n_sqt, n_sut = sem("n_sqc"), sem("n_suc"), sem("n_sqt"), sem("n_sut")
        n_h = [sem(f"n_h{i}") for i in range(2 * DEPTH + 1)]
        chain_d, chain_p = sem("chain_d"), sem("chain_p")
        s_swap, s_pads, s_wg, s_bias, s_pool = (sem(n) for n in ("s_swap", "s_pads", "s_wg", "s_bias", "s_pool"))
        proj_ea, proj_ed = sem("proj_ea"), sem("proj_ed")
        s_wt, s_wte = sem("s_wt"), sem("s_wte")
        s_lsq, s_lsum, s_lroot, s_lrstd, s_lbc, s_low = (sem(n) for n in (
            "s_lsq", "s_lsum", "s_lroot", "s_lrstd", "s_lbc", "s_low"))
        s_up, s_qe, s_ke, s_ve, s_rot = (sem(n) for n in ("s_up", "s_qe", "s_ke", "s_ve", "s_rot"))
        s_gv, s_groot, s_gn, s_mix, s_go = (sem(n) for n in ("s_gv", "s_groot", "s_gn", "s_mix", "s_go"))
        t_sc, t_mx, t_ex, t_tr, t_pa, t_pd, t_pv, t_o = (sem(n) for n in (
            "t_sc", "t_mx", "t_ex", "t_tr", "t_pa", "t_pd", "t_pv", "t_o"))
        m_ps, m_hi, m_lo, o_ev = sem("m_ps"), sem("m_hi"), sem("m_lo"), sem("o_ev")
        r_lt, r_le, r_lg, r_sg, s_placed = sem("r_lt"), sem("r_le"), sem("r_lg"), sem("r_sg"), sem("s_placed")
        s_const2, s_sel, s_pos, s_more, q_tok, q_ta, q_td = (sem(n) for n in (
            "s_const2", "s_sel", "s_pos", "s_more", "q_tok", "q_ta", "q_td"))
        q_p, g_hi, g_lo, x_hi, x_lo, q_s, q_m, q_t, q_th, q_tl, q_ya, q_yd = (sem(n) for n in (
            "q_p", "g_hi", "g_lo", "x_hi", "x_lo", "q_s", "q_m", "q_t", "q_th", "q_tl", "q_ya", "q_yd"))
        q_out = [sem("q_out_even"), sem("q_out_odd")]
        q_row, q_c, q_ct, x_moe = sem("q_row"), sem("q_c"), sem("q_ct"), sem("x_moe")
        q_back = [sem(f"q_back{t}") for t in range(4)]
        f_y, f_ev, f_out = sem("f_y"), sem("f_ev"), sem("f_out")

        def blocks_before(l):
            return N_MOE * sum(n - 1 for n in ROUNDS[:l])

        def rounds_before(l):
            return sum(ROUNDS[:l])

        modulation = lambda l, j0, j1: [(l, j) for j in range(j0, j1)]
        ORDER = []
        for l in range(DEPTH):
            w_in_blocks = [(l, N_ADA + b) for b in range(N_WIN)]
            w_out_blocks = [(l, N_ADA + N_WIN + b) for b in range(N_WOUT)]
            if l == 0:
                ORDER.append(modulation(0, 0, 16) + w_in_blocks + modulation(0, 16, 24) + modulation(1, 0, 4) + w_out_blocks
                             + modulation(1, 4, 12))
            else:
                ORDER.append(modulation(1, 12, 20) + w_in_blocks + w_out_blocks + modulation(1, 20, 24))

        def streams(l):
            return 2 if l < DEPTH - 1 else 1

        def split_index(l, r):
            return blocks_before(l) + l * SPLIT_PER_LAYER + r - N_ADA

        def raw_index(l, r):
            for n in range(DEPTH):
                before = blocks_before(n) + n * N_MOE + sum(len(o) for o in ORDER[:n])
                if (l, r) in ORDER[n]:
                    return before + ORDER[n].index((l, r))
            assert r == N_ADA + N_WIN + N_WOUT
            return blocks_before(l) + l * N_MOE + sum(len(o) for o in ORDER[:l + 1])

        def block_cols(r):
            return IN_W - 7 * BW + ROPE if r == N_ADA + 7 else BW

        def attention_jobs(l):
            jobs = [("na", h, t) for h in range(HEADS) for t in (0, 1)]
            if streams(l) == 2:
                jobs += [("na", h, t) for h in range(HEADS) for t in (2, 3)]
            jobs += [("mla", h, t) for h in range(HEADS) for t in (0, 1)]
            if streams(l) == 2:
                jobs += [("mla", h, t) for h in range(HEADS) for t in (2, 3)]
            return jobs

        SMALL = 8

        SUM_BANK = [6, 3, 7, 3, 7]

        ROW_BANKS = [(2, 3, 5, 6), (0, 1, 2, 3), (2,), (0, 1)]

        def tiles_before(i):
            return sum(2 * streams(n) for n in range(i // 2 - 1))

        X_BANK = [4, 5, 6, 7, 1, 2, 4, 5]

        IN_NORM = {0: [(0, j) for j in range(8, 16)], 1: [(1, j) for j in range(4, 12)],
                   2: [(1, j) for j in range(18, 20)], 3: [(1, j) for j in range(20, 24)], 4: []}

        HIGH_ORDER = [5, 0, 1, 2, 3, 4, 6, 7]
        LOW_ORDER = [0, 1, 2, 3, 4, 6, 7, 5]

        JOBS = 32

        def nth(role, i, j):
            if isinstance(i, int):
                e = 2 * i + j
                if role < 2:
                    return 3 * e + role if e else 1 + role
                return min(3 * e + 5, N_MOE)
            return i * 6 + (3 * j + (role if role < 2 else 5))

        def raw_place(role, i, j):
            if isinstance(i, int):
                q = nth(role, i, j) - 1
                return q % RAW, q // RAW + 1
            q = 3 * j + (role if role < 2 else 5) - 1
            return q % RAW, i + (q // RAW + 1)

        def before(role, i, j):
            if isinstance(i, int) and 2 * i + j == 0:
                return 0
            return nth(role, i, j - 1)

        def round_start(l, k):
            m = rounds_before(l) + k
            r = N_ADA + N_WIN + N_WOUT
            s0 = split_index(l, r) + k * N_MOE
            n0 = raw_index(l, r) + k * N_MOE
            assert n0 % RAW == 0 and s0 % HL == 0
            return m, s0, n0 // RAW

        def rounds(eng, l, one_round, skip):
            one_round(0)
            for k in range(1, ROUNDS[l]):
                if k == 1:
                    eng.wait_ge(s_more, l + 1)
                again = eng.value_load(more[0:1, k - 1:k], min_val=0, max_val=1)
                with eng.If(again > 0):
                    one_round(k)
                with eng.Else():
                    skip(k)

        def steps(eng, step, n_tail, k):
            peeled = 2 if k else 4
            for e in range(peeled):
                step(e // 2, e % 2, e)
            with eng.Fori(peeled // 2, E // 2 - 1) as i:
                for j in range(2):
                    step(i, j, None)
            for e in range(E - 2, E + n_tail):
                step(E // 2 - 1, e - (E - 2), e)

        def combine_units(l):
            return [(t, half) for t in range(2 * streams(l)) for half in range(2)]

        def done(l, r):
            return split_index(l, r) + 1

        ada_w, w_in, w_out = a["ada_w"], a["w_in"], a["w_out"]
        w_gate, w_up, w_down = a["moe_w_gate"], a["moe_w_up"], a["moe_w_down"]

        block = ctx.enter_context(nc.Block())

        @block.sync
        def _(sp):
            def free_slot(l, p):
                if p >= RAW:
                    bl, br = ORDER[l][p - RAW]
                    if br < N_ADA:
                        sp.wait_ge(ada_mm, bl * N_ADA + br + 1)
                    else:
                        sp.wait_ge(split_hi, split_index(bl, br) + 1)
                        sp.wait_ge(split_lo, split_index(bl, br) + 1)

            def load_block(l, p):
                bl, r = ORDER[l][p]
                n = raw_index(bl, r)
                if r < N_ADA:
                    src, c0, w = ada_w[bl], r * BW, BW
                elif r < N_ADA + N_WIN:
                    src, c0 = w_in[bl], (r - N_ADA) * BW
                    w = min(BW, IN_W - c0)
                else:
                    src, c0, w = w_out[bl], (r - N_ADA - N_WIN) * BW, BW
                sp.dma_start(raw[n % RAW][:, :, 0:w],
                             src[:, c0:c0 + w].rearrange("(k p) n -> p k n", p=P)).then_inc(loaded[n % RAW], 16)

            for p in range(RAW):
                load_block(0, p)
            for l in range(DEPTH):
                for p in range(RAW, len(ORDER[l])):
                    free_slot(l, p)
                    load_block(l, p)

                def one_round(k, l=l):
                    m, s0, n0 = round_start(l, k)

                    def load(role, i, j):
                        q, _ = raw_place(role, i, j)
                        if k == 0 and isinstance(i, int) and nth(role, i, j) <= RAW:
                            free_slot(l, len(ORDER[l]) + nth(role, i, j) - 1)
                        else:
                            sp.wait_ge(split_hi, nth(role, i, j) + (s0 - RAW))
                            sp.wait_ge(split_lo, nth(role, i, j) + (s0 - RAW))
                        src = (w_gate, w_up, w_down)[role][l][bass.ds(2 * i + j, 1)]
                        dst = raw[q][:, :, :]
                        if role < 2:
                            src = src.rearrange("a (k p) n -> p (a k) n", p=P)
                        else:
                            src = src.rearrange("a (f p) n -> p (a f) n", p=P)
                            dst = dst.rearrange("p (f k) n -> p f (k n)", f=2)
                        sp.dma_start(dst, src).then_inc(loaded[q], 16)

                    def step(i, j, e):
                        if e != E:
                            load(0, i, j)
                            load(1, i, j)
                        if e != 0:
                            load(2, i, j - 1)

                    steps(sp, step, 1, k)

                def from_round(k):
                    one_round(k)
                    if k + 1 < ROUNDS[l]:
                        if k == 0:
                            sp.wait_ge(s_more, l + 1)
                        again = sp.value_load(more[0:1, k:k + 1], min_val=0, max_val=1)
                        with sp.If(again > 0):
                            from_round(k + 1)
                        with sp.Else():
                            next_layer(k + 1)
                    else:
                        next_layer(k + 1)

                def next_layer(k):
                    m, s0, n0 = round_start(l, k)
                    for q in range(RAW):
                        if k < ROUNDS[l]:
                            sp.wait_ge(loaded[q], 16 * n0)
                            sp.sem_inc(loaded[q], 16 * (N_MOE // RAW) * (ROUNDS[l] - k))
                        if l + 1 < DEPTH:
                            sp.wait_ge(split_hi, s0 - RAW + q + 1)
                            sp.wait_ge(split_lo, s0 - RAW + q + 1)
                            load_block(l + 1, q)

                from_round(0)
            for t in range(2):
                sp.wait_ge(f_ev, 4)
                sp.dma_start(out[t * P:(t + 1) * P, :], y_tok[:, t, :]).then_inc(f_out, 16)
            sp.wait_ge(f_out, 32)


        @block.gpsimd
        def _(pool):
            made = [0]

            def then(ins):
                made[0] += 1
                ins.then_inc(chain_p, 1)
                pool.wait_ge(chain_p, made[0])

            def small_weights(l):
                if l:
                    pool.wait_ge(used, split_index(l, N_ADA))
                pool.memset(pool_bd[:, :, :], 0.0).then_inc(s_zero, 1)
                pool.wait_ge(s_small, l * (16 * SMALL) + 16 * SMALL)
                pool.wait_ge(s_vec, 1)
                pool.wait_ge(s_const, 16)
                for c in range(2):
                    pool.tensor_scalar(w_uq[:, c, :], w_uq[:, c, :], vec[:, V_QG + 2 * l + c:V_QG + 2 * l + c + 1], 1.0,
                                       ALU.mult, ALU.mult)
                then(pool.tensor_scalar(w_ukv[:, :], w_ukv[:, :], vec[:, V_KVG + l:V_KVG + l + 1], 1.0, ALU.mult, ALU.mult))
                w4 = w_uq[:, :, :].rearrange("p c (h m) -> p c h m", m=QK)
                for c in range(2):
                    pool.tensor_copy(w_uqs[:, c, :, 0:NOPE], w4[:, c, :, 0:NOPE])
                    for half in range(2):
                        for part in range(2):
                            to, fr = NOPE + 16 * part + 8 * half, NOPE + 16 * part + 8 * (1 - half)
                            last = pool.tensor_copy(w_uqs[:, c, :, to:to + 8], w4[:, c, :, fr:fr + 8])
                last.then_inc(s_wg, 1)
                for h in range(HEADS):
                    last = pool.tensor_tensor(na_bias[:, h, :, :], na_bias[:, h, :, :],
                                              const[:, C_NEGM:C_NEGM + GRID][:, None, :].to_broadcast([P, 6, GRID]), ALU.add)
                last.then_inc(s_bias, 1)

            small_weights(0)
            for l in range(DEPTH):
                ns = streams(l)
                n = raw_index(l, N_ADA + 7)
                pool.wait_ge(loaded[n % RAW], 16 * (n // RAW + 1))
                rk = raw[n % RAW]
                for half in range(2):
                    for part in range(2):
                        to, fr = 160 + 16 * part + 8 * half, 128 + 16 * part + 8 * (1 - half)
                        last = pool.tensor_copy(rk[:, :, to:to + 8], rk[:, :, fr:fr + 8])
                last.then_inc(s_swap, 1)
                pool.wait_ge(used, done(l, N_ADA))
                pool.memset(a_pad[:, :, :, 0:PAD], 0.0)
                pool.memset(a_pad[:, :, :, PAD + S:PW], 0.0).then_inc(s_pads, 1)
                pool.wait_ge(proj_ed, l * 5 + 1)
                pool.wait_ge(s_pads, l + 1)
                pool.wait_ge(used, split_index(l, N_ADA + 7) + 1)

                def window(dst, src, ch, p0, lo, hi, back, ahead):
                    return pool.tensor_tensor(dst[p0:P, ch, 0:ns, lo:hi], src[p0:P, ch, 0:ns, lo - back:hi - back],
                                              src[p0:P, ch, 0:ns, lo + ahead:hi + ahead], ALU.add)

                window(win_a, a_pad, 0, 0, 1, PW, 1, 0)
                then(window(win_a, a_pad, 1, 0, 1, PW, 1, 0))
                then(window(win_b, win_a, 0, 64, 2, PW - 1, 1, 1))
                then(window(win_b, win_a, 1, 0, 2, PW - 1, 1, 1))
                then(window(win_a, win_b, 1, 0, 4, PW - 3, 2, 2))
                then(window(win_b, win_a, 1, 64, 8, PW - 8, 4, 4))
                for g, w in enumerate((win_a, win_b, win_a, win_b)):
                    ch, p0 = g // 2, 64 * (g % 2)
                    sl = w[p0:p0 + 64, ch, 0:ns, PAD:PAD + S]
                    inv = const[p0:p0 + 64, C_INV + ch * S:C_INV + (ch + 1) * S][:, None, :].to_broadcast([64, ns, S])
                    then(pool.tensor_tensor(sl, sl, inv, ALU.mult))
                for g, w in enumerate((win_a, win_b, win_a, win_b)):
                    ch, p0 = g // 2, 64 * (g % 2)
                    ins = pool.tensor_tensor(pool_d[p0:p0 + 64, ch, 0:ns * S].rearrange("p (s t) -> p s t", s=ns),
                                             w[p0:p0 + 64, ch, 0:ns, PAD:PAD + S],
                                             a_pad[p0:p0 + 64, ch, 0:ns, PAD:PAD + S], ALU.subtract)
                    if g < 3:
                        then(ins)
                ins.then_inc(s_pool, 1)

                pool.wait_ge(q_row, l + 1)
                for par in range(2):
                    pool.wait_ge(q_out[par], 16 * (E // 2) * rounds_before(l + 1))

                def take(n):
                    if n < ROUNDS[l]:
                        again = pool.value_load(more[0:1, n - 1:n], min_val=0, max_val=1)
                        with pool.If(again > 0):
                            take(n + 1)
                        with pool.Else():
                            take_from(n)
                    else:
                        take_from(n)

                def take_from(n):
                    for t in range(2 * ns):
                        for i in range(2):
                            pool.indirect_dma_start(y_back[:, t, i, :], None, y_rows[0:n * E * SLOTS, :],
                                                    bass.IndirectOffsetOnAxis(ap=pick_row[:, t, i:i + 1], axis=0)).then_inc(q_back[t], 16)

                take(1)
                if l + 1 < DEPTH:
                    small_weights(l + 1)

        @block.scalar
        def _(act):
            def small_loads(l):
                if l:
                    act.wait_ge(used, split_index(l, N_ADA))
                act.wait_ge(s_zero, l + 1)
                pw = a["pool_w"]
                for half in range(2):
                    src = bass.AP(pw.tensor, (l * 4 + half) * 4096, [[64, 64], [8192, 2], [1, 64]])
                    act.dma_start(pool_bd[64 * half:64 * half + 64, :, 64 * half:64 * half + 64], src).then_inc(s_small, 16)
                act.dma_start(w_uq[:, :, :], a["mla_w_uq"][l].rearrange("(c p) n -> p c n", p=P)).then_inc(s_small, 16)
                act.dma_start(w_ukv[:, :], a["mla_w_ukv"][l]).then_inc(s_small, 16)
                act.dma_start(sgu_g[:, :], bass.AP(a["sgu_norm_g"].tensor, l * S, [[0, P], [1, S]])).then_inc(s_small, 16)
                act.dma_start(sgu_w[:, :, :], a["sgu_w"][l].rearrange("g p q -> p g q")).then_inc(s_small, 16)
                rp = a["na_rpb"]
                for half in range(2):
                    src = bass.AP(rp.tensor, (2 * l + half) * HEADS * 6 * P, [[1, GRID], [P, HEADS * 6], [1, GRID]])
                    act.dma_start(na_bias[64 * half:64 * half + 64, :, :, :].rearrange("p h r c -> p (h r) c"), src).then_inc(s_small, 16)

            act.dma_start(raw_vec[0][0:112, :], a["vec0"]).then_inc(s_vecin, 16)
            act.dma_start(raw_vec[1][0:N_VEC - 112, :], a["vec1"]).then_inc(s_vecin, 16)
            act.dma_start(const[:, 0:P], a["const"][:, 0:P]).then_inc(s_ident, 16)
            act.wait_ge(s_vec, 1)
            act.activation(c_act[:, :], vec[:, V_C:V_C + 16], ACT.Silu).then_inc(s_cact, 1)
            for t in range(4):
                act.dma_start(x_tok[t][:, :], a["x" if t < 2 else "ctx"][(t % 2) * P:(t % 2 + 1) * P, :]).then_inc(s_xin, 16)
            act.dma_start(const[:, P:N_CONST], a["const"][:, P:N_CONST]).then_inc(s_const, 16)
            act.dma_start(rw_in[:, :, :], a["router_w"].rearrange("(k p) e -> p k e", p=P)).then_inc(s_bcast, 16)
            act.dma_start(rb_row[:, :], bass.AP(a["router_b"].tensor, 0, [[0, P], [1, E]])).then_inc(s_bcast, 16)
            small_loads(0)
            act.wait_ge(s_bcast, 32)
            act.activation(rw_hi[:, :, :], rw_in[:, :, :], ACT.Copy).then_inc(s_rw, 1)

            def split(l, r):
                s, n = split_index(l, r), raw_index(l, r)
                act.wait_ge(loaded[n % RAW], 16 * (n // RAW + 1))
                if r == N_ADA + 7:
                    act.wait_ge(s_swap, l + 1)
                if s >= HL:
                    act.wait_ge(used, s - HL + 1)
                w = block_cols(r)
                act.activation(w_hi[s % HL][:, :, 0:w], raw[n % RAW][:, :, 0:w], ACT.Copy).then_inc(split_hi, 1)

            def norm(i, width, which, l):
                ns = width // S
                if i == 0:
                    for k in range(0, KC, 2):
                        if k >= 4:
                            act.wait_ge(n_sum, k - 3)
                        act.activation(nsq[:, k % 4, 0:width], x_t[:, k, 0:width], ACT.Square).then_inc(n_sqa, 1)
                    act.wait_ge(n_sum, KC)
                elif i % 2:
                    for c in range(KC):
                        act.wait_ge(o_ev, l * KC + c + 1)
                        if c >= 4:
                            act.wait_ge(n_suc, l * KC + c - 3)
                        act.activation(nsq[:, c % 4, 0:width], x_t[:, c, 0:width], ACT.Square).then_inc(n_sqc, 1)
                    act.wait_ge(n_suc, l * KC + KC)
                else:
                    units = sum(len(combine_units(n)) for n in range(i // 2 - 1))
                    for t in range(2 * streams(i // 2 - 1)):
                        act.wait_ge(x_moe, units + 2 * t + 2)
                        if t >= 2:
                            act.wait_ge(n_sut, tiles_before(i) + t - 1)
                        act.activation(nsq_t[:, t % 2, :, :], x_t[:, :, t * P:(t + 1) * P], ACT.Square).then_inc(n_sqt, 1)
                    act.wait_ge(n_sut, tiles_before(i) + width // P)
                if i == 0:
                    act.wait_ge(s_const, 16)
                act.activation(col[:, 0:width // P], bank[SUM_BANK[i]][:, 0:width // P], ACT.Sqrt, bias=eps, scale=1.0 / D).then_inc(n_root, 1)
                if which == 0:
                    for r in range(N_ADA, N_ADA + HL - 1):
                        split(l, r)
                if which is not None:
                    act.wait_ge(s_mod, (1, 3, 4, 5)[i])
                for k in range(KC):
                    act.wait_ge(n_x, i * KC + k + 1)
                    if k >= 2:
                        if which is None:
                            act.wait_ge(f_y, k - 1)
                        else:
                            act.wait_ge(n_lo, i * KC + k - 1)
                    if which is None:
                        act.activation(nh[:, k % 2, 0:width], nx[:, k % 2, 0:width], ACT.Identity,
                                       scale=vec[:, V_FIN + k:V_FIN + k + 1]).then_inc(n_h[i], 1)
                        continue
                    for s in range(ns):
                        act.activation(nh[:, k % 2, s * S:(s + 1) * S], nx[:, k % 2, s * S:(s + 1) * S], ACT.Identity,
                                       bias=mod_of[l][:, s, 24 * which + k:24 * which + k + 1],
                                       scale=amp[:, which, s, k:k + 1]).then_inc(n_h[i], 1)
                    act.wait_ge(n_h[i], ns * (k + 1))
                    act.activation(h_hi[:, k, 0:width], nh[:, k % 2, 0:width], ACT.Copy).then_inc(n_hi, 1)

            for l in range(DEPTH):
                ns = streams(l)
                nt, width = 2 * ns, ns * S
                if l == 0:
                    for k in range(1, KC, 2):
                        act.wait_ge(s_xt, k + 1)
                        act.activation(x_t[:, k, :], bank[X_BANK[k]][:, :], ACT.Copy).then_inc(s_xev, 1)
                    act.wait_ge(s_xevd, 4)
                norm(2 * l, T, 0, l)
                split(l, N_ADA + HL - 1)
                for b in range(N_WIN):
                    if b == 1:
                        act.wait_ge(used, done(l, N_ADA + 1))
                        act.activation(q_na[:, 0, 0:width], bank[2][:, 0:width], ACT.Copy, scale=NA_SCALE)
                        act.activation(q_na[:, 1, 0:width], bank[3][:, 0:width], ACT.Copy, scale=NA_SCALE).then_inc(proj_ea, 1)
                    if b in (4, 5):
                        act.wait_ge(used, done(l, N_ADA + b))
                        dst = sgu_u if b == 4 else sgu_v
                        for s in range(ns):
                            last = act.activation(dst[:, 2 * s:2 * s + 2, :].rearrange("p t n -> p (t n)"),
                                                  bank[2 * (b % 4) + s][:, :], ACT.Gelu_apprx_tanh)
                        last.then_inc(proj_ea, 1)
                    if b == 7:
                        act.wait_ge(used, done(l, N_ADA + 7))
                        act.activation(kv_low[:, :], bank[6][:, :], ACT.Copy).then_inc(proj_ea, 1)
                    if b + HL < N_WIN:
                        split(l, N_ADA + b + HL)
                act.wait_ge(used, split_index(l, N_ADA + 7) + 1)
                act.wait_ge(proj_ed, l * 5 + 4)
                act.activation(low_sq[:, 0:2, 0:width], q_low[:, :, 0:width], ACT.Square).then_inc(s_lsq, 1)
                act.wait_ge(proj_ea, l * 4 + 4)
                act.activation(low_sq[:, 2, :], kv_low[:, :], ACT.Square).then_inc(s_lsq, 1)
                act.wait_ge(s_lsum, l + 1)
                act.activation(col[:, 8:8 + nt], bank[7][:, 0:nt], ACT.Sqrt, bias=eps, scale=1.0 / 256)
                act.activation(col[:, 12:16], bank[7][:, 4:8], ACT.Sqrt, bias=eps, scale=1.0 / P).then_inc(s_lroot, 1)
                act.wait_ge(s_gv, l + 1)
                act.activation(col[:, 32:32 + 4 * nt], col[:, 16:16 + 4 * nt], ACT.Sqrt, bias=eps, scale=1.0 / 64).then_inc(s_groot, 1)
                act.wait_ge(s_wt, l + 1)
                act.activation(sgu_wt[:, :, :].rearrange("p g n -> p (g n)"), bank[6][:, :], ACT.Copy).then_inc(s_wte, 1)
                for h in range(HEADS):
                    act.wait_ge(s_up, l * 11 + h + 1)
                    act.activation(q_mla[0:QK, h, 0:width], bank[2 + h][0:QK, 0:width], ACT.Copy, scale=MLA_SCALE).then_inc(s_qe, 1)
                for h in range(HEADS):
                    act.wait_ge(s_up, l * 11 + 6 + h + 1)
                    act.activation(k_mla[0:NOPE, h, :], bank[h][0:NOPE, :], ACT.Copy).then_inc(s_ke, 1)
                act.wait_ge(s_up, l * 11 + 11)
                act.activation(v_mla[:, 0:2, :].rearrange("p t n -> p (t n)"), bank[4][:, :], ACT.Copy)
                act.activation(v_mla[:, 2:4, :].rearrange("p t n -> p (t n)"), bank[5][:, :], ACT.Copy).then_inc(s_ve, 1)
                jobs = attention_jobs(l)
                for i in range(len(jobs) + 1):
                    if i < len(jobs):
                        nk = T if jobs[i][2] < 2 else S
                        act.wait_ge(t_mx, l * JOBS + i + 1)
                        if i >= 3:
                            act.wait_ge(t_tr, l * JOBS + i - 2)
                        act.activation(prob[i % 3][:, 0:nk], bank[i % 3][:, 0:nk], ACT.Exp, bias=stat[:, i % 4, 0:1],
                                       accum_out=stat[:, i % 4, 1:2]).then_inc(t_ex, 1)
                    if i >= 1 and i % 2 == 1:
                        q = i - 1
                        nkt = 4 if jobs[q][2] < 2 else 2
                        act.wait_ge(t_tr, l * JOBS + q + 1)
                        if q >= 3:
                            act.wait_ge(t_pv, l * JOBS + q - 2)
                        act.activation(prob_t[q % 3][:, 0:nkt, :].rearrange("p k n -> p (k n)"),
                                       bank[3 + q % 2][:, 0:nkt * P], ACT.Copy).then_inc(t_pa, 1)
                for c in range(KC):
                    act.wait_ge(m_ps, l * KC + c + 1)
                    if c == 0:
                        act.wait_ge(t_pv, l * JOBS + len(jobs))
                    scale = vec[:, V_PS + 2 * l + c:V_PS + 2 * l + c + 1] if c < 2 else 1.0
                    act.activation(h_hi[:, c, 0:width], bank[c][:, 0:width], ACT.Identity if c < 2 else ACT.Copy,
                                   scale=scale).then_inc(m_hi, 1)
                act.dma_start(const2[:, :], a["const2"]).then_inc(s_const2, 16)
                for r in range(N_ADA + N_WIN, N_ADA + N_WIN + N_WOUT):
                    split(l, r)
                norm(2 * l + 1, width, 1, l)
                act.wait_ge(r_lt, l + 1)
                act.activation(logit_t[0:E, 0:width], bank[5][0:E, 0:width], ACT.Copy).then_inc(r_le, 1)
                act.wait_ge(r_lg, l + 1)
                act.activation(score[:, 0:nt, :].rearrange("p t e -> p (t e)"), bank[5][:, 0:nt * E], ACT.Sigmoid).then_inc(r_sg, 1)

                def split_expert(l, k, role, i, j):
                    m, s0, n0 = round_start(l, k)
                    q, n = raw_place(role, i, j)
                    act.wait_ge(loaded[q], n * 16 + 16 * n0)
                    act.wait_ge(used, before(role, i, j) + s0)
                    act.activation(w_hi[role][:, :, :], raw[q][:, :, :], ACT.Copy).then_inc(split_hi, 1)

                split_expert(l, 0, 0, 0, 0)
                act.wait_ge(q_tok, l * (2 * KC) + KC)
                for c in HIGH_ORDER:
                    act.activation(h_tok[0][:, 0:nt, c * P:(c + 1) * P], bank[c][:, 0:width].rearrange("p (t d) -> p t d", d=P),
                                   ACT.Copy).then_inc(q_ta, 1)
                split_expert(l, 0, 1, 0, 0)
                act.wait_ge(q_tok, (l + 1) * (2 * KC))
                for c in range(KC // 2):
                    act.activation(h_tok[1][:, 0:nt, c * P:(c + 1) * P], bank[c][:, 0:width].rearrange("p (t d) -> p t d", d=P),
                                   ACT.Copy).then_inc(q_ta, 1)

                def one_round(k, l=l):
                    m, s0, n0 = round_start(l, k)

                    def y_half(i, j):
                        par, i2 = j % 2, i + j // 2
                        act.wait_ge(used, nth(2, i, j) + s0)
                        act.wait_ge(q_out[par], i2 * 16 + 16 * (E // 2) * m)
                        act.activation(y_sb[par][:, 0:512], bank[6][:, :], ACT.Copy).then_inc(q_ya, 1)

                    def y_store(i, j, y_rows_=y_rows.rearrange("(k e p) d -> k e p d", e=E, p=SLOTS)):
                        act.wait_ge(q_ya, 2 * i + (m * E + j + 1))
                        act.wait_ge(q_yd, 2 * i + (m * E + j + 1))
                        act.dma_start(y_rows_[k, bass.ds(2 * i + j, 1), :, :].rearrange("a p d -> p (a d)"),
                                      y_sb[j % 2][:, :]).then_inc(q_out[j % 2], 16)

                    def step(i, j, e):
                        if (e is None or e < E) and j % 2 == 0:
                            for half in range(2):
                                act.wait_ge(g_hi, 2 * i + (m * E + half + 1))
                                for b in range(2):
                                    ins = act.activation(xg_hi[:, 4 * half + 2 * b:4 * half + 2 * b + 2, :].rearrange("p k n -> p (k n)"),
                                                         bank[2 * half + b][:, :], ACT.Copy)
                                ins.then_inc(x_hi, 1)
                        if e is None or e >= 2:
                            y_half(i, j - 2)
                        if e is None or 1 <= e <= E:
                            if e != E:
                                split_expert(l, k, 2, i, j - 1)
                            act.wait_ge(q_t, 2 * i + (m * E + j))
                            act.wait_ge(used, s0 if e in (1, 2) else nth(2, i, j - 3) + s0)
                            act.activation(ht_hi[(j - 1) % 2][:, :, :].rearrange("p f n -> p (f n)"), bank[5][:, 0:2 * SLOTS],
                                           ACT.Copy).then_inc(q_th, 1)
                            if e == E:
                                split_expert(l, k, 2, i, j - 1)
                        if e is None or e >= 2:
                            y_store(i, j - 2)
                        if e is None or e < E - 1:
                            split_expert(l, k, 0, i, j + 1)
                        if e is None or e < E:
                            act.wait_ge(used, nth(1, i, j) + s0)
                            act.wait_ge(q_m, 2 * i + (m * E + j))
                            act.activation(hid_g[:, :], bank[4][:, 0:FE], ACT.Silu).then_inc(q_s, 1)
                        if e is None or e < E - 1:
                            split_expert(l, k, 1, i, j + 1)

                    if k:
                        split_expert(l, k, 0, 0, 0)
                        split_expert(l, k, 1, 0, 0)
                    steps(act, step, 2, k)

                def skip(k, l=l):
                    m, s0, n0 = round_start(l, k)
                    act.wait_ge(split_hi, s0)
                    act.wait_ge(q_ya, m * E)
                    act.sem_inc(split_hi, N_MOE)
                    for sem_ in (x_hi, q_th, q_ya, q_s):
                        act.sem_inc(sem_, E)
                    for sem_ in q_out:
                        act.wait_ge(sem_, 16 * (E // 2) * m)
                        act.sem_inc(sem_, 16 * (E // 2))

                rounds(act, l, one_round, skip)
                if l + 1 < DEPTH:
                    small_loads(l + 1)
            norm(2 * DEPTH, S, None, DEPTH)
            for t in range(2):
                act.wait_ge(f_y, KC)
                act.activation(y_tok[:, t, 512:1024], bank[1 + 2 * t][:, :], ACT.Copy).then_inc(f_ev, 1)

        @block.tensor
        def _(pe):
            def product(dst, w_hi_, w_lo_, x_hi_, x_lo_, first, last):
                pe.matmul(dst, w_hi_, x_hi_, start=first, stop=False)
                pe.matmul(dst, w_hi_, x_lo_, start=False, stop=False)
                return pe.matmul(dst, w_lo_, x_hi_, start=False, stop=last)

            def wait_split(l, r):
                pe.wait_ge(split_lo, split_index(l, r) + 1)

            def column_sums(dst, src, k, n, last):
                for t in range(n):
                    ins = pe.matmul(dst[:, t:t + 1], src[:, t * P:(t + 1) * P], ones[:, 0:1], start=(k == 0 and t == 0),
                                    stop=last, skip_group_check=True)
                return ins

            def rows_of(dst, column, n):
                for t in range(n):
                    ap = column[:, t:t + 1].to_broadcast([P, P])
                    ins = pe.matmul(dst[:, t * P:(t + 1) * P], ap, ident, start=True, stop=True)
                return ins

            def modulate(l, j, dst):
                n = raw_index(l, j)
                pe.wait_ge(loaded[n % RAW], 16 * (n // RAW + 1))
                for k in range(KC):
                    ins = pe.matmul(dst, c_act[:, k:k + 9:8], raw[n % RAW][:, k, :], start=(k == 0), stop=(k == KC - 1))
                ins.then_inc(ada_mm, 1)

            turned = [0]

            def turn(blocks, dst):
                pe.wait_ge(m_row, turned[0] + 1)
                for b, (l, j) in enumerate(blocks):
                    for c in range(2):
                        o = 4 * j + 2 * c
                        o += 256 if dst is bank[7] else 0
                        ins = pe.transpose(dst[:, o:o + 2], mod_row[:, turned[0] % 2, b * BW + c * P:b * BW + (c + 1) * P], ident[0:2, 0:2])
                ins.then_inc(m_turn, 1)
                turned[0] += 1

            def half_bank(q, banks=range(8)):
                return bank[banks[q // 2]][0:2, (q % 2) * BW:(q % 2 + 1) * BW]

            def norm(i, width, columns):
                between = IN_NORM[i]
                n = width // P
                if i == 0:
                    for k in range(KC):
                        pe.wait_ge(n_sqa if k % 2 == 0 else n_sqd, k // 2 + 1)
                        column_sums(bank[6], nsq[:, k % 4, :], k, n, k == KC - 1).then_inc(n_sum, 1)
                for q, (l, j) in enumerate(between[:1]):
                    modulate(l, j, half_bank(q, ROW_BANKS[i]))
                pe.wait_ge(n_rstd, i + 1)
                rows_of(bank[7], rstd, n).then_inc(n_bc, 1)
                for q, (l, j) in enumerate(between):
                    if i == 0 and q == 2:
                        pe.wait_ge(s_mod, 1)
                    if q >= 1:
                        modulate(l, j, half_bank(q, ROW_BANKS[i]))
                if i % 2:
                    turn_in_norm(i, columns)

            def turn_in_norm(i, columns):
                for q in range(0, len(IN_NORM[i]), 2):
                    turn(IN_NORM[i][q:q + 2], columns)

            def combine(l, u):
                units = combine_units(l)
                n = sum(len(combine_units(i)) for i in range(l))
                t, half = units[u]
                pe.wait_ge(q_c, n // 2 + t + 1)
                if u >= 3:
                    pe.wait_ge(x_moe, n + u - 2)
                for c in range(4):
                    k = 4 * half + c
                    ins = pe.transpose(bank[4 + u % 3][:, c * P:(c + 1) * P], y_back[:, t, 0, k * P:(k + 1) * P], ident)
                ins.then_inc(q_ct, 1)
                if half and t:
                    tile_sums(l, t - 1)
                if u == len(units) - 1:
                    tile_sums(l, t)

            def tile_sums(l, t):
                pe.wait_ge(n_sqt, tiles_before(2 * l + 2) + t + 1)
                for k in range(KC):
                    ins = pe.matmul(bank[7][:, t:t + 1], nsq_t[:, t % 2, k, :], ones[:, 0:1], start=(k == 0 and t == 0),
                                    stop=(k == KC - 1), skip_group_check=True)
                ins.then_inc(n_sut, 1)

            pe.wait_ge(s_ident, 16)
            pe.wait_ge(s_vecin, 32)
            pe.transpose(bank[0][:, 0:112], raw_vec[0][0:112, :], ident[0:112, 0:112])
            pe.transpose(bank[0][:, 112:N_VEC], raw_vec[1][0:N_VEC - 112, :], ident[0:N_VEC - 112, 0:N_VEC - 112]).then_inc(s_vt, 1)
            pe.wait_ge(s_cact, 1)

            for l in range(DEPTH):
                ns = streams(l)
                nt, width = 2 * ns, ns * S

                if l == 0:
                    for j in range(8):
                        if j == 6:
                            turn([(0, 2), (0, 3)], bank[3])
                            pe.wait_ge(m_row, 3)
                            pe.wait_ge(s_xin, 64)
                            for k in range(KC):
                                if k >= 6:
                                    pe.wait_ge((s_xevd, s_xev)[k % 2], 1)
                                for t in range(4):
                                    ins = pe.transpose(bank[X_BANK[k]][:, t * P:(t + 1) * P], x_tok[t][:, k * P:(k + 1) * P], ident)
                                ins.then_inc(s_xt, 1)
                        modulate(0, j, half_bank(j if j < 6 else j - 6))
                        if j == 3:
                            turn([(0, 0), (0, 1)], bank[3])
                    turn([(0, 4), (0, 5)], bank[3])
                    turn([(0, 6), (0, 7)], bank[3])
                    pe.wait_ge(s_const, 16)
                    norm(0, T, bank[4])
                else:
                    for j in (12, 13):
                        modulate(1, j, half_bank(j - 12))
                    pe.wait_ge(q_ya, E * rounds_before(l))
                    pe.wait_ge(q_yd, E * rounds_before(l))
                    between = {0: (14,), 1: (15,), 2: (16, 17), 3: ()}
                    for u, (t, half) in enumerate(combine_units(l - 1)):
                        combine(l - 1, u)
                        if half:
                            for j in between[t]:
                                modulate(1, j, half_bank(j - 12))
                            if t:
                                j = 10 + 2 * t
                                turn([(1, j), (1, j + 1)], bank[3])
                    norm(2 * l, T, bank[3])

                def by_feature(b, c, dst, c0, m, width, l=l):
                    s = split_index(l, N_ADA + b) % HL
                    for k in range(KC):
                        ins = product(dst[0:m, 0:width], w_hi[s][:, k, c0:c0 + m], w_lo[s][:, k, c0:c0 + m],
                                      h_hi[:, k, 0:width], h_lo[:, k, 0:width], k == 0, k == KC - 1)
                    return ins

                for b in range(N_WIN):
                    wait_split(l, N_ADA + b)
                    if b == 1:
                        turn_in_norm(2 * l, bank[4] if l == 0 else bank[3])
                    if b == 2 - l:
                        pe.wait_ge(s_mod, 2 if l == 0 else 5)
                    if b == 4:
                        pe.wait_ge(proj_ed, l * 5 + 1)
                    if b == 5:
                        pe.wait_ge(proj_ea, l * 4 + 1)
                    if b == 6:
                        pe.wait_ge(proj_ed, l * 5 + 2)
                    if b == 7:
                        pe.wait_ge(proj_ed, l * 5 + 3)
                        pe.wait_ge(proj_ea, l * 4 + 2)
                    b0 = 2 * (b % 4)
                    if b in (3, 4, 5):
                        s = split_index(l, N_ADA + b) % HL
                        for t in range(4 if b == 3 else nt):
                            dst = bank[b0 + t // 2][:, (t % 2) * BW:(t % 2 + 1) * BW]
                            for k in range(KC):
                                pe.matmul(dst, h_hi[:, k, t * P:(t + 1) * P], w_hi[s][:, k, :], start=(k == 0), stop=False)
                                pe.matmul(dst, h_hi[:, k, t * P:(t + 1) * P], w_lo[s][:, k, :], start=False, stop=False)
                                ins = pe.matmul(dst, h_lo[:, k, t * P:(t + 1) * P], w_hi[s][:, k, :], start=False, stop=(k == KC - 1))
                    elif b == 7:
                        by_feature(b, 0, bank[6], 0, P, T)
                        by_feature(b, 1, bank[7], 64, QK, T)
                        ins = by_feature(b, 1, bank[0], 96, QK, S)
                    else:
                        if b == 0:
                            s = split_index(l, N_ADA) % HL
                            for k in range(KC):
                                pe.wait_ge(n_lo, (2 * l) * KC + k + 1)
                                for c in range(2):
                                    cs = slice(c * P, (c + 1) * P)
                                    ins = product(bank[c][:, 0:width], w_hi[s][:, k, cs], w_lo[s][:, k, cs],
                                                  h_hi[:, k, 0:width], h_lo[:, k, 0:width], k == 0, k == KC - 1)
                        else:
                            for c in range(2):
                                ins = by_feature(b, c, bank[b0 + c], c * P, P, T if b == 2 else width)
                    ins.then_inc(used, 1)

                pe.wait_ge(s_small, l * (16 * SMALL) + 16 * SMALL)
                pe.wait_ge(proj_ea, l * 4 + 4)
                for g in range(4):
                    ins = pe.transpose(bank[6][:, g * P:(g + 1) * P], sgu_w[:, g, :], ident)
                ins.then_inc(s_wt, 1)
                pe.wait_ge(s_lsq, l * 2 + 2)
                pe.wait_ge(proj_ed, l * 5 + 5)
                for c in range(2):
                    column_sums(bank[7][:, 0:4], low_sq[:, c, :], c, nt, c == 1)
                for t in range(4):
                    ins = pe.matmul(bank[7][:, 4 + t:5 + t], low_sq[:, 2, t * P:(t + 1) * P], ones[:, 0:1], start=False,
                                    stop=True, skip_group_check=True)
                ins.then_inc(s_lsum, 1)
                pe.wait_ge(s_lrstd, l + 1)
                rows_of(bank[0], col[:, 48:52], nt)
                rows_of(bank[1], col[:, 52:56], 4).then_inc(s_lbc, 1)
                pe.wait_ge(s_wg, l + 1)
                pe.wait_ge(s_low, l * 3 + 2)
                for h in range(HEADS):
                    for c in range(2):
                        ins = pe.matmul(bank[2 + h][0:QK, 0:width], w_uq[:, c, h * QK:(h + 1) * QK], q_low[:, c, 0:width],
                                        start=(c == 0), stop=(c == 1))
                    ins.then_inc(s_up, 1)
                pe.wait_ge(s_wte, l + 1)
                pe.wait_ge(s_lroot, l + 1)
                for h in range(HEADS):
                    for c in range(2):
                        ins = pe.matmul(bank[6 + h // 2][0:QK, (h % 2) * S:(h % 2 + 1) * S], w_uqs[:, c, h, :],
                                        q_low[:, c, 0:S], start=(c == 0), stop=(c == 1))
                    if h % 2:
                        ins.then_inc(s_up, 1)
                for h in range(HEADS):
                    if h == 0:
                        pe.wait_ge(s_low, l * 3 + 3)
                    if h == 2:
                        pe.wait_ge(s_qe, l * 4 + 2)
                    pe.matmul(bank[h][0:NOPE, :], w_ukv[:, h * P:h * P + NOPE], kv_low[:, :], start=True, stop=True).then_inc(s_up, 1)
                pe.wait_ge(s_qe, l * 4 + 4)
                for t in range(4):
                    ins = pe.matmul(bank[4 + t // 2][:, (t % 2) * S:(t % 2 + 1) * S], kv_low[:, t * P:(t + 1) * P],
                                    w_ukv[:, :].rearrange("p (h m) -> p h m", m=P)[:, :, NOPE:P], start=True, stop=True)
                ins.then_inc(s_up, 1)
                pe.wait_ge(s_gn, l + 1)
                pe.wait_ge(s_rot, l * 2 + 1)
                for g in range(4):
                    ins = pe.matmul(bank[6 + g // 2][:, (g % 2) * S:(g % 2) * S + nt * 64], sgu_wt[:, g, :],
                                    sgu_v[:, 0:nt, g * 64:(g + 1) * 64], start=True, stop=True)
                ins.then_inc(s_mix, 1)

                jobs = attention_jobs(l)
                n_jobs = len(jobs)
                pe.wait_ge(s_ke, l * 4 + 4)
                pe.wait_ge(s_ve, l + 1)
                pe.wait_ge(s_bias, l + 1)
                pe.wait_ge(s_rot, l * 2 + 2)
                pe.wait_ge(s_go, l + 1)
                for i in range(n_jobs + 2):
                    if i < n_jobs:
                        kind, h, t = jobs[i]
                        keys = slice(0, T) if t < 2 else slice(S, T)
                        nk = keys.stop - keys.start
                        if i >= 3:
                            pe.wait_ge(t_ex, l * JOBS + i - 2)
                        if kind == "na":
                            r = slice(64 * (h % 2), 64 * (h % 2) + 64)
                            ins = pe.matmul(bank[i % 3][:, 0:nk], q_na[r, h // 2, t * P:(t + 1) * P], k_na[r, h // 2, keys],
                                            start=True, stop=True)
                            if t < 2:
                                s = 2 - 2 * t
                                ins = pe.matmul(bank[i % 3][:, 0:S], const[:, C_FLIP:C_FLIP + P],
                                                na_bias[:, h, s:s + 4, :].rearrange("p r c -> p (r c)"),
                                                start=False, stop=True, skip_group_check=True)
                        else:
                            ins = pe.matmul(bank[i % 3][:, 0:nk], q_mla[0:QK, h, t * P:(t + 1) * P], k_mla[0:QK, h, keys],
                                            start=True, stop=True)
                        ins.then_inc(t_sc, 1)
                    if 1 <= i <= n_jobs:
                        q = i - 1
                        pe.wait_ge(t_ex, l * JOBS + q + 1)
                        if q >= 2:
                            pe.wait_ge(t_pa if q % 2 == 0 else t_pd, l * (JOBS // 2) + (q - 2) // 2 + 1)
                        for kt in range(4 if jobs[q][2] < 2 else 2):
                            ins = pe.transpose(bank[3 + q % 2][:, kt * P:(kt + 1) * P], prob[q % 3][:, kt * P:(kt + 1) * P], ident)
                        ins.then_inc(t_tr, 1)
                    if i >= 2:
                        q = i - 2
                        kind, h, t = jobs[q]
                        pe.wait_ge(t_pa if q % 2 == 0 else t_pd, l * (JOBS // 2) + q // 2 + 1)
                        if q >= 2:
                            pe.wait_ge(t_o, l * JOBS + q - 1)
                        v = v_na if kind == "na" else v_mla
                        tiles = range(4) if t < 2 else range(2, 4)
                        for n, kt in enumerate(tiles):
                            ins = pe.matmul(bank[5 + q % 2][:, 0:64], prob_t[q % 3][:, n, :], v[:, kt, h * 64:(h + 1) * 64],
                                            start=(n == 0), stop=(n == len(tiles) - 1))
                        ins.then_inc(t_pv, 1)
                    if l == 0 and i // 2 - 1 in range(12):
                        b = divmod(16 + i // 2 - 1, N_ADA)
                        if i % 2 == 0:
                            modulate(*b, bank[7][0:2, 0:BW])
                        else:
                            turn([b], bank[7])
                pe.wait_ge(s_pool, l + 1)
                pe.wait_ge(t_o, l * JOBS + n_jobs)
                pe.wait_ge(s_mod, 3)
                for c in range(KC):
                    if c < 2:
                        ins = pe.matmul(bank[c][:, 0:width], pool_bd[:, c, :], pool_d[:, c, 0:width], start=True, stop=True)
                    else:
                        for t in range(nt):
                            ins = pe.transpose(bank[c][:, t * P:(t + 1) * P], o_tok[:, t, (c - 2) * P:(c - 1) * P], ident)
                    ins.then_inc(m_ps, 1)
                pe.wait_ge(m_lo, l * KC + KC)
                for b in range(N_WOUT):
                    r = N_ADA + N_WIN + b
                    wait_split(l, r)
                    s = split_index(l, r) % HL
                    for c in range(2):
                        for k in range(KC):
                            ins = product(bank[2 * b + c][:, 0:width], w_hi[s][:, k, c * P:(c + 1) * P], w_lo[s][:, k, c * P:(c + 1) * P],
                                          h_hi[:, k, 0:width], h_lo[:, k, 0:width], k == 0, k == KC - 1)
                    ins.then_inc(used, 1)
                    if b >= 2:
                        pe.wait_ge(o_ev, l * KC + 4)
                        for c in range(4 * (b - 2), 4 * (b - 1)):
                            pe.wait_ge(n_sqc, l * KC + c + 1)
                            column_sums(bank[3], nsq[:, c % 4, :], c, nt, c == KC - 1).then_inc(n_suc, 1)

                norm(2 * l + 1, width, bank[4])
                pe.wait_ge(s_rw, 2)
                for k in range(KC):
                    pe.wait_ge(n_lo, (2 * l + 1) * KC + k + 1)
                    ins = product(bank[5][0:E, 0:width], rw_hi[:, k, :], rw_lo[:, k, :], h_hi[:, k, 0:width], h_lo[:, k, 0:width],
                                  k == 0, k == KC - 1)
                ins.then_inc(r_lt, 1)
                pe.wait_ge(r_le, l + 1)
                for t in range(nt):
                    ins = pe.transpose(bank[5][:, t * E:(t + 1) * E], logit_t[0:E, t * P:(t + 1) * P], ident[0:E, 0:E])
                ins.then_inc(r_lg, 1)

                pe.wait_ge(r_sg, l + 1)
                pe.wait_ge(s_mod, 4 if l == 0 else 6)
                for c in range(KC):
                    for t in range(nt):
                        ins = pe.transpose(bank[c][:, t * P:(t + 1) * P], h_hi[:, c, t * P:(t + 1) * P].bitcast(F32), ident)
                    ins.then_inc(q_tok, 1)
                pe.wait_ge(s_const2, 16 * (l + 1))
                pe.wait_ge(s_sel, l + 1)
                pe.wait_ge(q_ta, l * (KC + KC // 2) + 1)
                for t in range(nt + 1):
                    for t2 in range(min(t + 1, nt)):
                        lhs = const2[:, C2_TRI:C2_TRI + P] if t2 == t else ones
                        ins = pe.matmul(bank[5][:, t * E:(t + 1) * E], lhs, sel[:, t2, :], start=(t2 == 0), stop=(t2 == min(t, nt - 1)))
                ins.then_inc(s_pos, 1)
                for c in LOW_ORDER:
                    pe.wait_ge(q_ta, l * (KC + KC // 2) + HIGH_ORDER.index(c) + 1)
                    if c == 5:
                        pe.wait_ge(s_placed, l + 1)
                    for t in range(nt):
                        ins = pe.transpose(bank[c][:, t * P:(t + 1) * P], h_lo[:, c, t * P:(t + 1) * P].bitcast(F32), ident)
                    ins.then_inc(q_tok, 1)
                pe.wait_ge(q_ta, (l + 1) * (KC + KC // 2))
                pe.wait_ge(q_td, (l + 1) * (KC // 2))

                def one_round(k, l=l, nt=nt):
                    m, s0, n0 = round_start(l, k)

                    def gather(i, part):
                        if part == 0:
                            pe.wait_ge(q_p, i + (m * (E // 2) + 1))
                        for half in range(2):
                            if part == 1:
                                pe.wait_ge(x_hi, 2 * i + (m * E + half + 1))
                            for c in range(4 * half, 4 * half + 4):
                                for t in range(nt):
                                    ins = pe.matmul(bank[c // 2][:, (c % 2) * 2 * SLOTS:(c % 2 + 1) * 2 * SLOTS],
                                                    h_tok[part][:, t, c * P:(c + 1) * P], onehot[:, t, :],
                                                    start=(t == 0), stop=(t == nt - 1))
                            ins.then_inc((g_hi, g_lo)[part], 1)

                    def down(i, j, e):
                        pe.wait_ge(split_lo, nth(2, i, j) + s0)
                        pe.wait_ge(q_tl, 2 * i + (m * E + j + 1))
                        if m or e != 0:
                            pe.wait_ge(q_ya, 2 * i + (m * E + j))
                            pe.wait_ge(q_yd, 2 * i + (m * E + j))
                        wh = w_hi[2][:, :, :].rearrange("p (f k) n -> p f (k n)", f=2)
                        wl = w_lo[2][:, :, :].rearrange("p (f k) n -> p f (k n)", f=2)
                        for n in range(2):
                            for f in range(2):
                                cs = slice(n * 512, (n + 1) * 512)
                                ins = product(bank[6 + n][:, :], ht_hi[j % 2][:, f, :], ht_lo[j % 2][:, f, :],
                                              wh[:, f, cs], wl[:, f, cs], f == 0, f == 1)
                        ins.then_inc(used, 1)

                    def step(i, j, e):
                        even = j % 2 == 0 and (e is None or e < E)
                        if even:
                            gather(i, 0)
                        if e is None or e >= 2:
                            down(i, j - 2, e if e is None else e - 2)
                        if even:
                            gather(i, 1)
                        if e is None or 1 <= e <= E:
                            pe.wait_ge(q_m, 2 * i + (m * E + j))
                            if m or e != 1:
                                pe.wait_ge(q_th, 2 * i + (m * E + j - 1))
                                pe.wait_ge(q_tl, 2 * i + (m * E + j - 1))
                            for f in range(2):
                                ins = pe.transpose(bank[5][:, f * P:(f + 1) * P], hid_m[:, f * P:(f + 1) * P], ident)
                            ins.then_inc(q_t, 1)
                        if e is None or e < E:
                            for role in range(2):
                                pe.wait_ge(split_lo, nth(role, i, j) + s0)
                                if role == 0 and (m or e != 0):
                                    pe.wait_ge(q_m, 2 * i + (m * E + j))
                                for c in range(KC):
                                    if even and role == 0 and c % 4 == 0:
                                        pe.wait_ge(x_hi, 2 * i + (m * E + 2))
                                        pe.wait_ge(x_lo, 2 * i + (m * E + c // 4 + 1))
                                    sl = slice((j % 2) * SLOTS, (j % 2 + 1) * SLOTS)
                                    ins = product(bank[4][:, role * FE:(role + 1) * FE], xg_hi[:, c, sl], xg_lo[:, c, sl],
                                                  w_hi[role][:, c, :], w_lo[role][:, c, :], c == 0, c == KC - 1)
                                ins.then_inc(used, 1)

                    steps(pe, step, 2, k)

                def skip(k, l=l):
                    m, s0, n0 = round_start(l, k)
                    pe.wait_ge(used, s0)
                    pe.sem_inc(used, N_MOE)
                    for sem_ in (g_hi, g_lo, q_t):
                        pe.sem_inc(sem_, E)

                rounds(pe, l, one_round, skip)

            for u in range(len(combine_units(DEPTH - 1))):
                combine(DEPTH - 1, u)
            norm(2 * DEPTH, S, None)
            for k in range(KC):
                pe.wait_ge(n_h[2 * DEPTH], k + 1)
                for t in range(2):
                    ins = pe.transpose(bank[2 * t + k // 4][:, (k % 4) * P:(k % 4 + 1) * P], nh[:, k % 2, t * P:(t + 1) * P], ident)
                ins.then_inc(f_y, 1)

        @block.vector
        def _(dve):
            made = [0]

            def then(ins):
                made[0] += 1
                ins.then_inc(chain_d, 1)
                dve.wait_ge(chain_d, made[0])

            def split(l, r):
                s, n = split_index(l, r), raw_index(l, r)
                dve.wait_ge(split_hi, s + 1)
                w = block_cols(r)
                dve.tensor_tensor(w_lo[s % HL][:, :, 0:w], raw[n % RAW][:, :, 0:w], w_hi[s % HL][:, :, 0:w].bitcast(F32),
                                  ALU.subtract).then_inc(split_lo, 1)

            taken = [0]

            def take_rows(block, src):
                dve.wait_ge(ada_mm, block[0] * N_ADA + block[1] + 1)
                if taken[0] >= 2:
                    dve.wait_ge(m_turn, taken[0] - 1)
                dve.tensor_copy(mod_row[:, taken[0] % 2, 0:src.shape[1]], src).then_inc(m_row, 1)
                taken[0] += 1

            def take_modulation(n, src, parts):
                dve.wait_ge(m_turn, taken[0])
                at_ = 256 if src is bank[7] else 0
                for l, j0, j1 in parts:
                    for s in range(2):
                        ins = dve.tensor_tensor(mod_of[l][:, s, 2 * j0:2 * j1], src[:, at_ + 4 * j0 + s:at_ + 4 * j1:2],
                                                vec[:, V_ADAB + 48 * l + 2 * j0:V_ADAB + 48 * l + 2 * j1], ALU.add)
                    for which, v in enumerate((V_N1, V_N2)):
                        m = 24 * which + KC
                        if 2 * j0 <= m and m + KC <= 2 * j1:
                            then(ins)
                            for s in range(2):
                                ins = dve.scalar_tensor_tensor(amp[:, which, s, :], mod_of[l][:, s, m:m + KC], 1.0,
                                                               vec[:, v + KC * l:v + KC * (l + 1)], ALU.add, ALU.mult)
                ins.then_inc(s_mod, 1)
                dve.wait_ge(s_mod, n)

            def norm(i, width, last, before_modulation=None):
                n = width // P
                for k in range(1, KC, 2) if i == 0 else ():
                    if k >= 4:
                        dve.wait_ge(n_sum, k - 3)
                    dve.tensor_tensor(nsq[:, k % 4, 0:width], x_t[:, k, 0:width], x_t[:, k, 0:width], ALU.mult).then_inc(n_sqd, 1)
                dve.wait_ge(n_root, i + 1)
                dve.reciprocal(rstd[:, 0:n], col[:, 0:n]).then_inc(n_rstd, 1)
                if before_modulation:
                    before_modulation()
                dve.wait_ge(n_bc, i + 1)

                def low(k):
                    dve.wait_ge(n_hi, i * KC + k + 1)
                    dve.tensor_tensor(h_lo[:, k, 0:width], nh[:, k % 2, 0:width], h_hi[:, k, 0:width].bitcast(F32),
                                      ALU.subtract).then_inc(n_lo, 1)
                for k in range(KC):
                    if k >= 2:
                        dve.wait_ge(n_h[i], (k - 1) * (1 if last else width // S))
                    dve.tensor_tensor(nx[:, k % 2, 0:width], x_t[:, k, 0:width], bank[7][:, 0:width], ALU.mult).then_inc(n_x, 1)
                    if k and not last:
                        low(k - 1)
                    q = (k - 4) // 3
                    if k in (4, 7) and 2 * q < len(IN_NORM[i]):
                        take_rows(IN_NORM[i][2 * q + 1], bank[ROW_BANKS[i][q]][0:2, :])
                if not last:
                    low(KC - 1)
                for q in range(2, len(IN_NORM[i]) // 2):
                    take_rows(IN_NORM[i][2 * q + 1], bank[ROW_BANKS[i][q]][0:2, :])

            dve.wait_ge(s_vt, 1)
            dve.tensor_copy(vec[:, :], bank[0][:, 0:N_VEC]).then_inc(s_vec, 1)
            dve.wait_ge(s_rw, 1)
            dve.tensor_tensor(rw_lo[:, :, :], rw_in[:, :, :], rw_hi[:, :, :].bitcast(F32), ALU.subtract).then_inc(s_rw, 1)
            def combine(l, u):
                units = combine_units(l)
                n = sum(len(combine_units(i)) for i in range(l))
                if u < len(units) and units[u][1] == 0:
                    t = units[u][0]
                    dve.wait_ge(q_back[t], 32 * sum(2 * streams(i) > t for i in range(l + 1)))
                    then(dve.tensor_scalar(y_back[:, t, 0, :], y_back[:, t, 0, :], pick[:, t, 2:3], None, ALU.mult))
                    dve.scalar_tensor_tensor(y_back[:, t, 0, :], y_back[:, t, 1, :], pick[:, t, 3:4], y_back[:, t, 0, :],
                                             ALU.mult, ALU.add).then_inc(q_c, 1)
                if u >= 1:
                    t, half = units[u - 1]
                    dve.wait_ge(q_ct, n + u)
                    for c in range(4):
                        k = 4 * half + c
                        ins = dve.scalar_tensor_tensor(x_t[:, k, t * P:(t + 1) * P], bank[4 + (u - 1) % 3][:, c * P:(c + 1) * P],
                                                       mod_of[l][:, t // 2, 5 * KC + k:5 * KC + k + 1], x_t[:, k, t * P:(t + 1) * P],
                                                       ALU.mult, ALU.add)
                    ins.then_inc(x_moe, 1)

            for l in range(DEPTH):
                ns = streams(l)
                nt, width = 2 * ns, ns * S
                if l == 0:
                    for q in range(3):
                        take_rows((0, 2 * q + 1), bank[q][0:2, :])
                    for k in range(0, KC, 2):
                        dve.wait_ge(s_xt, k + 1)
                        dve.tensor_copy(x_t[:, k, :], bank[X_BANK[k]][:, :]).then_inc(s_xevd, 1)
                    take_rows((0, 7), bank[0][0:2, :])
                    dve.wait_ge(s_xev, 4)
                else:
                    for u in range(len(combine_units(l - 1)) + 1):
                        combine(l - 1, u)
                        if u in (1, 4, 6):
                            q = (1, 4, 6).index(u)
                            take_rows((1, 13 + 2 * q), bank[q][0:2, :])
                    dve.wait_ge(x_moe, sum(len(combine_units(n)) for n in range(l)))

                def before_modulation():
                    if l == 0:
                        take_modulation(1, bank[3], [(0, 0, 8)])
                    for r in range(N_ADA, N_ADA + HL - 1):
                        split(l, r)

                norm(2 * l, T, False, before_modulation)
                if l == 0:
                    take_modulation(2, bank[4], [(0, 8, 16)])
                else:
                    take_modulation(5, bank[3], [(1, 12, 20)])
                split(l, N_ADA + HL - 1)
                for b in range(N_WIN):
                    if b in (0, 2, 3, 6, 7):
                        dve.wait_ge(used, done(l, N_ADA + b))
                    b0 = 2 * (b % 4)
                    if b == 0:
                        for c in range(2):
                            ins = dve.tensor_copy(a_pad[:, c, 0:ns, PAD:PAD + S], bank[c][:, 0:width].rearrange("p (s t) -> p s t", s=ns))
                        ins.then_inc(proj_ed, 1)
                    if b in (2, 6):
                        dst, w = (k_na, T) if b == 2 else (q_low, width)
                        for c in range(2):
                            ins = dve.tensor_copy(dst[:, c, 0:w], bank[b0 + c][:, 0:w])
                        ins.then_inc(proj_ed, 1)
                    if b == 3:
                        for c in range(2):
                            ins = dve.tensor_copy(v_na[:, 2 * c:2 * c + 2, :].rearrange("p t n -> p (t n)"), bank[6 + c][:, :])
                        ins.then_inc(proj_ed, 1)
                    if b == 7:
                        rr = slice(NOPE, QK)
                        dve.tensor_copy(k_rope[rr, :], bank[7][rr, :])
                        then(dve.tensor_tensor(rope_t[rr, 0, :], bank[0][rr, 0:S], const[rr, C_SIN:C_SIN + S], ALU.mult))
                        ins = dve.tensor_tensor(k_rope[rr, 0:S], k_rope[rr, 0:S], const[rr, C_COS:C_COS + S], ALU.mult)
                        ins.then_inc(proj_ed, 1)
                        dve.wait_ge(proj_ed, l * 5 + 5)
                        then(dve.tensor_tensor(k_rope[rr, 0:S], k_rope[rr, 0:S], rope_t[rr, 0, :], ALU.add))
                        dve.tensor_copy(k_mla[rr, :, :], k_rope[rr, :][:, None, :].to_broadcast([ROPE, HEADS, T]))
                    if b + HL < N_WIN:
                        split(l, N_ADA + b + HL)
                n = 4 * nt
                dve.wait_ge(proj_ea, l * 4 + 3)
                vv = sgu_v[:, 0:nt, :].rearrange("p t (g c) -> p (t g) c", c=64)
                sq = sgu_sq[:, 0:nt, :].rearrange("p t (g c) -> p (t g) c", c=64)
                then(dve.tensor_tensor(sq, vv, vv, ALU.mult))
                dve.tensor_reduce(col[:, 16:16 + n], sq, AX.X, ALU.add).then_inc(s_gv, 1)
                dve.wait_ge(s_lroot, l + 1)
                dve.reciprocal(col[:, 48:48 + nt], col[:, 8:8 + nt])
                dve.reciprocal(col[:, 52:56], col[:, 12:16]).then_inc(s_lrstd, 1)
                dve.wait_ge(s_groot, l + 1)
                then(dve.reciprocal(col[:, 16:16 + n], col[:, 32:32 + n]))
                dve.wait_ge(s_lbc, l + 1)
                for c in range(2):
                    dve.tensor_tensor(q_low[:, c, 0:width], q_low[:, c, 0:width], bank[0][:, 0:width], ALU.mult).then_inc(s_low, 1)
                dve.wait_ge(proj_ea, l * 4 + 4)
                dve.tensor_tensor(kv_low[:, :], kv_low[:, :], bank[1][:, :], ALU.mult).then_inc(s_low, 1)
                then(dve.tensor_tensor(vv, vv, col[:, 16:16 + n][:, :, None].to_broadcast([P, n, 64]), ALU.mult))
                dve.tensor_tensor(sgu_v[:, 0:nt, :], sgu_v[:, 0:nt, :], sgu_g[:, :][:, None, :].to_broadcast([P, nt, S]),
                                  ALU.mult).then_inc(s_gn, 1)
                rr = slice(NOPE, QK)
                dve.wait_ge(s_up, l * 11 + 6)
                for h2 in range(2):
                    ins = dve.scalar_tensor_tensor(rope_t[rr, 2 * h2:2 * h2 + 2, :], bank[6 + h2][rr, :].rearrange("p (h t) -> p h t", h=2),
                                                   MLA_SCALE, const[rr, C_SIN:C_SIN + S][:, None, :].to_broadcast([ROPE, 2, S]),
                                                   ALU.mult, ALU.mult)
                ins.then_inc(s_rot, 1)
                dve.wait_ge(s_qe, l * 4 + 4)
                dve.wait_ge(s_rot, l * 2 + 1)
                then(dve.tensor_tensor(q_mla[rr, :, 0:S], q_mla[rr, :, 0:S], const[rr, C_COS:C_COS + S][:, None, :].to_broadcast([ROPE, HEADS, S]), ALU.mult))
                dve.tensor_tensor(q_mla[rr, :, 0:S], q_mla[rr, :, 0:S], rope_t[rr, :, :], ALU.add).then_inc(s_rot, 1)
                dve.wait_ge(s_mix, l + 1)
                for g in range(4):
                    v0 = V_SB + 4 * l + g
                    ins = dve.scalar_tensor_tensor(o_tok[:, 0:nt, S + g * 64:S + (g + 1) * 64],
                                                   bank[6 + g // 2][:, (g % 2) * S:(g % 2) * S + nt * 64].rearrange("p (t c) -> p t c", c=64),
                                                   vec[:, v0:v0 + 1], sgu_u[:, 0:nt, g * 64:(g + 1) * 64], ALU.add, ALU.mult)
                ins.then_inc(s_go, 1)
                jobs = attention_jobs(l)
                for i in range(len(jobs) + 2):
                    if l == 0 and i % 2 and i // 2 - 1 in range(12):
                        take_rows(divmod(16 + i // 2 - 1, N_ADA), bank[7][0:2, 0:BW])
                    if i < len(jobs):
                        nk = T if jobs[i][2] < 2 else S
                        dve.wait_ge(t_sc, l * JOBS + i + 1)
                        dve.tensor_reduce(stat[:, i % 4, 0:1], bank[i % 3][:, 0:nk], AX.X, ALU.max, negate=True).then_inc(t_mx, 1)
                    if 1 <= i <= len(jobs) and i % 2 == 0:
                        q = i - 1
                        nkt = 4 if jobs[q][2] < 2 else 2
                        dve.wait_ge(t_tr, l * JOBS + q + 1)
                        if q >= 3:
                            dve.wait_ge(t_pv, l * JOBS + q - 2)
                        dve.tensor_copy(prob_t[q % 3][:, 0:nkt, :].rearrange("p k n -> p (k n)"), bank[3 + q % 2][:, 0:nkt * P]).then_inc(t_pd, 1)
                    if i >= 2:
                        q = i - 2
                        kind, h, t = jobs[q]
                        dve.wait_ge(t_pv, l * JOBS + q + 1)
                        then(dve.reciprocal(stat[:, q % 4, 2:3], stat[:, q % 4, 1:2]))
                        c0 = (0 if kind == "na" else 2 * S) + h * 64
                        dve.tensor_scalar(o_tok[:, t, c0:c0 + 64], bank[5 + q % 2][:, 0:64], stat[:, q % 4, 2:3], None, ALU.mult).then_inc(t_o, 1)
                if l == 0:
                    take_modulation(3, bank[7], [(0, 16, 24), (1, 0, 4)])
                for c in range(KC):
                    dve.wait_ge(m_hi, l * KC + c + 1)
                    hi = h_hi[:, c, 0:width].bitcast(F32)
                    if c < 2:
                        v0 = V_PS + 2 * l + c
                        dve.scalar_tensor_tensor(h_lo[:, c, 0:width], bank[c][:, 0:width], vec[:, v0:v0 + 1], hi, ALU.mult, ALU.subtract).then_inc(m_lo, 1)
                    else:
                        dve.tensor_tensor(h_lo[:, c, 0:width], bank[c][:, 0:width], hi, ALU.subtract).then_inc(m_lo, 1)

                def add_gated(dc, src, gate, signal):
                    for s in range(ns):
                        sl = slice(s * S, (s + 1) * S)
                        ins = dve.scalar_tensor_tensor(x_t[:, dc, sl], src[:, sl], mod_of[l][:, s, gate * KC + dc:gate * KC + dc + 1], x_t[:, dc, sl],
                                                       ALU.mult, ALU.add)
                    ins.then_inc(signal, 1)

                for b in range(N_WOUT):
                    split(l, N_ADA + N_WIN + b)
                    if b >= 1:
                        dve.wait_ge(used, done(l, N_ADA + N_WIN + b - 1))
                        for c in range(2):
                            add_gated(2 * (b - 1) + c, bank[2 * (b - 1) + c], 2, o_ev)
                dve.wait_ge(used, done(l, N_ADA + N_WIN + 3))
                for c in range(2):
                    add_gated(6 + c, bank[6 + c], 2, o_ev)
                dve.wait_ge(o_ev, l * KC + KC)
                norm(2 * l + 1, width, False)

                if l == 0:
                    take_modulation(4, bank[4], [(1, 4, 12)])
                else:
                    take_modulation(6, bank[4], [(1, 20, 24)])
                dve.wait_ge(r_sg, l + 1)
                sc = score[:, 0:nt, :]
                bi, rk, cm = biased[:, 0:nt, :], rank[:, 0:nt, :], cmp[:, 0:nt, :]
                then(dve.tensor_tensor(bi, sc, rb_row[:, :][:, None, :].to_broadcast([P, nt, E]), ALU.add))

                def rank_of_four(values, ranks, scratch):
                    then(dve.tensor_copy(ranks, const[:, C_RANK:C_RANK + ranks.shape[1] * 4].rearrange("p (n f) -> p n f", f=4)))
                    for d in range(1, 4):
                        then(dve.tensor_tensor(scratch[:, :, 0:4 - d], values[:, :, 0:4 - d], values[:, :, d:4], ALU.is_ge))
                        then(dve.tensor_tensor(ranks[:, :, d:4], ranks[:, :, d:4], scratch[:, :, 0:4 - d], ALU.add))
                        then(dve.tensor_tensor(ranks[:, :, 0:4 - d], ranks[:, :, 0:4 - d], scratch[:, :, 0:4 - d], ALU.subtract))

                four = lambda ap: ap.rearrange("p t (g f) -> p (t g) f", f=4)
                rank_of_four(four(bi), four(rk), four(cm))
                then(dve.tensor_scalar(rk, rk, 1.5, None, ALU.is_lt))
                then(dve.tensor_tensor(cm, rk, bi, ALU.mult))
                g2 = grp[:, 0:nt, :]
                then(dve.tensor_reduce(g2.rearrange("p t g -> p (t g)"), four(cm), AX.X, ALU.add))
                gr = grank[:, 0:nt, :]
                rank_of_four(g2, gr, cmp[:, 0:nt, 0:4])
                then(dve.tensor_scalar(gr, gr, 0.5, None, ALU.is_lt))
                se, sl, ro, ga = sel[:, 0:nt, :], slot[:, 0:nt, :], row[:, 0:nt, :], gates[:, 0:nt, :]
                dve.tensor_tensor(four(se), four(rk), gr.rearrange("p t g -> p (t g)")[:, :, None].to_broadcast([P, 4 * nt, 4]),
                                  ALU.mult).then_inc(s_sel, 1)
                dve.wait_ge(s_sel, l + 1)
                then(dve.tensor_tensor(rk, se, sc, ALU.mult))
                then(dve.tensor_reduce(grp[:, 0:nt, 0], rk, AX.X, ALU.add))
                then(dve.reciprocal(grp[:, 0:nt, 1], grp[:, 0:nt, 0]))
                then(dve.tensor_tensor(ga, rk, grp[:, 0:nt, 1:2].to_broadcast([P, nt, E]), ALU.mult))

                def split_expert(l, k, role, i, j):
                    m, s0, n0 = round_start(l, k)
                    q, _ = raw_place(role, i, j)
                    dve.wait_ge(split_hi, nth(role, i, j) + s0)
                    dve.tensor_tensor(w_lo[role][:, :, :], raw[q][:, :, :], w_hi[role][:, :, :].bitcast(F32), ALU.subtract).then_inc(split_lo, 1)

                split_expert(l, 0, 0, 0, 0)
                dve.wait_ge(s_pos, l + 1)
                dve.tensor_copy(placed[:, 0:nt + 1, :].rearrange("p t e -> p (t e)"), bank[5][:, 0:(nt + 1) * E]).then_inc(s_placed, 1)
                dve.wait_ge(s_placed, l + 1)
                pos = placed[:, 0:nt, :]
                then(dve.scalar_tensor_tensor(sl, pos, 1.0, se, ALU.add, ALU.mult))
                then(dve.tensor_scalar(sl, sl, -1.0, None, ALU.add))

                def one_hot(l, k, i, pair):
                    lo = C2_IOTA + k * SLOTS
                    for j in range(2):
                        ins = dve.tensor_tensor(onehot[:, 0:nt, j * SLOTS:(j + 1) * SLOTS],
                                                const2[:, lo:lo + SLOTS][:, None, :].to_broadcast([P, nt, SLOTS]),
                                                slot[:, 0:nt, bass.ds(2 * i + (2 * pair + j), 1)].to_broadcast([P, nt, SLOTS]), ALU.is_equal)
                    ins.then_inc(q_p, 1)

                one_hot(l, 0, 0, 0)
                dve.wait_ge(q_tok, (l + 1) * (2 * KC))
                for c in LOW_ORDER[KC // 2:]:
                    dve.tensor_copy(h_tok[1][:, 0:nt, c * P:(c + 1) * P], bank[c][:, 0:width].rearrange("p (t d) -> p t d", d=P)).then_inc(q_td, 1)
                split_expert(l, 0, 1, 0, 0)
                then(dve.tensor_reduce(col[:, 60:61], placed[:, nt, :], AX.X, ALU.max))
                for k in range(1, ROUNDS[l]):
                    ins = dve.tensor_scalar(col[:, 60 + k:61 + k], col[:, 60:61], k * SLOTS + 0.5, None, ALU.is_gt)
                then(ins)
                dve.tensor_copy(more[:, 0:ROUNDS[l] - 1], col[:, 61:60 + ROUNDS[l]]).then_inc(s_more, 1)
                then(dve.tensor_tensor(cm, pos, const2[:, C2_EBASE:C2_EBASE + E][:, None, :].to_broadcast([P, nt, E]), ALU.add))
                for k in range(1, ROUNDS[l]):
                    then(dve.tensor_scalar(ro, pos, k * SLOTS - 0.5, float(E * SLOTS - SLOTS), ALU.is_gt, ALU.mult))
                    then(dve.tensor_tensor(cm, cm, ro, ALU.add))
                then(dve.tensor_tensor(ro, cm, se, ALU.mult))
                first, second = pick[:, 0:nt, 0:1], pick[:, 0:nt, 1:2]
                dve.tensor_reduce(pick[:, 0:nt, 0], ro, AX.X, ALU.max)
                then(dve.tensor_reduce(pick[:, 0:nt, 1], ro, AX.X, ALU.add))
                then(dve.tensor_tensor(second, second, first, ALU.subtract))
                for n in range(2):
                    then(dve.tensor_tensor(cm, ro, pick[:, 0:nt, n:n + 1].to_broadcast([P, nt, E]), ALU.is_equal))
                    then(dve.tensor_tensor(cm, cm, ga, ALU.mult))
                    then(dve.tensor_reduce(pick[:, 0:nt, 2 + n], cm, AX.X, ALU.add))
                then(dve.tensor_scalar(pick0[:, 0:nt, :], pick[:, 0:nt, 0:2], -1.0, None, ALU.add))
                dve.tensor_copy(pick_row[:, 0:nt, :], pick0[:, 0:nt, :]).then_inc(q_row, 1)

                def one_round(k, l=l):
                    m, s0, n0 = round_start(l, k)

                    def step(i, j, e):
                        if (e is None or e < E - 1) and j % 2:
                            one_hot(l, k, i, 1)
                        if e is None or e >= 2:
                            par, i2 = j % 2, i + (j - 2) // 2
                            dve.wait_ge(used, nth(2, i, j - 2) + s0)
                            dve.wait_ge(q_out[par], i2 * 16 + 16 * (E // 2) * m)
                            dve.tensor_copy(y_sb[par][:, 512:1024], bank[7][:, :]).then_inc(q_yd, 1)
                        if (e is None or e < E) and j % 2 == 0:
                            for half in range(2):
                                dve.wait_ge(g_lo, 2 * i + (m * E + half + 1))
                                for b in range(2):
                                    ins = dve.tensor_copy(xg_lo[:, 4 * half + 2 * b:4 * half + 2 * b + 2, :].rearrange("p k n -> p (k n)"),
                                                          bank[2 * half + b][:, :])
                                ins.then_inc(x_lo, 1)
                        if e is None or 1 <= e <= E:
                            dve.wait_ge(q_th, 2 * i + (m * E + j))
                            p = (j - 1) % 2
                            dve.tensor_tensor(ht_lo[p][:, :, :].rearrange("p f n -> p (f n)"), bank[5][:, 0:2 * SLOTS],
                                              ht_hi[p][:, :, :].rearrange("p f n -> p (f n)").bitcast(F32), ALU.subtract).then_inc(q_tl, 1)
                            split_expert(l, k, 2, i, j - 1)
                        if e is None or e < E - 1:
                            split_expert(l, k, 0, i, j + 1)
                        if e is None or e < E:
                            dve.wait_ge(q_s, 2 * i + (m * E + j + 1))
                            dve.wait_ge(q_t, 2 * i + (m * E + j))
                            dve.tensor_tensor(hid_m[:, :], bank[4][:, FE:2 * FE], hid_g[:, :], ALU.mult).then_inc(q_m, 1)
                        if e is None or e < E - 1:
                            split_expert(l, k, 1, i, j + 1)

                    if k:
                        dve.wait_ge(g_lo, m * E)
                        one_hot(l, k, 0, 0)
                        split_expert(l, k, 0, 0, 0)
                        split_expert(l, k, 1, 0, 0)
                    steps(dve, step, 2, k)

                def skip(k, l=l):
                    m, s0, n0 = round_start(l, k)
                    dve.wait_ge(split_lo, s0)
                    dve.wait_ge(q_yd, m * E)
                    dve.sem_inc(split_lo, N_MOE)
                    dve.sem_inc(q_p, E // 2)
                    for sem_ in (x_lo, q_m, q_tl, q_yd):
                        dve.sem_inc(sem_, E)

                rounds(dve, l, one_round, skip)
            for u in range(len(combine_units(DEPTH - 1)) + 1):
                combine(DEPTH - 1, u)
            dve.wait_ge(x_moe, sum(len(combine_units(n)) for n in range(DEPTH)))
            norm(2 * DEPTH, S, True)
            for t in range(2):
                dve.wait_ge(f_y, KC)
                dve.tensor_copy(y_tok[:, t, 0:512], bank[2 * t][:, :]).then_inc(f_ev, 1)


def kernel(**inputs):
    import numpy as _np
    import concourse.bacc as _bacc
    from concourse import mybir as _mybir
    from concourse.bass_utils import run_bass_kernel_spmd as _run

    g = {k: _np.ascontiguousarray(v) for k, v in inputs.items()}
    arrays = {n: g[n] for n in ("ada_w", "w_in", "w_out", "pool_w", "mla_w_uq", "mla_w_ukv", "sgu_norm_g", "sgu_w", "router_w",
                                "router_b", "moe_w_gate", "moe_w_up", "moe_w_down")}
    arrays["x"], arrays["ctx"] = g["x"][0], g["ctx"][0]
    arrays["vec0"] = _np.concatenate([g[n].reshape(-1, P) for n in ("ada_b", "c", "c_ctx")])
    arrays["vec1"] = _np.concatenate([g[n].reshape(-1, P) for n in (
        "norm1_g", "norm2_g", "final_g", "pool_s", "mla_q_norm_g", "mla_kv_norm_g", "sgu_b")])
    rpb = _np.zeros((DEPTH, 2, HEADS, 6, P), _np.float32)
    for half in range(2):
        rpb[:, half, :, :, 48:79] = g["na_rpb"][:, :, 5 - half:11 - half]
    arrays["na_rpb"] = rpb
    arrays["const"] = constants()
    arrays["const2"] = router_constants()
    nc = _bacc.Bacc("TRN2", target_bir_lowering=False, num_devices=1)
    aps = {}
    for n, v in arrays.items():
        aps[n] = nc.dram_tensor(f"in_{n}", v.shape, _mybir.dt.from_np(v.dtype), kind="ExternalInput").ap()
    out = nc.dram_tensor("out_0", (S, D), F32, kind="ExternalOutput").ap()
    build(nc, aps, out)
    r = _run(nc, [{f"in_{n}": v for n, v in arrays.items()}], core_ids=[0])
    return r.results[0]["out_0"].reshape(1, S, D)
```
